# Optimizing a Trainium2 kernel written in Bass

```python
import math
import jax, jax.numpy as jnp
from jax import lax
import numpy as np

D_MODEL = 1024
BATCH = 1
SEQ = 512
DEPTH = 2
DEC_BATCH = 8
DEC_SEQ = 4
PAST_LEN = 2048
PAGE_SIZE = 128

N_A_LAYERS = DEPTH // 2
N_B_LAYERS = DEPTH - N_A_LAYERS
POOL_WINDOWS = (2, 4, 8, 16)
POOL_GROUPS = len(POOL_WINDOWS)
POOL_GROUP_DIM = D_MODEL // POOL_GROUPS
POOL_PAD = max(POOL_WINDOWS) - 1
DIL_PATTERNS = ((128, 1), (512, 4), (2048, 16))
N_DIL_GROUPS = len(DIL_PATTERNS)
HEAD_DIM = 64
HEADS_PER_GROUP = D_MODEL // 128
N_HEADS = N_DIL_GROUPS * HEADS_PER_GROUP
ATTN_GROUP_WIDTH = HEADS_PER_GROUP * HEAD_DIM
Q_WIDTH = N_DIL_GROUPS * ATTN_GROUP_WIDTH
KV_WIDTH = 2 * Q_WIDTH
N_BUCKETS = 32
MAX_DISTANCE = 2048
D_FF = ((8 * D_MODEL // 3 + 127) // 128) * 128
ALPHA = (2.0 * DEPTH) ** 0.25
BETA = (8.0 * DEPTH) ** -0.25
LN_EPS = 1e-5
Q_BLOCK = 128
NEG = -1e30

kernel_name = 'yoco_pool_dilated_macaron_deepnorm_step'

def t5_buckets(dist):
    dist = np.asarray(dist, dtype=np.int64)
    max_exact = N_BUCKETS // 2
    ratio = np.maximum(dist, 1).astype(np.float64) / max_exact
    large = max_exact + (np.log(ratio) / np.log(MAX_DISTANCE / max_exact) * (N_BUCKETS - max_exact)).astype(np.int64)
    large = np.minimum(large, N_BUCKETS - 1)
    return np.where(dist < max_exact, dist, large).astype(np.int32)

def layer_norm(x, g, b):
    xf = x.astype(jnp.float32)
    mu = jnp.mean(xf, axis=-1, keepdims=True)
    var = jnp.mean(jnp.square(xf - mu), axis=-1, keepdims=True)
    y = (xf - mu) * lax.rsqrt(var + LN_EPS) * g.astype(jnp.float32) + b.astype(jnp.float32)
    return y.astype(x.dtype)

def swiglu(x, w13, w2):
    gate, up = jnp.split(x @ w13, 2, axis=-1)
    return (jax.nn.silu(gate) * up) @ w2

def pool_mixer(x, prefix, pos0, w_in, w_grp, scale, w_out):
    n = x.shape[1]
    u = x @ w_in
    u_ext = jnp.concatenate([prefix.astype(u.dtype), u], axis=1)
    csum = jnp.cumsum(u_ext.astype(jnp.float32), axis=1)
    csum = jnp.pad(csum, ((0, 0), (1, 0), (0, 0)))
    hi = csum[:, POOL_PAD + 1:POOL_PAD + 1 + n]
    pos = pos0 + jnp.arange(n)
    outs = []
    for g, w in enumerate(POOL_WINDOWS):
        cs = slice(g * POOL_GROUP_DIM, (g + 1) * POOL_GROUP_DIM)
        win_sum = hi[..., cs] - csum[:, POOL_PAD + 1 - w:POOL_PAD + 1 - w + n, cs]
        count = jnp.minimum(pos + 1, w).astype(jnp.float32)[None, :, None]
        pooled = win_sum / count - u[..., cs].astype(jnp.float32)
        outs.append(jnp.einsum('bnc,ce->bne', pooled.astype(u.dtype), w_grp[g]))
    z = jnp.concatenate(outs, axis=-1) * scale
    return z @ w_out, u_ext[:, -POOL_PAD:]

def dilated_group_attention(q, k, v, q_off, dilation, n_keys, bias):
    steps = jnp.arange(n_keys) * dilation

    def attend(q_blk, rows):
        idx = rows[:, None] - steps[None, :]
        valid = idx >= 0
        idx = jnp.maximum(idx, 0)
        kg = jnp.take(k, idx, axis=1, mode='clip')
        vg = jnp.take(v, idx, axis=1, mode='clip')
        s = jnp.einsum('bqhd,bqkhd->bhqk', q_blk, kg).astype(jnp.float32)
        s = s + bias.astype(jnp.float32)[None, :, None, :]
        s = jnp.where(valid[None, None], s, NEG)
        lse = jax.nn.logsumexp(s, axis=-1)
        p = jnp.exp(s - lse[..., None])
        o = jnp.einsum('bhqk,bqkhd->bqhd', p.astype(vg.dtype), vg)
        return o, jnp.transpose(lse, (0, 2, 1))

    b, nq, h, d = q.shape
    rows = q_off + jnp.arange(nq)
    if nq > Q_BLOCK and nq % Q_BLOCK == 0:
        nb = nq // Q_BLOCK
        qb = q.reshape(b, nb, Q_BLOCK, h, d).swapaxes(0, 1)
        rb = rows.reshape(nb, Q_BLOCK)
        o, lse = lax.map(lambda a: attend(a[0], a[1]), (qb, rb))
        o = o.swapaxes(0, 1).reshape(b, nq, h, d)
        lse = lse.swapaxes(0, 1).reshape(b, nq, h)
    else:
        o, lse = attend(q, rows)
    return o, lse

def dilated_mixer(x, kv_groups, q_offs, w_q, w_o, rel_bias):
    b, n, _ = x.shape
    q = (x @ w_q).reshape(b, n, N_DIL_GROUPS, HEADS_PER_GROUP, HEAD_DIM) * (HEAD_DIM ** -0.5)
    outs, lses = [], []
    for g, (win, dil) in enumerate(DIL_PATTERNS):
        n_keys = win // dil + 1
        buckets = t5_buckets(np.arange(n_keys) * dil)
        bias = rel_bias[buckets][:, g * HEADS_PER_GROUP:(g + 1) * HEADS_PER_GROUP].T
        k, v = kv_groups[g]
        o, lse = dilated_group_attention(q[:, :, g], k, v, q_offs[g], dil, n_keys, bias)
        outs.append(o)
        lses.append(lse)
    wts = jax.nn.softmax(jnp.stack(lses), axis=0)
    o = jnp.sum(jnp.stack(outs).astype(jnp.float32) * wts[..., None], axis=0).astype(x.dtype)
    return o.reshape(b, n, ATTN_GROUP_WIDTH) @ w_o

def trunk(x, pool_prefix, kv_past, pos0, ln_g, ln_b, ffn_w13, ffn_w2, pool_w_in, pool_w_grp, pool_scale,
          pool_w_out, attn_w_kv, attn_w_q, attn_w_o, rel_bias):
    pool_states = []
    kv_new = None
    kv_groups, q_offs = [], []
    for layer in range(DEPTH):
        if layer == N_A_LAYERS:
            b, n, _ = x.shape
            kv_new = (x @ attn_w_kv).reshape(b, n, N_DIL_GROUPS, 2, HEADS_PER_GROUP, HEAD_DIM)
            for g in range(N_DIL_GROUPS):
                if kv_past is None:
                    kv_g, off = kv_new[:, :, g], 0
                else:
                    kv_g = jnp.concatenate([kv_past[g].astype(kv_new.dtype), kv_new[:, :, g]], axis=1)
                    off = kv_past[g].shape[1]
                kv_groups.append((kv_g[:, :, 0], kv_g[:, :, 1]))
                q_offs.append(off)
        x = layer_norm(ALPHA * x + 0.5 * swiglu(x, ffn_w13[layer, 0], ffn_w2[layer, 0]), ln_g[layer, 0], ln_b[layer, 0])
        if layer < N_A_LAYERS:
            mix, st = pool_mixer(x, pool_prefix[layer], pos0, pool_w_in[layer], pool_w_grp[layer],
                                 pool_scale[layer], pool_w_out[layer])
            pool_states.append(st)
        else:
            j = layer - N_A_LAYERS
            mix = dilated_mixer(x, kv_groups, q_offs, attn_w_q[j], attn_w_o[j], rel_bias)
        x = layer_norm(ALPHA * x + mix, ln_g[layer, 1], ln_b[layer, 1])
        x = layer_norm(ALPHA * x + 0.5 * swiglu(x, ffn_w13[layer, 1], ffn_w2[layer, 1]), ln_g[layer, 2], ln_b[layer, 2])
    return x, jnp.stack(pool_states), kv_new

def setup_inputs(seed: int = 0) -> dict:
    key = jax.random.key(seed)
    ks = jax.random.split(key, 20)

    def nrm(k, shape, scale):
        return jax.random.normal(k, shape, jnp.float32) * scale

    x_prompt = nrm(ks[0], (BATCH, SEQ, D_MODEL), 1.0)
    x_sample = nrm(ks[1], (DEC_BATCH, DEC_SEQ, D_MODEL), 1.0)
    state_pool = nrm(ks[2], (N_A_LAYERS, DEC_BATCH, POOL_PAD, D_MODEL), 1.0)
    caches = [nrm(ks[3 + g], (DEC_BATCH, min(w, PAST_LEN), 2, HEADS_PER_GROUP, HEAD_DIM), 1.0)
              for g, (w, _) in enumerate(DIL_PATTERNS)]
    ln_g = 1.0 + nrm(ks[6], (DEPTH, 3, D_MODEL), 0.05)
    ln_b = nrm(ks[7], (DEPTH, 3, D_MODEL), 0.02)
    ffn_w13 = nrm(ks[8], (DEPTH, 2, D_MODEL, 2 * D_FF), D_MODEL ** -0.5)
    ffn_w2 = nrm(ks[9], (DEPTH, 2, D_FF, D_MODEL), (D_FF ** -0.5) * BETA)
    pool_w_in = nrm(ks[10], (N_A_LAYERS, D_MODEL, D_MODEL), D_MODEL ** -0.5)
    pool_w_grp = nrm(ks[11], (N_A_LAYERS, POOL_GROUPS, POOL_GROUP_DIM, POOL_GROUP_DIM), POOL_GROUP_DIM ** -0.5)
    pool_scale = 1.0 + nrm(ks[12], (N_A_LAYERS, D_MODEL), 0.1)
    pool_w_out = nrm(ks[13], (N_A_LAYERS, D_MODEL, D_MODEL), (D_MODEL ** -0.5) * BETA)
    kv_scale = jnp.array([1.0, BETA], jnp.float32)[None, None, :, None]
    attn_w_kv = (nrm(ks[14], (D_MODEL, N_DIL_GROUPS, 2, ATTN_GROUP_WIDTH), D_MODEL ** -0.5) * kv_scale).reshape(D_MODEL, KV_WIDTH)
    attn_w_q = nrm(ks[15], (N_B_LAYERS, D_MODEL, Q_WIDTH), D_MODEL ** -0.5)
    attn_w_o = nrm(ks[16], (N_B_LAYERS, ATTN_GROUP_WIDTH, D_MODEL), (ATTN_GROUP_WIDTH ** -0.5) * BETA)
    rel_bias = nrm(ks[17], (N_BUCKETS, N_HEADS), 0.3)
    return {'x_prompt': x_prompt, 'x_sample': x_sample, 'state_pool': state_pool,
            'cache_kv_w128': caches[0], 'cache_kv_w512': caches[1], 'cache_kv_w2048': caches[2],
            'ln_g': ln_g, 'ln_b': ln_b, 'ffn_w13': ffn_w13, 'ffn_w2': ffn_w2,
            'pool_w_in': pool_w_in, 'pool_w_grp': pool_w_grp, 'pool_scale': pool_scale, 'pool_w_out': pool_w_out,
            'attn_w_kv': attn_w_kv, 'attn_w_q': attn_w_q, 'attn_w_o': attn_w_o, 'rel_bias': rel_bias}

def reference(x_prompt, x_sample, state_pool, cache_kv_w128, cache_kv_w512, cache_kv_w2048, ln_g, ln_b, ffn_w13,
              ffn_w2, pool_w_in, pool_w_grp, pool_scale, pool_w_out, attn_w_kv, attn_w_q, attn_w_o, rel_bias):
    weights = (ln_g, ln_b, ffn_w13, ffn_w2, pool_w_in, pool_w_grp, pool_scale, pool_w_out,
               attn_w_kv, attn_w_q, attn_w_o, rel_bias)
    pool_zero = jnp.zeros((N_A_LAYERS, x_prompt.shape[0], POOL_PAD, D_MODEL), x_prompt.dtype)
    y_prompt, pool_p, kv_p = trunk(x_prompt, pool_zero, None, 0, *weights)
    y_sample, pool_s, kv_s = trunk(x_sample, state_pool, (cache_kv_w128, cache_kv_w512, cache_kv_w2048),
                                   PAST_LEN, *weights)
    n = x_prompt.shape[1]
    kv_p_groups = [kv_p[:, n - min(w, n):, g] for g, (w, _) in enumerate(DIL_PATTERNS)]
    return (y_prompt, y_sample, pool_p, pool_s, kv_p_groups[0], kv_p_groups[1], kv_p_groups[2],
            kv_s[:, :, 0], kv_s[:, :, 1], kv_s[:, :, 2])


_drawn_inputs = setup_inputs


def setup_inputs(seed=0):
    import zlib

    import numpy as np

    out = dict(_drawn_inputs(seed))
    spreads = {}
    factors = {'cache_kv_w128': 3.27, 'cache_kv_w512': 3.046, 'cache_kv_w2048': 3.248, 'rel_bias': 6.792}
    for name, (base, spread) in spreads.items():
        noise = np.random.default_rng([zlib.crc32(name.encode()), seed]).standard_normal(out[name].shape)
        drawn = base * np.exp(spread * noise) if base else spread * noise
        out[name] = __import__('jax').numpy.asarray(drawn.astype(out[name].dtype))
    for name, factor in factors.items():
        out[name] = (out[name] * factor).astype(out[name].dtype)
    return out
```

```python
import math
from contextlib import ExitStack

import concourse.bass as bass
import numpy as np
from concourse import mybir

F32 = mybir.dt.float32
F32R = mybir.dt.float32r
ACT = mybir.ActivationFunctionType
ALU = mybir.AluOpType
AX_X = mybir.AxisListType.X

P = 128
D, SEQ, DEC_B, DEC_S = 1024, 512, 8, 4
SAMP = DEC_B * DEC_S
T = SEQ + SAMP
HALF = T // 2
DC = D // P
FF = 2816
FC = FF // P
KH = FC // 2
PAD = 15
DH = 64
HEADS = 8
GW = HEADS * DH
GC = GW // P
NG = 3
DIL = (1, 4, 16)
WIN = (128, 512, 2048)
NKEY = 129
NBUCKET, MAXDIST = 32, 2048
QB = SEQ // P
ALPHA = (2.0 * 2) ** 0.25
LN_EPS = 1e-5 / ALPHA ** 2
NEG = -1e30
RP = 384
SK = 390

PG, PB, PS = 0, 48, 96
NPAR = 104

STAGES = [("up0", 22, 8), ("down0", 8, 11), ("pin", 4, 8), ("pgrp", 4, 2), ("pout", 4, 8),
          ("up1", 22, 8), ("down1", 8, 11), ("up2", 22, 8), ("down2", 8, 11),
          ("q", 6, 8), ("kv", 12, 8), ("wo", 4, 4), ("up3", 22, 8), ("down3", 8, 11)]
RES = ("down0", "pout", "down1", "down2", "wo", "down3")
UNITS = {n: u for n, u, _ in STAGES}
KT = {n: k for n, _, k in STAGES}
FIRST, AFTER = {}, {}
_at = 0
for _j, (_n, _u, _k) in enumerate(STAGES):
    FIRST[_n] = _at
    _at += _u
    AFTER[_n] = STAGES[_j + 1][0] if _j + 1 < len(STAGES) else None


def t5_bucket(dist):
    exact = NBUCKET // 2
    if dist < exact:
        return dist
    return min(exact + int(math.log(dist / exact) / math.log(MAXDIST / exact) * (NBUCKET - exact)), NBUCKET - 1)


def shape_constants():
    table = np.zeros((NBUCKET + 1, NG, RP), np.float32)
    for x in range(RP):
        for g in range(NG):
            if g == 0:
                d = 255 - x
                ok, j = 0 <= d < NKEY, d
            else:
                d = 127 - x
                step = DIL[g] // DIL[1]
                ok, j = d >= 0 and d % step == 0 and d // step < NKEY, d // step
            table[t5_bucket(j * DIL[g]) if ok else NBUCKET, g, x] = 1.0
    samp = np.zeros((NBUCKET + 1, 6, SK), np.float32)
    for i in range(DEC_S):
        for r in range(P + DEC_S):
            j = P + i - r
            col = r if r < P else 3 * P + r - P
            samp[t5_bucket(j) if 0 <= j < NKEY else NBUCKET, i, col] = 1.0
    for g in (1, 2):
        for r in range(P):
            samp[t5_bucket((P - r) * DIL[g]), 3 + g, g * P + r] = 1.0
        samp[t5_bucket(0), 3 + g, 3 * P + DEC_S + g - 1] = 1.0
    inv = np.zeros((4, 16), np.float32)
    for g in range(4):
        for t in range(16):
            inv[g, t] = 1.0 / min(t + 1, 2 ** (g + 1))
    return {"c_table": table, "c_samp": samp, "c_inv": inv.reshape(1, 64), "c_ident": np.eye(P, dtype=np.float32)}


def first_turn(i):
    return isinstance(i, int) and i == 0


class Steps:

    def __init__(self, sem):
        self.sem, self.n, self.i, self.start = sem, 0, None, 0

    def add(self, instruction, k=1):
        instruction.then_inc(self.sem, k)
        self.n += k

    def value(self):
        if self.i is None:
            return self.n
        return self.start + self.per * self.i + (self.n - self.start)

    def turn(self, i, per):
        self.i, self.per, self.start = i, per, self.n

    def turns(self, count):
        assert self.n - self.start == self.per, (self.n - self.start, self.per)
        self.n, self.i = self.start + count * self.per, None


def build(nc, A, O):
    ctx = ExitStack()
    names = [0]

    def sb(where, name, shape, dt=F32):
        return where.enter_context(nc.sbuf_tensor("t_" + name, shape, dt))

    def sem(name):
        return ctx.enter_context(nc.semaphore(name))

    with ctx:
        x = sb(ctx, "stream", [P, DC, T])
        raw = [sb(ctx, f"w_raw{s}", [P, KH, P]) for s in range(2)]
        whi = [sb(ctx, f"w_hi{s}", [P, KH, P], F32R) for s in range(2)]
        wlo = [sb(ctx, f"w_lo{s}", [P, KH, P], F32R) for s in range(2)]
        ident = sb(ctx, "ident", [P, P])
        invd = sb(ctx, "inv_d", [P, P])
        par = sb(ctx, "params", [P, NPAR])
        eps = sb(ctx, "eps", [P, 1])
        sg = sb(ctx, "silu", [P, T])
        hf = sb(ctx, "hidden", [P, T])
        sq = sb(ctx, "square", [P, T])
        tab = sb(ctx, "bias_rows", [HEADS, NG, RP])
        sb_w = sb(ctx, "samp_bias_new", [P, SK])
        work = sb(ctx, "work", [P, 5 * T])
        accs, accq, mean, var, rstd = (work[:, j * T:(j + 1) * T] for j in range(5))
        q_tok = work[0:SAMP, 0:NG * GW]
        s_sc = work[:, 1536:1536 + NG * 256].rearrange("p (g n) -> p g n", g=NG)
        s_bias = work[:, 2304:2304 + SK]
        hist = sb(ctx, "history", [P, DC, DEC_B * PAD])
        inv = sb(ctx, "inv_count", [P, 4, 16])

        rx = ExitStack()
        xhi = sb(rx, "x_hi", [P, DC, T], F32R)
        xlo = sb(rx, "x_lo", [P, DC, T], F32R)
        rh = ExitStack()
        hhi = sb(rh, "h_hi", [P, FC, T], F32R)
        hlo = sb(rh, "h_lo", [P, FC, T], F32R)
        rh.close()
        xtok = sb(rh, "x_tok", [P, 5, D])
        ptok = sb(rh, "par_tok", [NPAR, P])
        sttok = sb(rh, "state_tok", [DEC_B * PAD, D])
        oh_t = sb(rh, "onehot_table", [NBUCKET + 1, NG, RP])
        oh_s = sb(rh, "onehot_samp", [NBUCKET + 1, 6, SK])
        rbx = sb(rh, "bucket_bias", [NBUCKET + 1, NG * HEADS])
        rb_s = sb(rh, "bucket_bias_samp", [NBUCKET + 1, 6, P])
        rh.close()
        phi = sb(rh, "pool_hi", [P, DC, T], F32R)
        plo = sb(rh, "pool_lo", [P, DC, T], F32R)
        ue = [sb(rh, f"u_ext{s}", [P, 16 + SEQ + DEC_B * 20]) for s in range(2)]
        us = [sb(rh, f"u_sum{s}", [P, 16 + SEQ + DEC_B * 20]) for s in range(2)]
        utail = sb(rh, "u_tail", [P, DC, PAD + SAMP])
        utok = sb(rh, "u_tok", [PAD + SAMP, D])
        zhi = sb(rh, "z_hi", [P, DC, T], F32R)
        zlo = sb(rh, "z_lo", [P, DC, T], F32R)
        rh.close()
        qt = sb(rh, "q_feat", [P, NG * GC, T])
        hq = ExitStack()
        yhi = sb(hq, "kv_in_hi", [P, DC, T], F32R)
        ylo = sb(hq, "kv_in_lo", [P, DC, T], F32R)
        kvt = [sb(hq, f"kv_feat{s}", [P, T]) for s in range(2)]
        kvp = [sb(hq, f"kv_tok{s}", [P, QB, P]) for s in range(2)]
        kvs = [sb(hq, f"kv_samp{s}", [SAMP, P]) for s in range(2)]
        q_b1b = sb(hq, "q_cast1b", [P, DEC_S, GW])
        q_b2 = [sb(hq, f"q_cast2{s}", [P, DEC_S, GW]) for s in range(2)]
        hq.close()
        vc1 = [sb(hq, f"v_cache1{s}", [P, DEC_S, GW]) for s in range(2)]
        vc2 = [sb(hq, f"v_cache2{s}", [P, DEC_S, GW]) for s in range(2)]
        vc0 = [sb(hq, f"v_cache0{s}", [P, GW]) for s in range(2)]
        prod_n = sb(hq, "prod_new", [SAMP, 6, GW])
        s_new = sb(hq, "s_new", [SAMP, HEADS, 6])
        p_new = sb(hq, "p_new", [SAMP, HEADS, 6])
        o_new = sb(hq, "o_new", [SAMP, GW])
        s_row = sb(hq, "s_rows", [P, 2, SK])
        p_row = sb(hq, "p_rows", [P, 2, SK])
        s_nr = sb(hq, "s_new_rows", [P, 2, 6])
        s_stat = sb(hq, "s_stats", [P, 8])
        p_key = sb(hq, "p_keys", [P, NG, 256])
        hq.close()
        kt0 = sb(hq, "k_feat0", [P, GC, SEQ])
        kt12 = sb(hq, "k_feat12", [P, 2 * GC, SEQ])
        v_p = [sb(hq, f"v_prompt{g}", [P, QB, GW]) for g in range(NG)]
        b12 = sb(hq, "bias12", [P, HEADS, 256])
        q_r = sb(hq, "q_tile", [P, NG * GC, P])
        k_r = sb(hq, "k_tile", [P, 2 * GC, P])
        hq.close()
        rh.close()
        ohi = sb(rh, "o_hi", [P, GC, T], F32R)
        olo = sb(rh, "o_lo", [P, GC, T], F32R)
        rh.close()
        ytok = sb(rh, "y_tok", [P, QB + 1, D])
        rh.close()
        rx.close()
        kc1 = sb(rx, "k_cache1", [P, DEC_S, GW])
        kc2 = sb(rx, "k_cache2", [P, DEC_S, GW])
        kc0 = sb(rx, "k_cache0", [P, GW])
        q_b0 = sb(rx, "q_cast0", [P, DEC_S, GW])
        q_b1 = [sb(rx, "q_cast1a", [P, DEC_S, GW]), q_b1b]
        rx.close()
        ot = sb(rx, "o_feat", [P, GC, T])
        ro = ExitStack()
        k_new = sb(ro, "k_new", [SAMP, 6, GW])
        v_new = sb(ro, "v_new", [SAMP, 6, GW])
        ro.close()
        b0 = sb(ro, "bias0", [P, HEADS, 256])
        s_p = [sb(ro, f"s_prompt{s}", [P, 512]) for s in range(2)]
        p_p = [sb(ro, f"p_prompt{s}", [P, 512]) for s in range(2)]
        pt_p = [sb(ro, f"pt_prompt{s}", [P, 512]) for s in range(2)]
        o_n = sb(ro, "o_tok", [P, GW])
        a_stat = sb(ro, "a_stats", [P, 4, QB, HEADS])
        ro.close()
        rx.close()

        ps = [ctx.enter_context(nc.psum_tensor(f"pair{j}", [P, 2, 512], F32)) for j in range(4)]
        pa, pb, pc, pd = ps

        def halves(t):
            return t[:, :, 0:HALF]

        def split(t):
            return t.rearrange("p (a n) -> p a n", a=2)

        kt_d = nc.dram_tensor("scratch_kt", [NG * GC, P, SEQ], F32)
        kv0_d = nc.dram_tensor("scratch_kv0", [SEQ, 2 * GW], F32)
        xs_d = nc.dram_tensor("scratch_x_parts", [2, P, DC * T], F32)
        tab_d = nc.dram_tensor("scratch_bias_rows", [NG, HEADS, P, RP], F32)
        sb_d = nc.dram_tensor("scratch_samp_bias", [P, SK], F32)
        q_d = nc.dram_tensor("scratch_q", [SAMP, NG * GW], F32)
        sn_d = nc.dram_tensor("scratch_s_new", [SAMP, HEADS * 6], F32)
        pn_d = nc.dram_tensor("scratch_p_new", [2 * P, 6], F32)

        raw_in = [sem(f"raw_in{s}") for s in range(2)]
        hi_made = [sem(f"hi_made{s}") for s in range(2)]
        lo_made = [sem(f"lo_made{s}") for s in range(2)]
        w_used = [sem(f"w_used{s}") for s in range(2)]
        consts_in = sem("consts_in")
        xtok_in = sem("xtok_in")
        ptok_in = sem("ptok_in")
        consts_made = sem("consts_made")
        par_t = sem("par_transposed")
        par_ok = sem("par_ready")
        in_t = sem("in_transposed")
        in_evac = sem("in_evacuated")
        x_ready = sem("x_parts_ready")
        act_step = sem("act_step")
        dve_step = sem("dve_step")
        pool_step = sem("pool_step")
        res_made = sem("residual_made")
        sq_made = sem("squares_made")
        acc_made = sem("sums_made")
        acc_zero = sem("sums_zero")
        stats = sem("norm_sums")
        ln_mean = sem("norm_mean")
        ln_var = sem("norm_var")
        ln_std = sem("norm_std")
        ln_t = sem("norm_scaled")
        ln_x = sem("norm_out")
        gate_silu = sem("gate_silu")
        h_made = sem("hidden_made")
        h_hi_made = sem("hidden_hi_made")
        h_lo_made = sem("hidden_lo_made")
        u_evac = sem("u_evacuated")
        st_in = sem("state_in")
        st_t = sem("state_transposed")
        st_evac = sem("state_evacuated")
        pooled = sem("pooled")
        utail_t = sem("u_tail_transposed")
        utok_ok = sem("u_tok_ready")
        z_scaled = sem("z_scaled")
        z_hi_made = sem("z_hi_made")
        z_ready = sem("z_parts_ready")
        kv_evac = [sem(f"kv_evacuated{s}") for s in range(2)]
        kv_t = [sem(f"kv_transposed{s}") for s in range(2)]
        kv_tok = [sem(f"kv_tok_ready{s}") for s in range(2)]
        kt_out = [sem(f"kt_stored{s}") for s in range(2)]
        kv_out = [sem(f"kv_stored{s}") for s in range(2)]
        utok_out = sem("u_tok_stored")
        tab_in = sem("tab_in")
        rb_copied = sem("rb_copied")
        tab_mm = sem("tab_mm")
        tab_evac = sem("tab_evac")
        sb_mm = sem("sb_mm")
        sb_evac = sem("sb_evac")
        tab_out = sem("tab_out")
        sb_out = sem("sb_out")
        xs_out = sem("xs_out")
        xs_in = sem("xs_in")
        q_evac = sem("q_evac")
        q_tr = sem("q_tr")
        qtok_ok = sem("qtok_ok")
        q_out = sem("q_out")
        c0_in = sem("c0_in")
        c1_in = sem("c1_in")
        c2_in = sem("c2_in")
        mul0 = sem("mul0")
        mul1 = sem("mul1")
        mul2 = sem("mul2")
        red0 = sem("red0")
        red1 = sem("red1")
        red2 = sem("red2")
        knew_in = sem("knew_in")
        vnew_in = sem("vnew_in")
        sbias_in = sem("sbias_in")
        snew_ok = sem("snew_ok")
        snew_out = sem("snew_out")
        snr_in = sem("snr_in")
        srow_t = sem("srow_t")
        srow_ok = sem("srow_ok")
        smax_ok = sem("smax_ok")
        sexp_ok = sem("sexp_ok")
        snorm_ok = sem("snorm_ok")
        pkey_t = sem("pkey_t")
        pkey_ok = sem("pkey_ok")
        pnew_out = sem("pnew_out")
        pnew_in = sem("pnew_in")
        onew_ok = sem("onew_ok")
        onew_t = sem("onew_t")
        vcache_in = [sem(f"vcache_in{s}") for s in range(2)]
        sv_done = sem("sv_done")
        ots_ok = sem("ots_ok")
        kt_in = sem("kt_in")
        v_in = sem("v_in")
        b12_in = sem("b12_in")
        b0_pad = sem("b0_pad")
        qk_ok = sem("qk_ok")
        s_done = sem("s_done")
        s_ok = sem("s_ok")
        p_ok = sem("p_ok")
        pt_done = sem("pt_done")
        pt_ok = sem("pt_ok")
        pv_done = sem("pv_done")
        on_ok = sem("on_ok")
        on_t = sem("on_t")
        ot_ok = sem("ot_ok")
        o_ready = sem("o_ready")
        ohi_ok = sem("ohi_ok")
        y_t = sem("y_t")
        y_ok = [sem(f"y_ok{s}") for s in range(2)]
        y_out = sem("y_out")
        b0_in = [sem(f"b0_in{h}") for h in range(2)]
        done = sem("outputs_done")
        DONE = [0]

        def rows(w):
            return w.rearrange("(k p) n -> p k n", p=P)

        w13 = [rows(A["ffn_w13"][f // 2, f % 2]) for f in range(4)]
        w2 = [rows(A["ffn_w2"][f // 2, f % 2]) for f in range(4)]
        w_pin, w_pout = rows(A["pool_w_in"][0]), rows(A["pool_w_out"][0])
        w_grp = A["pool_w_grp"][0].rearrange("g (k p) n -> p g k n", p=P)
        w_kv, w_q, w_o = rows(A["attn_w_kv"]), rows(A["attn_w_q"][0]), rows(A["attn_w_o"][0])

        def unit_source(stage, s, i):
            if stage[:2] == "up":
                return w13[int(stage[2])][:, :, bass.ds(FF * s + i * P, P)]
            if stage[:4] == "down":
                return w2[int(stage[4])][:, KH * s:KH * (s + 1), bass.ds(i * P, P)]
            if stage == "pgrp":
                return w_grp[:, i, :, s * P:(s + 1) * P]
            w = {"pin": w_pin, "pout": w_pout, "kv": w_kv, "q": w_q, "wo": w_o}[stage]
            return w[:, :, bass.ds(2 * i * P + s * P, P)]

        block = ctx.enter_context(nc.Block())

        @block.sync
        def _(sp):
            def load(dst, src, s, k=16):
                sp.dma_start(dst, src).then_inc(s, k)

            load(ident[:], A["c_ident"], consts_in)
            load(inv[:].rearrange("p g t -> p (g t)"), A["c_inv"].partition_broadcast(P).rearrange("q a n -> q (a n)"),
                 consts_in)
            load(sttok[:], A["state_pool"][0].rearrange("b t d -> (b t) d"), st_in)
            load(xtok[:, 0:4, :], A["x_prompt"][0].rearrange("(j p) d -> p j d", p=P), xtok_in)
            load(xtok[0:SAMP, 4, :], A["x_sample"].rearrange("b s d -> (b s) d"), xtok_in)
            load(ptok[PG:PB, :], A["ln_g"].rearrange("l s (c p) -> (l s c) p", p=P), ptok_in)
            load(ptok[PB:PS, :], A["ln_b"].rearrange("l s (c p) -> (l s c) p", p=P), ptok_in)
            load(ptok[PS:NPAR, :], A["pool_scale"][0].rearrange("(c p) -> c p", p=P), ptok_in)

            load(oh_t[:], A["c_table"], tab_in)
            load(oh_s[:], A["c_samp"], tab_in)
            sp.wait_ge(rb_copied, 1)
            load(rbx[0:NBUCKET, :], A["rel_bias"], tab_in)

            def stream(stage, i):
                for s in range(2):
                    if not (stage == "up0" and first_turn(i)):
                        sp.wait_ge(lo_made[s], FIRST[stage] + i)
                    sp.dma_start(raw[s][:, 0:KT[stage], :], unit_source(stage, s, i)).then_inc(raw_in[s], 16)

            def stream_all(stage, start=0):
                with sp.Fori(start, UNITS[stage]) as i:
                    stream(stage, i)

            stream("up0", 0)
            stream_all("up0", 1)
            sp.wait_ge(tab_evac, NG)
            for g in range(NG):
                sp.dma_start(tab_d.ap()[g], tab[:, g, :].unsqueeze(1).to_broadcast([HEADS, P, RP])).then_inc(tab_out, 16)
            sp.wait_ge(sb_evac, 1)
            sp.dma_start(sb_d.ap(), sb_w[:]).then_inc(sb_out, 16)
            for stage in ("down0", "pin", "pgrp", "pout", "up1", "down1"):
                stream_all(stage)
            stream("up2", 0)
            stream("up2", 1)
            sp.wait_ge(x_ready, 4 * DC)
            for n, part in enumerate((xhi, xlo)):
                sp.dma_start(xs_d.ap()[n], part[:].rearrange("p c t -> p (c t)").bitcast(F32)).then_inc(xs_out, 16)
            stream_all("up2", 2)
            stream_all("down2")
            stream("q", 0)
            sp.wait_ge(res_made, DC * RES.index("down2") + DC)
            sp.wait_ge(xs_out, 32)
            for n, part in enumerate((yhi, ylo)):
                sp.dma_start(part[:].rearrange("p c t -> p (c t)").bitcast(F32), xs_d.ap()[n]).then_inc(xs_in, 16)
            stream_all("q", 1)

            def kt_store(i, s):
                g, j = i // 4, i % 4
                if j < 2:
                    sp.wait_ge(kv_evac[s], i + 1)
                    sp.dma_start(kt_d.ap()[g * GC + 2 * j + s], kvt[s][:, 0:SEQ]).then_inc(kt_out[s], 16)

            def kv_store(i, s):
                g, col = i // 4, ((i % 4) * 2 + s) * P
                sp.wait_ge(kv_tok[s], 2 * i + 2)
                if g == 0:
                    sp.dma_start(kv0_d.ap().rearrange("(j p) n -> p j n", p=P)[:, :, col:col + P],
                                 kvp[s][:]).then_inc(kv_out[s], 16)
                    sp.dma_start(O["kv_p0"].rearrange("b w k h d -> (b w) (k h d)")[:, col:col + P],
                                 kvp[s][:, QB - 1, :]).then_inc(kv_out[s], 16)
                else:
                    view = O[f"kv_p{g}"].rearrange("b (j p) k h d -> p (b j) (k h d)", p=P)
                    for h in range(2):
                        sp.dma_start(view[:, 2 * h:2 * h + 2, col:col + P],
                                     kvp[s][:, 2 * h:2 * h + 2, :]).then_inc(kv_out[s], 16)
                sp.dma_start(O[f"kv_s{g}"].rearrange("b t k h d -> (b t) (k h d)")[:, col:col + P],
                             kvs[s][:]).then_inc(kv_out[s], 16)

            c0 = A["cache_kv_w128"].rearrange("b p k h d -> b p k (h d)")
            c1 = A["cache_kv_w512"].rearrange("b (p i) k h d -> b p i k (h d)", i=DIL[1])
            c2 = A["cache_kv_w2048"].rearrange("b (p i) k h d -> b p i k (h d)", i=DIL[2])

            def q_cast(b, g):
                return q_d.ap()[DEC_S * b:DEC_S * (b + 1), g * GW:(g + 1) * GW].partition_broadcast(P)

            def sample_keys(b):
                if b >= 1:
                    sp.wait_ge(mul0, b)
                    sp.wait_ge(red0, b)
                load(kc0[:], c0[b, :, 0, :], c0_in)
                load(q_b0[:], q_cast(b, 0), c0_in)
                if b >= 1:
                    sp.wait_ge(mul1, b)
                if b >= 2:
                    sp.wait_ge(red1, b - 1)
                load(kc1[:], c1[b, :, :, 0, :], c1_in)
                load(q_b1[b % 2][:], q_cast(b, 1), c1_in)
                if b >= 1:
                    sp.wait_ge(mul2, b)
                if b >= 2:
                    sp.wait_ge(red2, b - 1)
                load(kc2[:], c2[b, :, 0:DEC_S, 0, :], c2_in)
                load(q_b2[b % 2][:], q_cast(b, 2), c2_in)

            for i in range(UNITS["kv"]):
                stream("kv", i)
                if i == 0:
                    sp.wait_ge(qtok_ok, NG)
                    sp.dma_start(q_d.ap(), q_tok).then_inc(q_out, 16)
                if i == 1:
                    sp.wait_ge(q_out, 16)
                if i >= 1:
                    kt_store(i - 1, 0)
                    if i >= 2:
                        kv_store(i - 2, 1)
                    kt_store(i - 1, 1)
                    kv_store(i - 1, 0)
                    if 2 <= i < DEC_B + 2:
                        sample_keys(i - 2)
            stream("wo", 0)
            kv_store(UNITS["kv"] - 2, 1)
            kv_store(UNITS["kv"] - 1, 0)
            kv_store(UNITS["kv"] - 1, 1)

            sp.wait_ge(mul0, DEC_B)
            sp.wait_ge(red0, DEC_B)
            sp.wait_ge(red1, DEC_B)
            sp.wait_ge(red2, DEC_B)
            for s in range(2):
                sp.wait_ge(kv_out[s], 48 * UNITS["kv"])
            sp.wait_ge(sb_out, 16)
            load(s_bias, sb_d.ap(), sbias_in)
            new = [O[f"kv_s{g}"].rearrange("b t k h d -> b t k (h d)") for g in range(NG)]
            for k, (dst, into) in enumerate(((k_new, knew_in), (v_new, vnew_in))):
                for j in range(DEC_S):
                    for b in range(DEC_B):
                        load(dst[DEC_S * b:DEC_S * (b + 1), j, :], new[0][b, j, k, :].partition_broadcast(DEC_S), into)
                for g in (1, 2):
                    load(dst[:, DEC_S + g - 1, :], new[g].rearrange("b t k n -> (b t) k n")[:, k, :], into)

            def sample_values(b):
                if b >= 2:
                    sp.wait_ge(sv_done, b - 1)
                load(vc0[b % 2][:], c0[b, :, 1, :], vcache_in[b % 2])
                load(vc1[b % 2][:], c1[b, :, :, 1, :], vcache_in[b % 2])
                load(vc2[b % 2][:], c2[b, :, 0:DEC_S, 1, :], vcache_in[b % 2])

            sample_values(0)
            sample_values(1)
            sp.wait_ge(snew_ok, 1)
            sp.dma_start(sn_d.ap(), s_new[:].rearrange("p h j -> p (h j)")).then_inc(snew_out, 16)
            sp.wait_ge(snew_out, 16)
            load(s_nr[:],
                 bass.AP(tensor=sn_d, offset=0, ap=[[6, P], [6 * P, 2], [1, 6]]), snr_in)
            sp.wait_ge(snorm_ok, 1)
            sp.dma_start(bass.AP(tensor=pn_d, offset=0, ap=[[6, P], [6 * P, 2], [1, 6]]),
                         p_row[:, :, NG * P:SK]).then_inc(pnew_out, 16)
            sp.wait_ge(pnew_out, 16)
            load(p_new[:].rearrange("p h j -> p (h j)"),
                 bass.AP(tensor=pn_d, offset=0, ap=[[HEADS * 6, SAMP], [1, HEADS * 6]]), pnew_in)
            for b in range(2, DEC_B):
                sample_values(b)

            sp.wait_ge(ots_ok, 1)
            sp.wait_ge(tab_out, 16 * NG)
            for s in range(2):
                sp.wait_ge(kt_out[s], 16 * UNITS["kv"] // 2)
            load(kt0[:], kt_d.ap()[0:GC].rearrange("c p t -> p c t"), kt_in)
            load(kt12[:], kt_d.ap()[GC:NG * GC].rearrange("c p t -> p c t"), kt_in)
            for g in (1, 2):
                load(b12[:, :, (g - 1) * P:g * P],
                     bass.AP(tensor=tab_d, offset=g * HEADS * P * RP + P - 1, ap=[[RP - 1, P], [P * RP, HEADS], [1, P]]),
                     b12_in)

            def bias0(r, h, first=False):
                if not first:
                    sp.wait_ge(s_ok, HEADS * (r - 1) + 4 * h + 4)
                for c in range(QB):
                    k0 = P if c == 0 else 0
                    sp.dma_start(b0[32 * c:32 * c + 32, 4 * h:4 * h + 4, k0:256],
                                 bass.AP(tensor=tab_d, offset=4 * h * P * RP + P - 1 - r + k0,
                                         ap=[[RP - 4, 32], [P * RP, 4], [1, 256 - k0]])).then_inc(b0_in[h], 16)

            sp.wait_ge(b0_pad, 1)
            bias0(0, 0, True)
            bias0(0, 1, True)
            load(v_p[0][:], kv0_d.ap().rearrange("(c p) n -> p c n", p=P)[:, :, GW:2 * GW], v_in)
            for g in (1, 2):
                load(v_p[g][:], O[f"kv_p{g}"].rearrange("b (p r) k h d -> p (b r) k (h d)", r=QB)[:, :, 1, :], v_in)
            for r in range(1, QB):
                bias0(r, 0)
                bias0(r, 1)
            stream_all("wo", 1)
            stream_all("up3")
            stream_all("down3")

            out_p = O["y_p"].rearrange("b (j p) d -> p (b j) d", p=P)
            for j in range(QB):
                sp.wait_ge(y_ok[0], j + 1)
                sp.wait_ge(y_ok[1], j + 1)
                sp.dma_start(out_p[:, j, :], ytok[:, j, :]).then_inc(y_out, 16)
            sp.wait_ge(y_ok[0], QB + 1)
            sp.wait_ge(y_ok[1], QB + 1)
            sp.dma_start(O["y_s"].rearrange("b t d -> (b t) d"), ytok[0:SAMP, QB, :]).then_inc(y_out, 16)
            sp.wait_ge(y_out, 16 * (QB + 1))
            sp.dma_start(O["pool_s"][0, :, 0:PAD - DEC_S, :], A["state_pool"][0, :, DEC_S:PAD, :]).then_inc(done, 16)
            sp.wait_ge(done, 16)
            sp.wait_ge(utok_out, 32)
            for s in range(2):
                sp.wait_ge(kv_out[s], 48 * UNITS["kv"])
                sp.wait_ge(kt_out[s], 16 * UNITS["kv"] // 2)

        @block.tensor
        def _(pe):
            def products(out, s, kt, hi, lo, first=True, last=True, each=None):
                for k in range(kt):
                    if each:
                        each(k)
                    for n, (w, a) in enumerate(((whi[s], hi), (whi[s], lo), (wlo[s], hi))):
                        for j in range(2):
                            m = nc.tensor.matmul(out[:, j, 0:HALF], w[:, k, :], a(k)[:, j * HALF:(j + 1) * HALF],
                                                 start=first and k == 0 and n == 0,
                                                 stop=last and k == kt - 1 and n == 2)
                return m

            def stream_x(k):
                return xhi[:, k, :]

            def stream_xl(k):
                return xlo[:, k, :]

            def chunk_wait(count):
                def each(k):
                    pe.wait_ge(x_ready, count - DC + k + 1)
                return each

            pe.wait_ge(consts_in, 32)
            pe.wait_ge(ptok_in, 48)
            nc.tensor.transpose(pc[:, 0, 0:NPAR], ptok[:], ident[0:NPAR, 0:NPAR]).then_inc(par_t, 1)
            pe.wait_ge(xtok_in, 32)
            for c in range(DC):
                if c >= 2:
                    pe.wait_ge(in_evac, c - 1)
                for j in range(QB):
                    nc.tensor.transpose(ps[c % 2][:, 0, j * P:(j + 1) * P], xtok[:, j, c * P:(c + 1) * P], ident[:])
                nc.tensor.transpose(ps[c % 2][:, 1, 0:SAMP], xtok[0:SAMP, 4, c * P:(c + 1) * P],
                                    ident[0:SAMP, 0:SAMP]).then_inc(in_t, 1)

            def up(stage, ready):
                f, base = int(stage[2]), FIRST[stage]

                def turn(i, each=None):
                    pe.wait_ge(lo_made[0], base + i + 1)
                    if each is None:
                        pe.wait_ge(gate_silu, FC * f + i)
                    products(pa, 0, DC, stream_x, stream_xl, each=each).then_inc(w_used[0], 1)
                    pe.wait_ge(lo_made[1], base + i + 1)
                    if each is None:
                        pe.wait_ge(h_made, FC * f + i)
                    products(pb, 1, DC, stream_x, stream_xl).then_inc(w_used[1], 1)

                turn(0, chunk_wait(ready))
                with pe.Fori(1, FC) as i:
                    turn(i)

            def down(stage):
                f, base = int(stage[4]), FIRST[stage]

                def chunk(i, out, first=False):
                    for s in range(2):
                        pe.wait_ge(lo_made[s], base + i + 1)
                        if first:
                            pe.wait_ge(h_lo_made, FC * f + (KH if s == 0 else FC))
                        elif s == 0:
                            pe.wait_ge(res_made, DC * RES.index(stage) + i - 1)
                        products(out, s, KH, lambda k: hhi[:, KH * s + k, :], lambda k: hlo[:, KH * s + k, :],
                                 first=s == 0, last=s == 1).then_inc(w_used[s], 1)

                chunk(0, pa, True)
                chunk(1, pb, True)
                with pe.Fori(2, DC, 2) as i:
                    chunk(i, pa)
                    chunk(i + 1, pb)

            def linear(stage, hi, lo, evac, ready=None, each=None):
                base = FIRST[stage]

                def turn(i, first):
                    for s in range(2):
                        pe.wait_ge(lo_made[s], base + i + 1)
                        if not first:
                            evac(s, i)
                        products(ps[s], s, KT[stage], hi, lo,
                                 each=chunk_wait(ready) if first and s == 0 and ready else None).then_inc(w_used[s], 1)

                turn(0, True)
                with pe.Fori(1, UNITS[stage]) as i:
                    turn(i, False)

            def norm(stage):
                for n, (acc, out) in enumerate(((accs, pc), (accq, pd))):
                    pe.wait_ge(acc_made, 2 * DC * RES.index(stage) + 2 * DC)
                    for j in range(2):
                        m = nc.tensor.matmul(out[:, j, 0:HALF], invd[:], acc[:, j * HALF:(j + 1) * HALF],
                                             start=True, stop=True)
                    m.then_inc(stats, 1)

            pe.wait_ge(st_in, 16)
            for c in range(DC):
                n = DEC_B * PAD
                m = nc.tensor.transpose(pd[:, c // 4, (c % 4) * n:(c % 4 + 1) * n], sttok[:, c * P:(c + 1) * P],
                                        ident[0:n, 0:n])
            m.then_inc(st_t, 1)
            pe.wait_ge(tab_in, 48)
            pe.wait_ge(rb_copied, 4)
            pe.wait_ge(par_ok, 1)
            pe.wait_ge(in_evac, DC)
            for g, out in enumerate((pa[:, 0, :], pa[:, 1, :], pb[:, 0, :])):
                m = nc.tensor.matmul(out[0:HEADS, 0:RP], rbx[:, g * HEADS:(g + 1) * HEADS], oh_t[:, g, :],
                                     start=True, stop=True)
            m.then_inc(tab_mm, 1)
            for v in range(6):
                m = nc.tensor.matmul(pc[:, 0, 0:SK], rb_s[:, v, :], oh_s[:, v, :], start=v == 0, stop=v == 5)
            m.then_inc(sb_mm, 1)
            pe.wait_ge(tab_evac, NG)
            pe.wait_ge(consts_made, 2)
            pe.wait_ge(in_evac, DC)
            ready = DC
            up("up0", ready)
            down("down0")
            norm("down0")
            ready += DC
            linear("pin", stream_x, stream_xl, lambda s, i: pe.wait_ge(u_evac, 2 * i - 1 + s), ready)
            pe.wait_ge(u_evac, DC)
            for c in range(DC):
                m = nc.tensor.transpose(pc[0:PAD + SAMP, c // 4, (c % 4) * P:(c % 4 + 1) * P], utail[:, c, :], ident[:])
            m.then_inc(utail_t, 1)
            for g in range(4):
                for s in range(2):
                    pe.wait_ge(lo_made[s], FIRST["pgrp"] + g + 1)
                    pe.wait_ge(pooled, 2 * g + 2)
                    if g >= 1:
                        pe.wait_ge(z_scaled, 2 * g - 1 + s)
                    products(ps[s], s, 2, lambda k: phi[:, 2 * g + k, :], lambda k: plo[:, 2 * g + k, :]) \
                        .then_inc(w_used[s], 1)
            pe.wait_ge(z_ready, DC)
            linear("pout", lambda k: zhi[:, k, :], lambda k: zlo[:, k, :],
                   lambda s, i: pe.wait_ge(res_made, DC * RES.index("pout") + 2 * i - 1 + s))
            norm("pout")
            ready += DC
            up("up1", ready)
            down("down1")
            norm("down1")
            ready += DC

            up("up2", ready)
            down("down2")
            norm("down2")
            ready += DC
            linear("q", stream_x, stream_xl, lambda s, i: pe.wait_ge(q_evac, 2 * i - 1 + s), ready)
            pe.wait_ge(q_evac, NG * GC)
            for c in range(NG * GC):
                out = (pc[:, 0, :], pc[:, 1, :], pd[:, 0, :])[c // GC]
                m = nc.tensor.transpose(out[0:SAMP, (c % GC) * P:(c % GC + 1) * P], qt[:, c, SEQ:T], ident[:])
            m.then_inc(q_tr, 1)

            def kv_units(s, i, first=False):
                pe.wait_ge(lo_made[s], FIRST["kv"] + i + 1)
                if not first:
                    pe.wait_ge(kv_evac[s], i)
                products(ps[s], s, DC, lambda k: yhi[:, k, :], lambda k: ylo[:, k, :]).then_inc(w_used[s], 1)

            def kv_transposes(s, i, first=False):
                pe.wait_ge(kv_evac[s], i + 1)
                if not first:
                    pe.wait_ge(kv_tok[s], 2 * i)
                for j in range(QB):
                    nc.tensor.transpose(ps[2 + s][:, 0, j * P:(j + 1) * P], kvt[s][:, j * P:(j + 1) * P], ident[:])
                nc.tensor.transpose(ps[2 + s][0:SAMP, 1, 0:P], kvt[s][:, SEQ:T], ident[:]).then_inc(kv_t[s], 1)

            pe.wait_ge(xs_in, 32)
            kv_units(0, 0, True)
            kv_units(1, 0, True)
            pe.wait_ge(qtok_ok, NG)
            kv_transposes(0, 0, True)
            kv_units(0, 1)
            kv_transposes(1, 0, True)
            kv_units(1, 1)
            kv_transposes(0, 1)
            with pe.Fori(2, UNITS["kv"]) as i:
                kv_units(0, i)
                kv_transposes(1, i - 1)
                kv_units(1, i)
                kv_transposes(0, i)
            kv_transposes(1, UNITS["kv"] - 1)

            pe.wait_ge(red0, DEC_B)
            pe.wait_ge(red1, DEC_B)
            pe.wait_ge(red2, DEC_B)
            pe.wait_ge(kv_evac[1], UNITS["kv"])
            for k in range(2):
                for g in range(NG):
                    m = nc.tensor.transpose(pa[:, k, g * P:(g + 1) * P], s_sc[:, g, k * P:(k + 1) * P], ident[:])
            m.then_inc(srow_t, 1)
            pe.wait_ge(snorm_ok, 1)
            for g in range(NG):
                for k in range(2):
                    at = (g % 2) * 256 + k * P
                    m = nc.tensor.transpose(pb[:, g // 2, at:at + P], p_row[:, k, g * P:(g + 1) * P], ident[:])
            m.then_inc(pkey_t, 1)
            pe.wait_ge(pkey_ok, 2)
            pe.wait_ge(kv_tok[0], 2 * UNITS["kv"])
            pe.wait_ge(kv_tok[1], 2 * UNITS["kv"])

            def sample_outputs(b, n, v):
                pe.wait_ge(vcache_in[v], 48 * n + 48)
                for c in range(GC):
                    rhs = p_key[:, 0, bass.ds(32 * b, 32)].rearrange("p (i h) -> p i h", h=HEADS)[:, :, 2 * c:2 * c + 2]
                    nc.tensor.matmul(pc[:, 0, bass.ds(64 * c + 8 * b, 8)], vc0[v][:, c * P:(c + 1) * P], rhs,
                                     start=True, stop=True)
                    for g, vc in ((1, vc1[v]), (2, vc2[v])):
                        for i in range(DEC_S):
                            m = nc.tensor.matmul(pd[:, g - 1, bass.ds(64 * c + 8 * b + 2 * i, 2)],
                                                 vc[:, i, c * P:(c + 1) * P],
                                                 p_key[:, g, bass.ds(32 * b + 8 * i + 2 * c, 2)], start=True, stop=True)
                m.then_inc(sv_done, 1)

            with pe.Fori(0, DEC_B // 2) as n:
                sample_outputs(2 * n, n, 0)
                sample_outputs(2 * n + 1, n, 1)
            pe.wait_ge(onew_ok, 1)
            for c in range(GC):
                m = nc.tensor.transpose(pc[:, 1, 32 * c:32 * c + SAMP], o_new[:, c * P:(c + 1) * P],
                                        ident[0:SAMP, 0:SAMP])
            m.then_inc(onew_t, 1)

            def scores(r, h, first):
                c, lo = h // 2, DH * (h % 2)
                out = pa[:, h % 2, :]
                hd = slice(lo, lo + DH)
                if h >= 2 or not first:
                    pe.wait_ge(s_ok, HEADS * r + h - 1)
                for g in (1, 2):
                    nc.tensor.matmul(out[:, (g + 1) * P:(g + 2) * P], q_r[hd, g * GC + c, :],
                                     k_r[hd, (g - 1) * GC + c, :], start=True, stop=True)
                for b in range(QB):
                    q = q_r[hd, c, 32 * b:32 * b + 32]
                    rows_ = slice(32 * b, 32 * b + 32)
                    if b == 0:
                        for half in range(2):
                            nc.tensor.matmul(out[rows_, half * P:(half + 1) * P], q, kt0[hd, c, 0:P],
                                             start=True, stop=True)
                    else:
                        m = nc.tensor.matmul(out[rows_, 0:256], q, kt0[hd, c, (b - 1) * P:(b + 1) * P],
                                             start=True, stop=True)
                m.then_inc(s_done, 1)

            def turn_probs(r, h, first):
                pe.wait_ge(p_ok, HEADS * r + h + 1)
                if not (first and h < 2):
                    pe.wait_ge(pt_ok, HEADS * r + h - 1)
                for k in range(4):
                    m = nc.tensor.transpose(pb[:, h % 2, k * P:(k + 1) * P], p_p[h % 2][:, k * P:(k + 1) * P], ident[:])
                m.then_inc(pt_done, 1)

            def values(r, h, first):
                pe.wait_ge(pt_ok, HEADS * r + h + 1)
                if h == 0 and not first:
                    pe.wait_ge(on_ok, r)
                out = pc[:, 0, h * DH:(h + 1) * DH]
                pt, cols = pt_p[h % 2], slice(h * DH, (h + 1) * DH)
                for g in (1, 2):
                    nc.tensor.matmul(out, pt[:, (g + 1) * P:(g + 2) * P], v_p[g][:, r, cols], start=g == 1, stop=False,
                                     skip_group_check=True)
                for b in range(QB):
                    rows_ = slice(32 * b, 32 * b + 32)
                    if b:
                        nc.tensor.matmul(out[rows_, :], pt[:, rows_], v_p[0][:, b - 1, cols],
                                         start=False, stop=False, skip_group_check=True)
                    m = nc.tensor.matmul(out[rows_, :], pt[:, P + 32 * b:P + 32 * b + 32], v_p[0][:, b, cols],
                                         start=False, stop=b == QB - 1, skip_group_check=True)
                m.then_inc(pv_done, 1)

            def tile(r, first):
                pe.wait_ge(qk_ok, GC * (r + 1))
                scores(r, 0, first)
                scores(r, 1, first)
                for h in range(HEADS):
                    turn_probs(r, h, first)
                    if h + 2 < HEADS:
                        scores(r, h + 2, first)
                    if first and h == 0:
                        pe.wait_ge(v_in, 16 * NG)
                    values(r, h, first)
                pe.wait_ge(on_ok, r + 1)
                if not first:
                    pe.wait_ge(ot_ok, r)
                for c in range(GC):
                    m = nc.tensor.transpose(pc[:, 1, c * P:(c + 1) * P], o_n[:, c * P:(c + 1) * P], ident[:])
                m.then_inc(on_t, 1)

            pe.wait_ge(kt_in, 32)
            pe.wait_ge(ots_ok, 1)
            tile(0, True)
            with pe.Fori(1, QB) as r:
                tile(r, False)
            pe.wait_ge(o_ready, 1)
            linear("wo", lambda k: ohi[:, k, :], lambda k: olo[:, k, :],
                   lambda s, i: pe.wait_ge(res_made, DC * RES.index("wo") + 2 * i - 1 + s))
            norm("wo")
            ready += DC
            up("up3", ready)
            down("down3")
            norm("down3")
            pe.wait_ge(ln_x, DC * RES.index("down3") + DC)
            for j in range(QB + 1):
                if j >= 2:
                    pe.wait_ge(y_ok[0], j - 1)
                    pe.wait_ge(y_ok[1], j - 1)
                n, t0 = (P, j * P) if j < QB else (SAMP, SEQ)
                for c in range(DC):
                    m = nc.tensor.transpose(ps[j % 2][0:n, c // 4, (c % 4) * P:(c % 4 + 1) * P], x[:, c, t0:t0 + n],
                                            ident[:])
                m.then_inc(y_t, 1)

        @block.scalar
        def _(act):
            step = Steps(act_step)

            def round_hi(stage, s, i):
                if stage is None:
                    return
                u = FIRST[stage] + i
                act.wait_ge(raw_in[s], 16 * (u + 1))
                if not (stage == "up0" and first_turn(i)):
                    act.wait_ge(w_used[s], u)
                nc.scalar.activation(whi[s][:, 0:KT[stage], :], raw[s][:, 0:KT[stage], :], ACT.Copy) \
                    .then_inc(hi_made[s], 1)

            def turns(n, stage, body):
                body(0, stage, 1)
                with act.Fori(1, n - 1) as i:
                    body(i, stage, i + 1)
                body(n - 1, AFTER[stage], 0)

            round_hi("up0", 0, 0)
            round_hi("up0", 1, 0)
            act.wait_ge(par_t, 1)
            nc.scalar.activation(par[:], pc[:, 0, 0:NPAR], ACT.Copy).then_inc(par_ok, 1)
            for c in range(DC):
                act.wait_ge(in_t, c + 1)
                nc.scalar.activation(x[:, c, 0:SEQ], ps[c % 2][:, 0, :], ACT.Copy)
                step.add(nc.scalar.activation(x[:, c, SEQ:T], ps[c % 2][:, 1, 0:SAMP], ACT.Copy))
                act.wait_ge(act_step, step.value())
                nc.scalar.activation(xhi[:, c, :], x[:, c, :], ACT.Copy).then_inc(in_evac, 1)
            act.wait_ge(tab_mm, 1)
            for g, src in enumerate((pa[:, 0, :], pa[:, 1, :], pb[:, 0, :])):
                nc.scalar.activation(tab[:, g, :], src[0:HEADS, 0:RP], ACT.Copy).then_inc(tab_evac, 1)
            act.wait_ge(sb_mm, 1)
            nc.scalar.activation(sb_w[:], pc[:, 0, 0:SK], ACT.Copy).then_inc(sb_evac, 1)
            act.wait_ge(st_t, 1)
            nc.scalar.activation(hist[:].rearrange("p (a c) n -> p a (c n)", a=2), pd[:, :, 0:4 * DEC_B * PAD],
                                 ACT.Copy).then_inc(st_evac, 1)

            def up(stage):
                f, base = int(stage[2]), FIRST[stage]

                def turn(i, nxt, j):
                    act.wait_ge(w_used[0], base + i + 1)
                    if not first_turn(i):
                        act.wait_ge(h_made, FC * f + i)
                    nc.scalar.activation(split(sg[:]), halves(pa), ACT.Silu).then_inc(gate_silu, 1)
                    round_hi(nxt, 0, j)
                    round_hi(nxt, 1, j)
                    act.wait_ge(h_made, FC * f + i + 1)
                    nc.scalar.activation(hhi[:, i, :], hf[:], ACT.Copy).then_inc(h_hi_made, 1)

                turns(FC, stage, turn)

            def square(stage, c, i):
                act.wait_ge(res_made, DC * RES.index(stage) + i + 1)
                if not first_turn(i):
                    act.wait_ge(acc_made, 2 * DC * RES.index(stage) + 2 * i)
                nc.scalar.activation(sq[:], x[:, c, :], ACT.Square).then_inc(sq_made, 1)

            def down(stage):
                def turn(i, nxt, j):
                    round_hi(nxt, 0, j)
                    round_hi(nxt, 1, j)
                    square(stage, i, i)

                turns(DC, stage, turn)

            def norm(stage, k):
                act.wait_ge(stats, 2 * RES.index(stage) + 1)
                nc.scalar.activation(split(mean[:]), halves(pc), ACT.Copy)
                nc.scalar.activation(split(var[:]), halves(pc), ACT.Square).then_inc(ln_mean, 1)
                act.wait_ge(ln_var, 1 * RES.index(stage) + 1)
                nc.scalar.activation(rstd[:], var[:], ACT.Sqrt, bias=eps[:, 0:1]).then_inc(ln_std, 1)
                for c in range(DC):
                    act.wait_ge(ln_t, DC * RES.index(stage) + c + 1)
                    m = nc.scalar.activation(x[:, c, :], x[:, c, :], ACT.Identity,
                                             bias=par[:, PB + k * DC + c:PB + k * DC + c + 1],
                                             scale=par[:, PG + k * DC + c:PG + k * DC + c + 1])
                    if stage == "down3":
                        m.then_inc(ln_x, 1)
                        continue
                    step.add(m)
                    act.wait_ge(act_step, step.value())
                    nc.scalar.activation(xhi[:, c, :], x[:, c, :], ACT.Copy).then_inc(ln_x, 1)

            up("up0")
            down("down0")
            norm("down0", 0)

            def pin(i, nxt, j):
                for s in range(2):
                    c = 2 * i + s
                    act.wait_ge(w_used[s], FIRST["pin"] + i + 1)
                    if i >= 1:
                        act.wait_ge(pooled, 2 * (i - 1) + s + 1)
                    else:
                        act.wait_ge(consts_made, 4)
                    samples = ue[s][:, 16 + SEQ:].rearrange("p (b t) -> p b t", t=20)[:, :, 16:20]
                    nc.scalar.activation(ue[s][:, 16:16 + HALF], ps[s][:, 0, 0:HALF], ACT.Copy)
                    nc.scalar.activation(ue[s][:, 16 + HALF:16 + SEQ], ps[s][:, 1, 0:SEQ - HALF], ACT.Copy)
                    nc.scalar.activation(samples, ps[s][:, 1, SEQ - HALF:HALF].rearrange("p (b t) -> p b t", t=4),
                                         ACT.Copy)
                    nc.scalar.activation(utail[:, c, :], ps[s][:, 1, HALF - PAD - SAMP:HALF], ACT.Copy) \
                        .then_inc(u_evac, 1)
                    round_hi(nxt, s, j)

            for i in range(UNITS["pin"]):
                if i + 1 < UNITS["pin"]:
                    pin(i, "pin", i + 1)
                else:
                    pin(i, "pgrp", 0)
            act.wait_ge(utail_t, 1)
            for b in range(2):
                m = nc.scalar.activation(utok[:, b * 512:(b + 1) * 512], pc[0:PAD + SAMP, b, :], ACT.Copy)
            m.then_inc(utok_ok, 1)

            def pgrp(i, nxt, j):
                for s in range(2):
                    c = 2 * i + s
                    act.wait_ge(w_used[s], FIRST["pgrp"] + i + 1)
                    if c >= 2:
                        act.wait_ge(z_ready, c - 1)
                    zf = (sg, hf)[s]
                    step.add(nc.scalar.activation(split(zf[:]), halves(ps[s]), ACT.Copy,
                                                  scale=par[:, PS + c:PS + c + 1]))
                    z_step = step.value()
                    act.wait_ge(act_step, z_step)
                    nc.scalar.activation(zhi[:, c, :], zf[:], ACT.Copy).then_inc(z_scaled, 1)
                for s in range(2):
                    round_hi(nxt, s, j)

            act.wait_ge(pooled, DC)
            for i in range(4):
                if i < 3:
                    pgrp(i, "pgrp", i + 1)
                else:
                    pgrp(i, "pout", 0)

            def residual_pair(stage):
                def turn(i, nxt, j):
                    for s in range(2):
                        round_hi(nxt, s, j)
                        square(stage, 2 * i + s, 2 * i + s)

                turns(UNITS[stage], stage, turn)

            residual_pair("pout")
            norm("pout", 1)
            act.wait_ge(utok_out, 32)
            up("up1")
            down("down1")
            norm("down1", 2)

            up("up2")
            down("down2")
            act.wait_ge(xs_out, 32)
            norm("down2", 3)

            def q_turn(i, nxt, j):
                for s in range(2):
                    act.wait_ge(w_used[s], FIRST["q"] + i + 1)
                    nc.scalar.activation(split(qt[:, 2 * i + s, :]), halves(ps[s]), ACT.Copy, scale=DH ** -0.5) \
                        .then_inc(q_evac, 1)
                    round_hi(nxt, s, j)

            turns(UNITS["q"], "q", q_turn)
            act.wait_ge(q_tr, 1)
            for g, src in enumerate((pc[:, 0, :], pc[:, 1, :], pd[:, 0, :])):
                nc.scalar.activation(q_tok[:, g * GW:(g + 1) * GW], src[0:SAMP, :], ACT.Copy).then_inc(qtok_ok, 1)

            def kv_chunk(s, i, stored, nxt, j, first=False):
                act.wait_ge(w_used[s], FIRST["kv"] + i + 1)
                if not first:
                    act.wait_ge(kv_t[s], i)
                    act.wait_ge(kt_out[s], 16 * stored)
                nc.scalar.activation(split(kvt[s][:]), halves(ps[s]), ACT.Copy).then_inc(kv_evac[s], 1)
                round_hi(nxt, s, j)

            def kv_tokens(s, i, first=False):
                act.wait_ge(kv_t[s], i + 1)
                if not first:
                    act.wait_ge(kv_out[s], 48 * i)
                nc.scalar.activation(kvp[s][:].rearrange("p j n -> p (j n)"), ps[2 + s][:, 0, :], ACT.Copy) \
                    .then_inc(kv_tok[s], 1)
                nc.scalar.activation(kvs[s][:], ps[2 + s][0:SAMP, 1, 0:P], ACT.Copy).then_inc(kv_tok[s], 1)

            def kv_turn(i, stored, nxt, j):
                kv_chunk(0, i, stored, nxt, j)
                kv_tokens(1, i - 1)
                kv_chunk(1, i, stored, nxt, j)
                kv_tokens(0, i)

            kv_chunk(0, 0, 0, "kv", 1, True)
            kv_chunk(1, 0, 0, "kv", 1, True)
            kv_tokens(0, 0, True)
            kv_chunk(0, 1, 1, "kv", 2)
            kv_tokens(1, 0, True)
            kv_chunk(1, 1, 1, "kv", 2)
            kv_tokens(0, 1)
            for g in range(NG):
                if g:
                    with act.Fori(0, 2) as i:
                        kv_turn(i + 4 * g, i + 2 * g, "kv", i + 4 * g + 1)
                if g < 2:
                    with act.Fori(0, 2) as i:
                        kv_turn(i + 4 * g + 2, 2 * g + 2, "kv", i + 4 * g + 3)
            kv_turn(10, 6, "kv", 11)
            kv_turn(11, 6, "wo", 0)
            kv_tokens(1, 11)

            act.wait_ge(smax_ok, 1)
            for k in range(2):
                nc.scalar.activation(p_row[:, k, :], s_row[:, k, :], ACT.Exp, bias=s_stat[:, 2 + k:3 + k],
                                     accum_out=s_stat[:, 4 + k:5 + k]).then_inc(sexp_ok, 1)
            act.wait_ge(pkey_t, 1)
            nc.scalar.activation(p_key[:, 0:2, :].rearrange("p g n -> p (g n)"), pb[:, 0, :], ACT.Copy).then_inc(pkey_ok, 1)
            nc.scalar.activation(p_key[:, 2, :], pb[:, 1, 0:256], ACT.Copy).then_inc(pkey_ok, 1)

            def exps(r, h, first):
                act.wait_ge(s_ok, HEADS * r + h + 1)
                if not (first and h < 2):
                    act.wait_ge(pt_done, HEADS * r + h - 1)
                nc.scalar.activation(p_p[h % 2][:], s_p[h % 2][:], ACT.Exp, bias=a_stat[:, 1, r, h:h + 1],
                                     accum_out=a_stat[:, 2, r, h:h + 1]).then_inc(p_ok, 1)

            def turned(r, h, first):
                act.wait_ge(pt_done, HEADS * r + h + 1)
                if not (first and h < 2):
                    act.wait_ge(pv_done, HEADS * r + h - 1)
                nc.scalar.activation(pt_p[h % 2][:], pb[:, h % 2, :], ACT.Copy).then_inc(pt_ok, 1)

            def tile(r, first):
                exps(r, 0, first)
                for h in range(HEADS):
                    if h + 1 < HEADS:
                        exps(r, h + 1, first)
                    turned(r, h, first)
                act.wait_ge(on_t, r + 1)
                tokens = ot[:, :, 0:SEQ].rearrange("p c (q r) -> p c q r", r=QB)
                nc.scalar.activation(tokens[:, :, :, r], pc[:, 1, :].rearrange("p (c q) -> p c q", c=GC), ACT.Copy) \
                    .then_inc(ot_ok, 1)

            tile(0, True)
            with act.Fori(1, QB) as r:
                tile(r, False)
            act.wait_ge(ot_ok, QB)
            nc.scalar.activation(ohi[:], ot[:], ACT.Copy).then_inc(ohi_ok, 1)
            residual_pair("wo")
            norm("wo", 4)
            up("up3")
            down("down3")
            norm("down3", 5)
            for j in range(QB + 1):
                n = P if j < QB else SAMP
                act.wait_ge(y_t, j + 1)
                nc.scalar.activation(ytok[0:n, j, 0:512], ps[j % 2][0:n, 0, :], ACT.Copy).then_inc(y_ok[0], 1)

        @block.vector
        def _(dve):
            step = Steps(dve_step)

            def round_lo(stage, s, i):
                if stage is None:
                    return
                k = KT[stage]
                dve.wait_ge(hi_made[s], FIRST[stage] + i + 1)
                nc.vector.tensor_tensor(wlo[s][:, 0:k, :], raw[s][:, 0:k, :], whi[s][:, 0:k, :].bitcast(F32),
                                        ALU.subtract).then_inc(lo_made[s], 1)

            def turns(n, stage, body):
                body(0, stage, 1)
                with dve.Fori(1, n - 1) as i:
                    body(i, stage, i + 1)
                body(n - 1, AFTER[stage], 0)

            nc.vector.memset(invd[:], 1.0 / D).then_inc(consts_made, 1)
            nc.vector.memset(eps[:], LN_EPS).then_inc(consts_made, 1)
            nc.vector.memset(rbx[NBUCKET:NBUCKET + 1, :], NEG).then_inc(rb_copied, 1)
            nc.vector.memset(rb_s[:], 0.0).then_inc(rb_copied, 1)
            round_lo("up0", 0, 0)
            round_lo("up0", 1, 0)
            dve.wait_ge(tab_in, 48)
            dve.wait_ge(rb_copied, 2)
            n = NBUCKET + 1
            for i in range(DEC_S):
                m = nc.vector.tensor_copy(
                    rb_s[:, i, :].rearrange("k (b i h) -> k b i h", i=DEC_S, h=HEADS)[:, :, i, :],
                    rbx[:, 0:HEADS].unsqueeze(1).to_broadcast([n, 4, HEADS]))
            m.then_inc(rb_copied, 1)
            for g in (1, 2):
                m = nc.vector.tensor_copy(rb_s[:, 3 + g, :].rearrange("k (t h) -> k t h", h=HEADS),
                                          rbx[:, g * HEADS:(g + 1) * HEADS].unsqueeze(1).to_broadcast([n, 16, HEADS]))
            m.then_inc(rb_copied, 1)
            for c in range(DC):
                dve.wait_ge(in_evac, c + 1)
                nc.vector.tensor_tensor(xlo[:, c, :], x[:, c, :], xhi[:, c, :].bitcast(F32), ALU.subtract) \
                    .then_inc(x_ready, 1)

            def up(stage):
                f, base = int(stage[2]), FIRST[stage]

                def turn(i, nxt, j):
                    round_lo(nxt, 0, j)
                    dve.wait_ge(w_used[1], base + i + 1)
                    dve.wait_ge(gate_silu, FC * f + i + 1)
                    if not first_turn(i):
                        dve.wait_ge(h_lo_made, FC * f + i)
                    nc.vector.tensor_tensor(split(hf[:]), split(sg[:]), halves(pb), ALU.mult).then_inc(h_made, 1)
                    round_lo(nxt, 1, j)
                    dve.wait_ge(h_hi_made, FC * f + i + 1)
                    nc.vector.tensor_tensor(hlo[:, i, :], hf[:], hhi[:, i, :].bitcast(F32), ALU.subtract) \
                        .then_inc(h_lo_made, 1)

                turns(FC, stage, turn)

            def residual(stage, out, c, scale, s, used):
                dve.wait_ge(w_used[s], used)
                nc.vector.scalar_tensor_tensor(out=split(x[:, c, :]), in0=halves(out), scalar=scale,
                                               in1=split(x[:, c, :]), op0=ALU.mult, op1=ALU.add) \
                    .then_inc(res_made, 1)

            def down(stage):
                base = FIRST[stage]

                def pair(i, last):
                    for h in range(2):
                        nxt, j = (AFTER[stage], 0) if last and h else (stage, i + h + 1)
                        round_lo(nxt, 0, j)
                        residual(stage, ps[h], i + h, 0.5 / ALPHA, 1, base + i + h + 1)
                        round_lo(nxt, 1, j)

                with dve.Fori(0, DC - 2, 2) as i:
                    pair(i, False)
                pair(DC - 2, True)

            def norm(stage, last=False):
                dve.wait_ge(stats, 2 * RES.index(stage) + 2)
                dve.wait_ge(ln_mean, 1 * RES.index(stage) + 1)
                nc.vector.tensor_tensor(split(var[:]), halves(pd), split(var[:]), ALU.subtract) \
                    .then_inc(ln_var, 1)
                dve.wait_ge(ln_std, 1 * RES.index(stage) + 1)
                step.add(nc.vector.reciprocal(rstd[:], rstd[:]))
                for c in range(DC):
                    step.add(nc.vector.tensor_tensor(x[:, c, :], x[:, c, :], mean[:], ALU.subtract))
                    dve.wait_ge(dve_step, step.value())
                    nc.vector.tensor_tensor(x[:, c, :], x[:, c, :], rstd[:], ALU.mult).then_inc(ln_t, 1)
                    if c >= 1 and not last:
                        low(stage, c - 1)
                if not last:
                    low(stage, DC - 1)

            def low(stage, c):
                dve.wait_ge(ln_x, DC * RES.index(stage) + c + 1)
                nc.vector.tensor_tensor(xlo[:, c, :], x[:, c, :], xhi[:, c, :].bitcast(F32), ALU.subtract) \
                    .then_inc(x_ready, 1)

            up("up0")
            down("down0")
            norm("down0")

            for s in range(2):
                nc.vector.memset(ue[s][:, 0:16], 0.0).then_inc(consts_made, 1)
            def pin(i, nxt, j):
                for s in range(2):
                    c = 2 * i + s
                    g = c // 2
                    tail = lambda t: t[:, 16 + SEQ:].rearrange("p (b t) -> p b t", t=20)
                    e = ue[s]
                    if i == 0:
                        dve.wait_ge(st_evac, 1)
                    if c:
                        dve.wait_ge(pooled, c)
                    step.add(nc.vector.tensor_copy(tail(e)[:, :, 1:16], hist[:, c, :].rearrange("p (b t) -> p b t", t=PAD)))
                    dve.wait_ge(dve_step, step.value())
                    dve.wait_ge(u_evac, c + 1)
                    src, w = e, 1
                    for level in range(g + 1):
                        dst = us[level % 2]
                        nc.vector.tensor_tensor(dst[:, 2 * w - 1:16 + SEQ], src[:, 2 * w - 1:16 + SEQ],
                                                src[:, w - 1:16 + SEQ - w], ALU.add)
                        step.add(nc.vector.tensor_tensor(tail(dst)[:, :, 2 * w:20], tail(src)[:, :, 2 * w:20],
                                                         tail(src)[:, :, w:20 - w], ALU.add))
                        dve.wait_ge(dve_step, step.value())
                        src, w = dst, 2 * w
                    mean_, diff = us[(g + 1) % 2], us[g % 2]
                    nc.vector.tensor_tensor(mean_[:, 16:32], src[:, 16:32], inv[:, g, :], ALU.mult)
                    nc.vector.tensor_scalar(mean_[:, 32:16 + SEQ], src[:, 32:16 + SEQ], 1.0 / w, None, ALU.mult)
                    step.add(nc.vector.tensor_scalar(tail(mean_)[:, :, 16:20], tail(src)[:, :, 16:20], 1.0 / w, None,
                                                     ALU.mult))
                    dve.wait_ge(dve_step, step.value())
                    nc.vector.tensor_tensor(diff[:, 0:SEQ], mean_[:, 16:16 + SEQ], e[:, 16:16 + SEQ], ALU.subtract)
                    step.add(nc.vector.tensor_tensor(diff[:, SEQ:T].rearrange("p (b t) -> p b t", t=4),
                                                     tail(mean_)[:, :, 16:20], tail(e)[:, :, 16:20], ALU.subtract))
                    dve.wait_ge(dve_step, step.value())
                    step.add(nc.vector.tensor_copy(phi[:, c, :], diff[:, 0:T]))
                    dve.wait_ge(dve_step, step.value())
                    nc.vector.tensor_tensor(plo[:, c, :], diff[:, 0:T], phi[:, c, :].bitcast(F32), ALU.subtract) \
                        .then_inc(pooled, 1)
                    round_lo(nxt, s, j)

            dve.wait_ge(consts_in, 32)
            for i in range(UNITS["pin"]):
                if i + 1 < UNITS["pin"]:
                    pin(i, "pin", i + 1)
                else:
                    pin(i, "pgrp", 0)

            def pgrp(i, nxt, j):
                for s in range(2):
                    c = 2 * i + s
                    dve.wait_ge(z_scaled, c + 1)
                    nc.vector.tensor_tensor(zlo[:, c, :], (sg, hf)[s][:], zhi[:, c, :].bitcast(F32), ALU.subtract) \
                        .then_inc(z_ready, 1)
                    round_lo(nxt, s, j)

            for i in range(4):
                if i < 3:
                    pgrp(i, "pgrp", i + 1)
                else:
                    pgrp(i, "pout", 0)

            def residual_pair(stage):
                def turn(i, nxt, j):
                    for s in range(2):
                        residual(stage, ps[s], 2 * i + s, 1.0 / ALPHA, s, FIRST[stage] + i + 1)
                        round_lo(nxt, s, j)

                turns(UNITS[stage], stage, turn)

            residual_pair("pout")
            norm("pout")
            dve.wait_ge(utok_out, 32)
            up("up1")
            down("down1")
            norm("down1")

            up("up2")
            down("down2")
            norm("down2")

            def q_turn(i, nxt, j):
                round_lo(nxt, 0, j)
                round_lo(nxt, 1, j)

            turns(UNITS["q"], "q", q_turn)

            def key_products(b):
                dve.wait_ge(c0_in, 32 * b + 32)
                nc.vector.tensor_tensor(q_b0[:], q_b0[:], kc0[:].unsqueeze(1).to_broadcast([P, DEC_S, GW]), ALU.mult) \
                    .then_inc(mul0, 1)

            def key_sums(b, g, q, made, summed):
                dve.wait_ge(made, b + 1)
                nc.vector.reduce_sum(s_sc[:, g, bass.ds(32 * b, 32)],
                                     q[:].rearrange("p i (h d) -> p (i h) d", d=DH), axis=AX_X).then_inc(summed, 1)

            def kv_turn(i, nxt, j, b0_=None, b1_=None, odd=0):
                round_lo(nxt, 0, j)
                if b1_ is not None:
                    key_sums(b1_, 1, q_b1[odd], mul1, red1)
                if b0_ is not None:
                    key_products(b0_)
                round_lo(nxt, 1, j)
                if b1_ is not None:
                    key_sums(b1_, 2, q_b2[odd], mul2, red2)
                if b0_ is not None:
                    key_sums(b0_, 0, q_b0, mul0, red0)

            kv_turn(0, "kv", 1)
            kv_turn(1, "kv", 2)
            kv_turn(2, "kv", 3, b0_=0)
            kv_turn(3, "kv", 4, b0_=1, b1_=0, odd=0)
            with dve.Fori(0, 3) as n:
                kv_turn(2 * n + 4, "kv", 2 * n + 5, b0_=2 * n + 2, b1_=2 * n + 1, odd=1)
                kv_turn(2 * n + 5, "kv", 2 * n + 6, b0_=2 * n + 3, b1_=2 * n + 2, odd=0)
            kv_turn(10, "kv", 11, b1_=7, odd=1)
            kv_turn(11, "wo", 0)

            def spread(t):
                return t[:, 0:GW].unsqueeze(1).to_broadcast([SAMP, DEC_S, GW])

            dve.wait_ge(qtok_ok, NG)
            dve.wait_ge(knew_in, 16 * (DEC_S * DEC_B + 2))
            nc.vector.tensor_tensor(prod_n[:, 0:DEC_S, :], k_new[:, 0:DEC_S, :], spread(q_tok), ALU.mult)
            step.add(nc.vector.tensor_tensor(prod_n[:, DEC_S:6, :], k_new[:, DEC_S:6, :],
                                             q_tok[:, GW:NG * GW].rearrange("p (g n) -> p g n", g=2), ALU.mult))
            dve.wait_ge(dve_step, step.value())
            nc.vector.reduce_sum(s_new[:].rearrange("p h j -> p j h"),
                                 prod_n[:].rearrange("p j (h d) -> p j h d", d=DH), axis=AX_X).then_inc(snew_ok, 1)
            dve.wait_ge(srow_t, 1)
            dve.wait_ge(sbias_in, 16)
            for k in range(2):
                nc.vector.tensor_tensor(s_row[:, k, 0:NG * P], pa[:, k, 0:NG * P], s_bias[:, 0:NG * P], ALU.add)
            dve.wait_ge(snr_in, 16)
            step.add(nc.vector.tensor_tensor(s_row[:, :, NG * P:SK], s_nr[:],
                                             s_bias[:, NG * P:SK].unsqueeze(1).to_broadcast([P, 2, 6]), ALU.add))
            dve.wait_ge(dve_step, step.value())
            step.add(nc.vector.reduce_max(s_stat[:, 0:2], s_row[:], axis=AX_X))
            dve.wait_ge(dve_step, step.value())
            nc.vector.tensor_scalar(s_stat[:, 2:4], s_stat[:, 0:2], -1.0, None, ALU.mult).then_inc(smax_ok, 1)
            dve.wait_ge(sexp_ok, 2)
            step.add(nc.vector.reciprocal(s_stat[:, 6:8], s_stat[:, 4:6]))
            dve.wait_ge(dve_step, step.value())
            for k in range(2):
                m = nc.vector.tensor_scalar(p_row[:, k, :], p_row[:, k, :], s_stat[:, 6 + k:7 + k], None, ALU.mult)
            m.then_inc(snorm_ok, 1)
            dve.wait_ge(pnew_in, 16)
            dve.wait_ge(vnew_in, 16 * (DEC_S * DEC_B + 2))
            for j in range(6):
                m = nc.vector.tensor_tensor(prod_n[:, j, :].rearrange("p (h d) -> p h d", d=DH),
                                            v_new[:, j, :].rearrange("p (h d) -> p h d", d=DH),
                                            p_new[:, :, j:j + 1].to_broadcast([SAMP, HEADS, DH]), ALU.mult)
            step.add(m)
            dve.wait_ge(dve_step, step.value())
            nc.vector.reduce_sum(o_new[:], prod_n[:].rearrange("p j n -> p n j"), axis=AX_X).then_inc(onew_ok, 1)
            dve.wait_ge(sv_done, DEC_B)
            dve.wait_ge(onew_t, 1)
            for n, src in enumerate((pc[:, 0, :], pd[:, 0, :], pd[:, 1, :], pc[:, 1, :])):
                for hh in range(2):
                    part = slice(DH * hh, DH * hh + DH)
                    dst = ot[part, :, SEQ:T]
                    if n < 3:
                        v = src[part, 0:256].rearrange("p (c t h) -> p c t h", c=GC, h=2)[:, :, :, hh]
                    else:
                        v = src[part, 0:GC * SAMP].rearrange("p (c t) -> p c t", c=GC)
                    if n == 0:
                        m = nc.vector.tensor_copy(dst, v)
                    else:
                        m = nc.vector.tensor_tensor(dst, v, dst, ALU.add)
                if n < 3:
                    step.add(m)
                    dve.wait_ge(dve_step, step.value())
            m.then_inc(ots_ok, 1)

            dve.wait_ge(ots_ok, 1)
            for h in range(HEADS):
                m = nc.vector.memset(b0[0:32, h, 0:P], NEG)
            m.then_inc(b0_pad, 1)

            def qk_tile(r, c):
                q = qt[:, :, 0:SEQ].rearrange("p (g c) (q r) -> p g c q r", g=NG, r=QB)
                k = kt12[:].rearrange("p (g c) (q r) -> p g c q r", g=2, r=QB)
                for g in range(NG):
                    nc.vector.tensor_copy(q_r[:, g * GC + c, :], q[:, g, c, :, r])
                for g in range(2):
                    m = nc.vector.tensor_copy(k_r[:, g * GC + c, :], k[:, g, c, :, r])
                m.then_inc(qk_ok, 1)

            def head(r, h):
                dve.wait_ge(s_done, HEADS * r + h + 1)
                dve.wait_ge(b0_in[h // 4], 64 * (r + 1))
                b = h % 2
                if not (first_turn(r) and h < 2):
                    dve.wait_ge(p_ok, HEADS * r + h - 1)
                nc.vector.tensor_tensor(s_p[b][:, 0:256], pa[:, b, 0:256], b0[:, h, :], ALU.add)
                step.add(nc.vector.tensor_tensor(s_p[b][:, 256:512], pa[:, b, 256:512], b12[:, h, :], ALU.add))
                dve.wait_ge(dve_step, step.value())
                step.add(nc.vector.reduce_max(a_stat[:, 0, r, h:h + 1], s_p[b][:], axis=AX_X))
                dve.wait_ge(dve_step, step.value())
                nc.vector.tensor_scalar(a_stat[:, 1, r, h:h + 1], a_stat[:, 0, r, h:h + 1], -1.0, None, ALU.mult) \
                    .then_inc(s_ok, 1)

            def tile(r, last):
                for h in range(HEADS):
                    head(r, h)
                    if h % 2 and not last:
                        qk_tile(r + 1, h // 2)
                dve.wait_ge(p_ok, HEADS * (r + 1))
                step.add(nc.vector.reciprocal(a_stat[:, 3, r, :], a_stat[:, 2, r, :]))
                dve.wait_ge(dve_step, step.value())
                dve.wait_ge(pv_done, HEADS * (r + 1))
                if not first_turn(r):
                    dve.wait_ge(on_t, r)
                nc.vector.tensor_tensor(o_n[:].rearrange("p (h d) -> p h d", d=DH),
                                        pc[:, 0, :].rearrange("p (h d) -> p h d", d=DH),
                                        a_stat[:, 3, r, :].unsqueeze(2).to_broadcast([P, HEADS, DH]), ALU.mult) \
                    .then_inc(on_ok, 1)

            dve.wait_ge(kt_in, 32)
            for c in range(GC):
                qk_tile(0, c)
            dve.wait_ge(b12_in, 32)
            tile(0, False)
            with dve.Fori(1, QB - 1) as r:
                step.turn(r - 1, 2 * HEADS + 1)
                tile(r, False)
                step.turns(QB - 2)
            tile(QB - 1, True)
            dve.wait_ge(ohi_ok, 1)
            nc.vector.tensor_tensor(olo[:], ot[:], ohi[:].bitcast(F32), ALU.subtract).then_inc(o_ready, 1)
            residual_pair("wo")
            norm("wo")
            up("up3")
            down("down3")
            norm("down3", last=True)
            for j in range(QB + 1):
                n = P if j < QB else SAMP
                dve.wait_ge(y_t, j + 1)
                nc.vector.tensor_copy(ytok[0:n, j, 512:D], ps[j % 2][0:n, 1, :]).then_inc(y_ok[1], 1)

        @block.gpsimd
        def _(pool):
            def sums(stage):
                nc.gpsimd.memset(accs[:], 0.0).then_inc(acc_zero, 1)
                nc.gpsimd.memset(accq[:], 0.0).then_inc(acc_zero, 1)
                pool.wait_ge(acc_zero, 2 * RES.index(stage) + 2)
                base = RES.index(stage)

                def add(c):
                    if not first_turn(c):
                        pool.wait_ge(acc_made, 2 * DC * base + 2 * c)
                    pool.wait_ge(res_made, DC * base + c + 1)
                    nc.gpsimd.tensor_tensor(accs[:], accs[:], x[:, c, :], ALU.add).then_inc(acc_made, 1)
                    pool.wait_ge(sq_made, DC * base + c + 1)
                    nc.gpsimd.tensor_tensor(accq[:], accq[:], sq[:], ALU.add).then_inc(acc_made, 1)

                add(0)
                with pool.Fori(1, DC) as c:
                    add(c)

            sums("down0")
            pool.wait_ge(stats, 2 * RES.index("down0") + 2)
            pool.wait_ge(utok_ok, 1)
            pool.dma_start(O["pool_p"][0, 0, :, :], utok[0:PAD, :]).then_inc(utok_out, 16)
            pool.dma_start(O["pool_s"][0, :, PAD - DEC_S:PAD, :], utok[PAD:PAD + SAMP, :]).then_inc(utok_out, 16)
            sums("pout")
            pool.wait_ge(stats, 2 * RES.index("pout") + 2)
            sums("down1")

            pool.wait_ge(stats, 2 * RES.index("down1") + 2)
            sums("down2")

            def key_products(b, s):
                for kc, q, into, made in ((kc1, q_b1[s], c1_in, mul1), (kc2, q_b2[s], c2_in, mul2)):
                    pool.wait_ge(into, 32 * b + 32)
                    nc.gpsimd.tensor_tensor(q[:], q[:], kc[:], ALU.mult).then_inc(made, 1)

            with pool.Fori(0, DEC_B // 2) as n:
                key_products(2 * n, 0)
                key_products(2 * n + 1, 1)
            pool.wait_ge(o_ready, 1)
            sums("wo")
            pool.wait_ge(stats, 2 * RES.index("wo") + 2)
            sums("down3")


OUTPUTS = [("y_p", (1, SEQ, D)), ("y_s", (DEC_B, DEC_S, D)), ("pool_p", (1, 1, PAD, D)), ("pool_s", (1, DEC_B, PAD, D)),
           ("kv_p0", (1, 128, 2, HEADS, DH)), ("kv_p1", (1, SEQ, 2, HEADS, DH)), ("kv_p2", (1, SEQ, 2, HEADS, DH)),
           ("kv_s0", (DEC_B, DEC_S, 2, HEADS, DH)), ("kv_s1", (DEC_B, DEC_S, 2, HEADS, DH)),
           ("kv_s2", (DEC_B, DEC_S, 2, HEADS, DH))]


def kernel(**inputs):
    import concourse.bacc as bacc
    from concourse.bass_utils import run_bass_kernel_spmd

    nc = bacc.Bacc("TRN2", target_bir_lowering=False, num_devices=1)
    arrays, A, O = {}, {}, {}
    for name, a in {**inputs, **shape_constants()}.items():
        a = np.ascontiguousarray(a)
        arrays["in_" + name] = a
        A[name] = nc.dram_tensor("in_" + name, a.shape, mybir.dt.from_np(a.dtype), kind="ExternalInput").ap()
    for name, shape in OUTPUTS:
        O[name] = nc.dram_tensor("out_" + name, shape, F32, kind="ExternalOutput").ap()
    build(nc, A, O)
    r = run_bass_kernel_spmd(nc, [arrays], core_ids=[0])
    return tuple(r.results[0]["out_" + name] for name, _ in OUTPUTS)
```

```python
import math
from contextlib import ExitStack

import concourse.bass as bass
import numpy as np
from concourse import mybir

F32 = mybir.dt.float32
F32R = mybir.dt.float32r
ACT = mybir.ActivationFunctionType
ALU = mybir.AluOpType
AX_X = mybir.AxisListType.X

P = 128
D, SEQ, DEC_B, DEC_S = 1024, 512, 8, 4
SAMP = DEC_B * DEC_S
T = SEQ + SAMP
HALF = T // 2
DC = D // P
FF = 2816
FC = FF // P
KH = FC // 2
PAD = 15
DH = 64
HEADS = 8
GW = HEADS * DH
GC = GW // P
NG = 3
DIL = (1, 4, 16)
WIN = (128, 512, 2048)
NKEY = 129
NBUCKET, MAXDIST = 32, 2048
QB = SEQ // P
ALPHA = (2.0 * 2) ** 0.25
LN_EPS = 1e-5 / ALPHA ** 2
NEG = -1e30
RP = 384
SK = NG * (P + SAMP)
NCK = 9
BW = 16 + SAMP

PG, PB, PS = 0, 48, 96
NPAR = 104

STAGES = [("up0", 22, 8), ("down0", 8, 11), ("pin", 4, 8), ("pgrp", 4, 2), ("pout", 4, 8),
          ("up1", 22, 8), ("down1", 8, 11), ("up2", 22, 8), ("down2", 8, 11),
          ("q", 6, 8), ("kv", 12, 8), ("wo", 4, 4), ("up3", 22, 8), ("down3", 8, 11)]
EARLY = 3
ACCS = 2 * (DC - 1)
RES = ("down0", "pout", "down1", "down2", "wo", "down3")
UNITS = {n: u for n, u, _ in STAGES}
KT = {n: k for n, _, k in STAGES}
FIRST, AFTER = {}, {}
_at = 0
for _j, (_n, _u, _k) in enumerate(STAGES):
    FIRST[_n] = _at
    _at += _u
    AFTER[_n] = STAGES[_j + 1][0] if _j + 1 < len(STAGES) else None


def t5_bucket(dist):
    exact = NBUCKET // 2
    if dist < exact:
        return dist
    return min(exact + int(math.log(dist / exact) / math.log(MAXDIST / exact) * (NBUCKET - exact)), NBUCKET - 1)


def shape_constants():
    table = np.zeros((NBUCKET + 1, NG, RP), np.float32)
    for x in range(RP):
        for g in range(NG):
            if g == 0:
                d = 255 - x
                ok, j = 0 <= d < NKEY, d
            else:
                d = 127 - x
                step = DIL[g] // DIL[1]
                ok, j = d >= 0 and d % step == 0 and d // step < NKEY, d // step
            table[t5_bucket(j * DIL[g]) if ok else NBUCKET, g, x] = 1.0
    samp = np.zeros((NBUCKET + 1, 6, NG * (P + BW)), np.float32)
    for i in range(DEC_S):
        for r in range(P):
            samp[t5_bucket(P + i - r) if P + i - r < NKEY else NBUCKET, i, r] = 1.0
        for k in range(BW):
            samp[t5_bucket(i - k % DEC_S) if k % DEC_S <= i else NBUCKET, i, NG * P + k] = 1.0
    for g in (1, 2):
        for r in range(P):
            samp[t5_bucket((P - r) * DIL[g]), 3 + g, g * P + r] = 1.0
        samp[t5_bucket(0), 3 + g, NG * P + g * BW:NG * P + (g + 1) * BW] = 1.0
    mask = np.full((4, GC, DEC_S, 2, NG, BW), NEG, np.float32)
    for b in range(4):
        for i in range(DEC_S):
            mask[b, :, i, :, 0, 16 + DEC_S * b:16 + DEC_S * (b + 1)] = 0.0
            mask[b, :, i, :, 1:, 16 + DEC_S * b + i] = 0.0
    inv = np.zeros((4, 16), np.float32)
    for g in range(4):
        for t in range(16):
            inv[g, t] = 1.0 / min(t + 1, 2 ** (g + 1))
    return {"c_table": table, "c_samp": samp, "c_mask": mask.reshape(P, NG * BW), "c_inv": inv.reshape(1, 64),
            "c_ident": np.eye(P, dtype=np.float32)}


def first_turn(i):
    return isinstance(i, int) and i == 0


class Steps:

    def __init__(self, sem):
        self.sem, self.n, self.i, self.start = sem, 0, None, 0

    def add(self, instruction, k=1):
        instruction.then_inc(self.sem, k)
        self.n += k

    def value(self):
        if self.i is None:
            return self.n
        return self.start + self.per * self.i + (self.n - self.start)

    def turn(self, i, per):
        self.i, self.per, self.start = i, per, self.n

    def turns(self, count):
        assert self.n - self.start == self.per, (self.n - self.start, self.per)
        self.n, self.i = self.start + count * self.per, None


def build(nc, A, O):
    ctx = ExitStack()
    names = [0]

    def sb(where, name, shape, dt=F32):
        return where.enter_context(nc.sbuf_tensor("t_" + name, shape, dt))

    def sem(name):
        return ctx.enter_context(nc.semaphore(name))

    with ctx:
        x = sb(ctx, "stream", [P, DC, T])
        rw = ExitStack()
        v_c = [sb(rw, f"cached_v{s}", [P, NCK - 1, GW]) for s in range(2)]
        rw.close()
        raw = [sb(ctx, f"w_raw{s}", [P, KH, P]) for s in range(2)]
        whi = [sb(ctx, f"w_hi{s}", [P, KH, P], F32R) for s in range(2)]
        wlo = [sb(ctx, f"w_lo{s}", [P, KH, P], F32R) for s in range(2)]
        ident = sb(ctx, "ident", [P, P])
        invd = sb(ctx, "inv_d", [P, P])
        par = sb(ctx, "params", [P, NPAR])
        eps = sb(ctx, "eps", [P, 1])
        root = sb(ctx, "root", [P, 1])
        elem = sb(ctx, "elementwise", [P, 3 * T])
        sg, hf, sq = (elem[:, j * T:(j + 1) * T] for j in range(3))
        tab = sb(ctx, "bias_rows", [HEADS, NG, RP])
        s_bias = sb(ctx, "samp_bias", [P, NG * (P + BW)])
        work = sb(ctx, "work", [P, 5 * T])
        accs, accq, mean, var, rstd = (work[:, j * T:(j + 1) * T] for j in range(5))
        s_sc = work[:, 0:NG * 256].rearrange("p (g n) -> p g n", g=NG)
        s_row = work[:, 768:768 + 2 * SK].rearrange("p (k n) -> p k n", k=2)
        p_b = [work[:, n * NCK * 32:(n + 1) * NCK * 32].rearrange("p (t n) -> p t n", t=NCK) for n in range(2)]
        o_s = work[0:2 * 32, 768:768 + GW]
        s_stat = work[:, 1920:1928]
        s_nk = work[0:SAMP, 1928:1928 + NG * 256]
        p_key = elem[:, 0:NG * 256]
        p_nk = elem[0:SAMP, NG * 256:2 * NG * 256]
        hist = sb(ctx, "history", [P, DC, DEC_B * PAD])
        inv = sb(ctx, "inv_count", [P, 4, 16])

        rx = ExitStack()
        xhi = sb(rx, "x_hi", [P, DC, T], F32R)
        xlo = sb(rx, "x_lo", [P, DC, T], F32R)
        rh = ExitStack()
        hhi = sb(rh, "h_hi", [P, FC, T], F32R)
        hlo = sb(rh, "h_lo", [P, FC, T], F32R)
        rh.close()
        xtok = sb(rh, "x_tok", [P, 5, D])
        ptok = sb(rh, "par_tok", [NPAR, P])
        sttok = sb(rh, "state_tok", [DEC_B * PAD, D])
        oh_t = sb(rh, "onehot_table", [NBUCKET + 1, NG, RP])
        oh_s = sb(rh, "onehot_samp", [NBUCKET + 1, 6, NG * (P + BW)])
        rbx = sb(rh, "bucket_bias", [NBUCKET + 1, NG * HEADS])
        rb_s = sb(rh, "bucket_bias_samp", [NBUCKET + 1, 6, P])
        smask = sb(rh, "samp_mask", [P, NG * BW])
        rh.close()
        phi = sb(rh, "pool_hi", [P, DC, T], F32R)
        plo = sb(rh, "pool_lo", [P, DC, T], F32R)
        ue = [sb(rh, f"u_ext{s}", [P, 16 + SEQ + DEC_B * 20]) for s in range(2)]
        us = [sb(rh, f"u_sum{s}", [P, 16 + SEQ + DEC_B * 20]) for s in range(2)]
        utail = sb(rh, "u_tail", [P, DC, PAD + SAMP])
        utok = sb(rh, "u_tok", [PAD + SAMP, D])
        zhi = sb(rh, "z_hi", [P, DC, T], F32R)
        zlo = sb(rh, "z_lo", [P, DC, T], F32R)
        rh.close()
        qt = sb(rh, "q_feat", [P, NG * GC, T])
        hq = ExitStack()
        yhi = sb(hq, "kv_in_hi", [P, DC, T], F32R)
        ylo = sb(hq, "kv_in_lo", [P, DC, T], F32R)
        cached_odd = sb(hq, "cached1", [P, NCK, GW])
        kvt = [sb(hq, f"kv_feat{s}", [P, T]) for s in range(2)]
        kvp = [sb(hq, f"kv_tok{s}", [P, QB, P]) for s in range(2)]
        q_bd = sb(hq, "q_blocks", [P, NG * GC, 2 * SAMP])
        q_b = sb(hq, "q_blocks_b", [P, NG * GC, 2 * DEC_S])
        kn_t = sb(hq, "k_new_feat", [P, NG * GC, SAMP])
        k_t2 = sb(hq, "k_turned2", [P, GW])
        hq.close()
        ot = sb(hq, "o_feat", [P, GC, T])
        kt0 = sb(hq, "k_feat0", [P, GC, SEQ])
        kt12 = sb(hq, "k_feat12", [P, 2 * GC, SEQ])
        v_p = [sb(hq, f"v_prompt{g}", [P, QB, GW]) for g in range(NG)]
        b12 = sb(hq, "bias12", [P, HEADS, 256])
        v_c0 = [hist[:].rearrange("p c n -> p (c n)")[:, 0:GW], sb(hq, "cached_v_g0", [P, GW])]
        hq.close()
        rh.close()
        ohi = sb(rh, "o_hi", [P, GC, T], F32R)
        olo = sb(rh, "o_lo", [P, GC, T], F32R)
        rh.close()
        ytok = sb(rh, "y_tok", [P, QB + 1, D])
        rh.close()
        rx.close()
        cached = [sb(rx, "cached0", [P, NCK, GW]), cached_odd]
        kv_n = sb(rx, "kv_new", [SAMP, NG * 2 * GW])
        k_t = [sb(rx, f"k_turned{s}", [P, GW]) for s in range(2)] + [k_t2]
        rx.close()
        b0 = sb(rx, "bias0", [P, HEADS, 256])
        s_p = [sb(rx, f"s_prompt{s}", [P, 512]) for s in range(2)]
        p_p = [sb(rx, f"p_prompt{s}", [P, 512]) for s in range(2)]
        pt_p = [sb(rx, f"pt_prompt{s}", [P, 512]) for s in range(2)]
        o_n = sb(rx, "o_tok", [P, GW])
        a_stat = sb(rx, "a_stats", [P, 4, QB, HEADS])
        q_r = sb(rx, "q_tile", [P, NG * GC, P])
        k_r = sb(rx, "k_tile", [P, 2 * GC, P])
        rx.close()

        ps = [ctx.enter_context(nc.psum_tensor(f"pair{j}", [P, 2, 512], F32)) for j in range(4)]
        pa, pb, pc, pd = ps

        def halves(t):
            return t[:, :, 0:HALF]

        def split(t):
            return t.rearrange("p (a n) -> p a n", a=2)

        kt_d = nc.dram_tensor("scratch_kt", [NG * GC, P, SEQ], F32)
        kv0_d = nc.dram_tensor("scratch_kv0", [SEQ, 2 * GW], F32)
        xs_d = nc.dram_tensor("scratch_x_parts", [2, P, DC * T], F32)
        tab_d = nc.dram_tensor("scratch_bias_rows", [NG, HEADS, P, RP], F32)

        raw_in = [sem(f"raw_in{s}") for s in range(2)]
        hi_made = [sem(f"hi_made{s}") for s in range(2)]
        lo_made = [sem(f"lo_made{s}") for s in range(2)]
        w_used = [sem(f"w_used{s}") for s in range(2)]
        consts_in = sem("consts_in")
        xtok_in = sem("xtok_in")
        ptok_in = sem("ptok_in")
        consts_made = sem("consts_made")
        par_t = sem("par_transposed")
        par_ok = sem("par_ready")
        in_t = sem("in_transposed")
        in_evac = sem("in_evacuated")
        x_ready = sem("x_parts_ready")
        act_step = sem("act_step")
        dve_step = sem("dve_step")
        pool_step = sem("pool_step")
        res_made = sem("residual_made")
        sq_made = sem("squares_made")
        acc_made = sem("sums_made")
        acc_zero = sem("sums_zero")
        stats = sem("norm_sums")
        ln_mean = sem("norm_mean")
        ln_sq = sem("norm_mean_squared")
        ln_var = sem("norm_var")
        ln_std = sem("norm_std")
        ln_sub = sem("norm_centred")
        ln_t = sem("norm_scaled")
        ln_x = sem("norm_out")
        gate_silu = sem("gate_silu")
        h_made = sem("hidden_made")
        h_hi_made = sem("hidden_hi_made")
        h_lo_made = sem("hidden_lo_made")
        u_evac = sem("u_evacuated")
        st_in = sem("state_in")
        st_t = sem("state_transposed")
        st_evac = sem("state_evacuated")
        pooled = sem("pooled")
        utail_t = sem("u_tail_transposed")
        utok_ok = sem("u_tok_ready")
        z_scaled = sem("z_scaled")
        z_hi_made = sem("z_hi_made")
        z_ready = sem("z_parts_ready")
        kv_evac = [sem(f"kv_evacuated{s}") for s in range(2)]
        kv_t = [sem(f"kv_transposed{s}") for s in range(2)]
        kv_tok = [sem(f"kv_tok_ready{s}") for s in range(2)]
        kt_out = [sem(f"kt_stored{s}") for s in range(2)]
        kv_out = [sem(f"kv_stored{s}") for s in range(2)]
        utok_out = sem("u_tok_stored")
        tab_in = sem("tab_in")
        rb_copied = sem("rb_copied")
        tab_mm = sem("tab_mm")
        tab_evac = sem("tab_evac")
        sb_mm = sem("sb_mm")
        sb_evac = sem("sb_evac")
        sbn_ok = sem("samp_bias_new")
        tab_out = sem("tab_out")
        xs_out = sem("xs_out")
        xs_in = sem("xs_in")
        q_evac = sem("q_evac")
        kvn_out = sem("kv_new_stored")
        cached_in = [sem(f"cached_in{s}") for s in range(2)]
        value_in = [sem(f"value_in{s}") for s in range(2)]
        pb_zero = sem("samp_probs_zero")
        os_t = sem("samp_outputs_turned")
        qbd_ok = sem("q_blocks_ready")
        qb_ok = sem("q_blocks_b_ready")
        kc_t = sem("cached_keys_turned")
        kc_ok = sem("cached_keys_evacuated")
        kc_used = sem("cached_keys_used")
        snk_mm = sem("samp_new_scores")
        snk_ok = sem("samp_new_scores_evacuated")
        srow_t = sem("samp_rows_turned")
        smax_ok = sem("samp_max")
        sexp_ok = sem("samp_exp")
        snorm_ok = sem("samp_probs")
        pkey_t = sem("samp_probs_turned")
        pkey_ok = sem("samp_probs_evacuated")
        pb_ok = sem("samp_probs_b")
        snv_done = sem("samp_new_values")
        snv_ok = sem("samp_new_values_evacuated")
        sv_done = sem("samp_values")
        sv_evac = sem("samp_values_evacuated")
        ots_ok = sem("samp_outputs_added")
        kt_in = sem("kt_in")
        v_in = sem("v_in")
        b12_in = sem("b12_in")
        b0_pad = sem("b0_pad")
        qk_ok = sem("qk_ok")
        s_done = sem("s_done")
        s_ok = sem("s_ok")
        p_ok = sem("p_ok")
        pt_done = sem("pt_done")
        pt_ok = sem("pt_ok")
        pv_done = sem("pv_done")
        on_ok = sem("on_ok")
        on_t = sem("on_t")
        ot_ok = sem("ot_ok")
        o_ready = sem("o_ready")
        ohi_ok = sem("ohi_ok")
        y_t = sem("y_t")
        y_ok = [sem(f"y_ok{s}") for s in range(2)]
        y_out = sem("y_out")
        b0_in = [sem(f"b0_in{h}") for h in range(2)]
        done = sem("outputs_done")
        DONE = [0]

        def rows(w):
            return w.rearrange("(k p) n -> p k n", p=P)

        w13 = [rows(A["ffn_w13"][f // 2, f % 2]) for f in range(4)]
        w2 = [rows(A["ffn_w2"][f // 2, f % 2]) for f in range(4)]
        w_pin, w_pout = rows(A["pool_w_in"][0]), rows(A["pool_w_out"][0])
        w_grp = A["pool_w_grp"][0].rearrange("g (k p) n -> p g k n", p=P)
        w_kv, w_q, w_o = rows(A["attn_w_kv"]), rows(A["attn_w_q"][0]), rows(A["attn_w_o"][0])

        def unit_source(stage, s, i):
            if stage[:2] == "up":
                return w13[int(stage[2])][:, :, bass.ds(FF * s + i * P, P)]
            if stage[:4] == "down":
                return w2[int(stage[4])][:, KH * s:KH * (s + 1), bass.ds(i * P, P)]
            if stage == "pgrp":
                return w_grp[:, i, :, s * P:(s + 1) * P]
            w = {"pin": w_pin, "pout": w_pout, "kv": w_kv, "q": w_q, "wo": w_o}[stage]
            return w[:, :, bass.ds(2 * i * P + s * P, P)]

        block = ctx.enter_context(nc.Block())

        @block.sync
        def _(sp):
            def load(dst, src, s, k=16):
                sp.dma_start(dst, src).then_inc(s, k)

            load(ident[:], A["c_ident"], consts_in)
            load(inv[:].rearrange("p g t -> p (g t)"), A["c_inv"].partition_broadcast(P).rearrange("q a n -> q (a n)"),
                 consts_in)
            load(sttok[:], A["state_pool"][0].rearrange("b t d -> (b t) d"), st_in)
            load(xtok[:, 0:4, :], A["x_prompt"][0].rearrange("(j p) d -> p j d", p=P), xtok_in)
            load(xtok[0:SAMP, 4, :], A["x_sample"].rearrange("b s d -> (b s) d"), xtok_in)
            load(ptok[PG:PB, :], A["ln_g"].rearrange("l s (c p) -> (l s c) p", p=P), ptok_in)
            load(ptok[PB:PS, :], A["ln_b"].rearrange("l s (c p) -> (l s c) p", p=P), ptok_in)
            load(ptok[PS:NPAR, :], A["pool_scale"][0].rearrange("(c p) -> c p", p=P), ptok_in)

            load(oh_t[:], A["c_table"], tab_in)
            load(oh_s[:], A["c_samp"], tab_in)
            load(smask[:], A["c_mask"], tab_in)
            sp.wait_ge(rb_copied, 1)
            load(rbx[0:NBUCKET, :], A["rel_bias"], tab_in)

            def stream(stage, i):
                for s in range(2):
                    if not (stage == "up0" and first_turn(i)):
                        sp.wait_ge(lo_made[s], FIRST[stage] + i)
                    sp.dma_start(raw[s][:, 0:KT[stage], :], unit_source(stage, s, i)).then_inc(raw_in[s], 16)

            def stream_all(stage, start=0):
                with sp.Fori(start, UNITS[stage]) as i:
                    stream(stage, i)

            stream("up0", 0)
            stream_all("up0", 1)
            sp.wait_ge(tab_evac, NG)
            for g in range(NG):
                sp.dma_start(tab_d.ap()[g], tab[:, g, :].unsqueeze(1).to_broadcast([HEADS, P, RP])).then_inc(tab_out, 16)
            for stage in ("down0", "pin", "pgrp", "pout", "up1", "down1"):
                stream_all(stage)
            stream("up2", 0)
            stream("up2", 1)
            sp.wait_ge(x_ready, 4 * DC)
            for n, part in enumerate((xhi, xlo)):
                sp.dma_start(xs_d.ap()[n], part[:].rearrange("p c t -> p (c t)").bitcast(F32)).then_inc(xs_out, 16)
            stream_all("up2", 2)
            stream_all("down2")
            stream("q", 0)
            sp.wait_ge(res_made, DC * RES.index("down2") + DC)
            sp.wait_ge(xs_out, 32)
            for n, part in enumerate((yhi, ylo)):
                sp.dma_start(part[:].rearrange("p c t -> p (c t)").bitcast(F32), xs_d.ap()[n]).then_inc(xs_in, 16)
            stream_all("q", 1)

            def kt_store(i, s):
                g, j = i // 4, i % 4
                if j < 2:
                    sp.wait_ge(kv_evac[s], i + 1)
                    sp.dma_start(kt_d.ap()[g * GC + 2 * j + s], kvt[s][:, 0:SEQ]).then_inc(kt_out[s], 16)

            def kv_store(i, s):
                g, col = i // 4, ((i % 4) * 2 + s) * P
                sp.wait_ge(kv_tok[s], 2 * i + 2)
                if g == 0:
                    sp.dma_start(kv0_d.ap().rearrange("(j p) n -> p j n", p=P)[:, :, col:col + P],
                                 kvp[s][:]).then_inc(kv_out[s], 16)
                    sp.dma_start(O["kv_p0"].rearrange("b w k h d -> (b w) (k h d)")[:, col:col + P],
                                 kvp[s][:, QB - 1, :]).then_inc(kv_out[s], 16)
                else:
                    view = O[f"kv_p{g}"].rearrange("b (j p) k h d -> p (b j) (k h d)", p=P)
                    for h in range(2):
                        sp.dma_start(view[:, 2 * h:2 * h + 2, col:col + P],
                                     kvp[s][:, 2 * h:2 * h + 2, :]).then_inc(kv_out[s], 16)

            for i in range(UNITS["kv"]):
                stream("kv", i)
                if i >= 1:
                    kt_store(i - 1, 0)
                    if i >= 2:
                        kv_store(i - 2, 1)
                    kt_store(i - 1, 1)
                    kv_store(i - 1, 0)
            kv_store(UNITS["kv"] - 2, 1)
            kv_store(UNITS["kv"] - 1, 0)
            kv_store(UNITS["kv"] - 1, 1)
            for g in range(NG):
                sp.dma_start(O[f"kv_s{g}"].rearrange("b t k h d -> (b t) (k h d)"),
                             kv_n[:, g * 2 * GW:(g + 1) * 2 * GW]).then_inc(kvn_out, 16)

            for s in range(2):
                sp.wait_ge(w_used[s], FIRST["wo"])
                sp.wait_ge(kt_out[s], 16 * UNITS["kv"] // 2)
            load(kt0[:], kt_d.ap()[0:GC].rearrange("c p t -> p c t"), kt_in)
            load(kt12[:], kt_d.ap()[GC:NG * GC].rearrange("c p t -> p c t"), kt_in)
            sp.wait_ge(tab_out, 16 * NG)
            for s in range(2):
                sp.wait_ge(kv_out[s], 32 * UNITS["kv"])
            sp.wait_ge(snk_mm, 1)
            for g in (1, 2):
                load(b12[:, :, (g - 1) * P:g * P],
                     bass.AP(tensor=tab_d, offset=g * HEADS * P * RP + P - 1, ap=[[RP - 1, P], [P * RP, HEADS], [1, P]]),
                     b12_in)

            def bias0(r, h, first=False):
                if not first:
                    sp.wait_ge(s_ok, HEADS * (r - 1) + 4 * h + 4)
                for c in range(QB):
                    k0 = P if c == 0 else 0
                    sp.dma_start(b0[32 * c:32 * c + 32, 4 * h:4 * h + 4, k0:256],
                                 bass.AP(tensor=tab_d, offset=4 * h * P * RP + P - 1 - r + k0,
                                         ap=[[RP - 4, 32], [P * RP, 4], [1, 256 - k0]])).then_inc(b0_in[h], 16)

            sp.wait_ge(b0_pad, 1)
            bias0(0, 0, True)
            bias0(0, 1, True)
            load(v_p[0][:], kv0_d.ap().rearrange("(c p) n -> p c n", p=P)[:, :, GW:2 * GW], v_in)
            for g in (1, 2):
                load(v_p[g][:], O[f"kv_p{g}"].rearrange("b (p r) k h d -> p (b r) k (h d)", r=QB)[:, :, 1, :], v_in)
            for r in range(1, QB):
                bias0(r, 0)
                bias0(r, 1)
            sp.wait_ge(sv_done, DEC_B)
            stream_all("wo")
            stream_all("up3")
            stream_all("down3")

            out_p = O["y_p"].rearrange("b (j p) d -> p (b j) d", p=P)
            for j in range(QB):
                sp.wait_ge(y_ok[0], j + 1)
                sp.wait_ge(y_ok[1], j + 1)
                sp.dma_start(out_p[:, j, :], ytok[:, j, :]).then_inc(y_out, 16)
            sp.wait_ge(y_ok[0], QB + 1)
            sp.wait_ge(y_ok[1], QB + 1)
            sp.dma_start(O["y_s"].rearrange("b t d -> (b t) d"), ytok[0:SAMP, QB, :]).then_inc(y_out, 16)
            sp.wait_ge(y_out, 16 * (QB + 1))
            sp.dma_start(O["pool_s"][0, :, 0:PAD - DEC_S, :], A["state_pool"][0, :, DEC_S:PAD, :]).then_inc(done, 16)
            sp.wait_ge(done, 16)
            sp.wait_ge(utok_out, 32)
            for s in range(2):
                sp.wait_ge(kv_out[s], 32 * UNITS["kv"])
                sp.wait_ge(kt_out[s], 16 * UNITS["kv"] // 2)
            sp.wait_ge(kvn_out, 16 * NG)

        @block.tensor
        def _(pe):
            def products(out, s, kt, hi, lo, first=True, last=True, each=None):
                for k in range(kt):
                    if each:
                        each(k)
                    for n, (w, a) in enumerate(((whi[s], hi), (whi[s], lo), (wlo[s], hi))):
                        for j in range(2):
                            m = nc.tensor.matmul(out[:, j, 0:HALF], w[:, k, :], a(k)[:, j * HALF:(j + 1) * HALF],
                                                 start=first and k == 0 and n == 0,
                                                 stop=last and k == kt - 1 and n == 2)
                return m

            def stream_x(k):
                return xhi[:, k, :]

            def stream_xl(k):
                return xlo[:, k, :]

            def first_units(stage, count):
                for s in range(2):
                    pe.wait_ge(lo_made[s], FIRST[stage] + 1)
                for k in range(DC):
                    pe.wait_ge(x_ready, count - DC + k + 1)
                    for s in range(2):
                        for n, (w, a) in enumerate(((whi[s], xhi), (whi[s], xlo), (wlo[s], xhi))):
                            for j in range(2):
                                m = nc.tensor.matmul(ps[s][:, j, 0:HALF], w[:, k, :],
                                                     a[:, k, j * HALF:(j + 1) * HALF],
                                                     start=k == 0 and n == 0, stop=k == DC - 1 and n == 2)
                        if k == DC - 1:
                            m.then_inc(w_used[s], 1)

            pe.wait_ge(consts_in, 32)
            pe.wait_ge(ptok_in, 48)
            nc.tensor.transpose(pc[:, 0, 0:NPAR], ptok[:], ident[0:NPAR, 0:NPAR]).then_inc(par_t, 1)
            pe.wait_ge(xtok_in, 32)
            for c in range(DC):
                if c >= 2:
                    pe.wait_ge(in_evac, c - 1)
                for j in range(QB):
                    nc.tensor.transpose(ps[c % 2][:, 0, j * P:(j + 1) * P], xtok[:, j, c * P:(c + 1) * P], ident[:])
                nc.tensor.transpose(ps[c % 2][:, 1, 0:SAMP], xtok[0:SAMP, 4, c * P:(c + 1) * P],
                                    ident[0:SAMP, 0:SAMP]).then_inc(in_t, 1)

            def up(stage, ready):
                f, base = int(stage[2]), FIRST[stage]

                def turn(i):
                    pe.wait_ge(lo_made[0], base + i + 1)
                    pe.wait_ge(gate_silu, FC * f + i)
                    products(pa, 0, DC, stream_x, stream_xl).then_inc(w_used[0], 1)
                    pe.wait_ge(lo_made[1], base + i + 1)
                    pe.wait_ge(h_made, FC * f + i)
                    products(pb, 1, DC, stream_x, stream_xl).then_inc(w_used[1], 1)

                first_units(stage, ready)
                with pe.Fori(1, FC) as i:
                    turn(i)

            def down(stage):
                f, base = int(stage[4]), FIRST[stage]

                def chunk(i, out, first=False):
                    for s in range(2):
                        pe.wait_ge(lo_made[s], base + i + 1)
                        if first:
                            pe.wait_ge(h_lo_made, FC * f + (KH if s == 0 else FC))
                        elif s == 0:
                            pe.wait_ge(res_made, DC * RES.index(stage) + i - 1)
                        products(out, s, KH, lambda k: hhi[:, KH * s + k, :], lambda k: hlo[:, KH * s + k, :],
                                 first=s == 0, last=s == 1).then_inc(w_used[s], 1)

                chunk(0, pa, True)
                chunk(1, pb, True)
                with pe.Fori(2, DC, 2) as i:
                    chunk(i, pa)
                    chunk(i + 1, pb)

            def linear(stage, hi, lo, evac, ready=None):
                base = FIRST[stage]

                def turn(i, first):
                    for s in range(2):
                        pe.wait_ge(lo_made[s], base + i + 1)
                        if not first:
                            evac(s, i)
                        products(ps[s], s, KT[stage], hi, lo).then_inc(w_used[s], 1)

                if ready:
                    first_units(stage, ready)
                else:
                    turn(0, True)
                with pe.Fori(1, UNITS[stage]) as i:
                    turn(i, False)

            def norm(stage):
                n = RES.index(stage)

                def add(out, a, first):
                    for j in range(2):
                        m = nc.tensor.matmul(out[:, j, 0:HALF], invd[:], a[:, j * HALF:(j + 1) * HALF],
                                             start=first, stop=not first)
                    return m

                pe.wait_ge(acc_made, ACCS * (n + 1))
                add(pc, accs, True)
                add(pd, accq, True)
                pe.wait_ge(res_made, DC * (n + 1))
                add(pc, x[:, DC - 1, :], False).then_inc(stats, 1)
                pe.wait_ge(sq_made, DC * (n + 1))
                add(pd, sq, False).then_inc(stats, 1)

            pe.wait_ge(st_in, 16)
            for c in range(DC):
                n = DEC_B * PAD
                m = nc.tensor.transpose(pd[:, c // 4, (c % 4) * n:(c % 4 + 1) * n], sttok[:, c * P:(c + 1) * P],
                                        ident[0:n, 0:n])
            m.then_inc(st_t, 1)
            pe.wait_ge(tab_in, 64)
            pe.wait_ge(rb_copied, 4)
            pe.wait_ge(par_ok, 1)
            pe.wait_ge(in_evac, DC)
            for g, out in enumerate((pa[:, 0, :], pa[:, 1, :], pb[:, 0, :])):
                m = nc.tensor.matmul(out[0:HEADS, 0:RP], rbx[:, g * HEADS:(g + 1) * HEADS], oh_t[:, g, :],
                                     start=True, stop=True)
            m.then_inc(tab_mm, 1)
            for v in range(6):
                for half, cols in enumerate((slice(0, NG * P), slice(NG * P, NG * (P + BW)))):
                    m = nc.tensor.matmul(pc[:, half, 0:cols.stop - cols.start], rb_s[:, v, :], oh_s[:, v, cols],
                                         start=v == 0, stop=v == 5)
            m.then_inc(sb_mm, 1)
            pe.wait_ge(tab_evac, NG)
            pe.wait_ge(consts_made, 2)
            pe.wait_ge(in_evac, DC)
            ready = DC
            up("up0", ready)
            down("down0")
            norm("down0")
            ready += DC
            linear("pin", stream_x, stream_xl, lambda s, i: pe.wait_ge(u_evac, 2 * i - 1 + s), ready)
            pe.wait_ge(u_evac, DC)
            for c in range(DC):
                m = nc.tensor.transpose(pc[0:PAD + SAMP, c // 4, (c % 4) * P:(c % 4 + 1) * P], utail[:, c, :], ident[:])
            m.then_inc(utail_t, 1)
            for g in range(4):
                for s in range(2):
                    pe.wait_ge(lo_made[s], FIRST["pgrp"] + g + 1)
                    pe.wait_ge(pooled, 2 * g + 2)
                    if g >= 1:
                        pe.wait_ge(z_scaled, 2 * g - 1 + s)
                    products(ps[s], s, 2, lambda k: phi[:, 2 * g + k, :], lambda k: plo[:, 2 * g + k, :]) \
                        .then_inc(w_used[s], 1)
            pe.wait_ge(z_ready, DC)
            linear("pout", lambda k: zhi[:, k, :], lambda k: zlo[:, k, :],
                   lambda s, i: pe.wait_ge(res_made, DC * RES.index("pout") + 2 * i - 1 + s))
            norm("pout")
            ready += DC
            up("up1", ready)
            down("down1")
            norm("down1")
            ready += DC

            up("up2", ready)
            down("down2")
            norm("down2")
            ready += DC
            linear("q", stream_x, stream_xl, lambda s, i: pe.wait_ge(q_evac, 2 * i - 1 + s), ready)
            def kv_units(s, i, first=False, each=None):
                pe.wait_ge(lo_made[s], FIRST["kv"] + i + 1)
                if not first:
                    pe.wait_ge(kv_evac[s], i)
                products(ps[s], s, DC, lambda k: yhi[:, k, :], lambda k: ylo[:, k, :], each=each) \
                    .then_inc(w_used[s], 1)

            def kv_transposes(s, i, first=False):
                pe.wait_ge(kv_evac[s], i + 1)
                if not first:
                    pe.wait_ge(kv_tok[s], 2 * i)
                for j in range(QB):
                    nc.tensor.transpose(ps[2 + s][:, 0, j * P:(j + 1) * P], kvt[s][:, j * P:(j + 1) * P], ident[:])
                nc.tensor.matmul(pc[SAMP * s:SAMP * (s + 1), 1, 0:P], kvt[s][:, SEQ:T], ident[:], start=True,
                                 stop=True).then_inc(kv_t[s], 1)

            def turn_keys(b, s, t):
                if t == 0:
                    pe.wait_ge(cached_in[s], 24 * (b - s) + 48)
                if not (first_turn(b) and t == 0):
                    pe.wait_ge(kc_ok, NCK * b + t)
                for c in range(GC):
                    m = nc.tensor.transpose(pd[:, 1, c * P:(c + 1) * P], cached[s][:, t, c * P:(c + 1) * P], ident[:])
                m.then_inc(kc_t, 1)

            def key_scores(b, t):
                if t == 0:
                    pe.wait_ge(qb_ok, b + 1)
                pe.wait_ge(kc_ok, NCK * b + t + 1)
                g, i, n = (0, 0, 2 * DEC_S) if t == 0 else ((t - 1) // 4 + 1, (t - 1) % 4, 2)
                for c in range(GC):
                    at = HALF + g % 2 * 32 + c * 2 * DEC_S + 2 * i
                    m = nc.tensor.matmul(ps[g // 2][:, 1, at:at + n], k_t[t % 3][:, c * P:(c + 1) * P],
                                         q_b[:, g * GC + c, 2 * i:2 * i + n], start=False, stop=False,
                                         skip_group_check=True)
                m.then_inc(kc_used, 1)

            def kv_turn(i, b=None, s=0):
                def each0(k):
                    if k in (2, 3, 4, 6, 7):
                        key_scores(b, (2, 3, 4, 6, 7).index(k))
                    if k in (0, 1, 2, 4, 5, 7):
                        turn_keys(b, s, (0, 1, 2, 4, 5, 7).index(k))

                def each1(k):
                    if 1 <= k < 5:
                        key_scores(b, k + 4)
                    if k < 3:
                        turn_keys(b, s, k + 6)

                kv_units(0, i, each=None if b is None else each0)
                kv_transposes(1, i - 1)
                kv_units(1, i, each=None if b is None else each1)
                kv_transposes(0, i)

            pe.wait_ge(xs_in, 32)
            kv_units(0, 0, True)
            kv_units(1, 0, True)
            kv_transposes(0, 0, True)
            kv_units(0, 1)
            kv_transposes(1, 0, True)
            kv_units(1, 1)
            kv_transposes(0, 1)
            kv_turn(2, 0, 0)
            kv_turn(3, 1, 1)
            with pe.Fori(1, DEC_B // 2) as n:
                kv_turn(2 * n + 2, 2 * n, 0)
                kv_turn(2 * n + 3, 2 * n + 1, 1)
            kv_turn(10)
            kv_turn(11)
            kv_transposes(1, UNITS["kv"] - 1)

            pe.wait_ge(kv_evac[1], UNITS["kv"])
            pe.wait_ge(qbd_ok, 3)
            for g in range(NG):
                for c in range(GC):
                    row = pb[0:SAMP, g // 2, (g % 2) * 256:(g % 2 + 1) * 256]
                    m = nc.tensor.matmul(row.rearrange("p (b c n) -> p b c n", b=DEC_B, c=GC)[:, :, c, :],
                                         kn_t[:, g * GC + c, :],
                                         q_bd[:, g * GC + c, :].rearrange("p (b n) -> p b n", b=DEC_B),
                                         start=True, stop=True)
            m.then_inc(snk_mm, 1)
            pe.wait_ge(kv_evac[0], UNITS["kv"])
            for k in range(2):
                for g in range(NG):
                    nc.tensor.transpose(pa[:, k, g * P:(g + 1) * P], s_sc[:, g, k * P:(k + 1) * P], ident[:])
            pe.wait_ge(snk_ok, 2)
            for k in range(2):
                for g in range(NG):
                    at = NG * P + g * SAMP
                    m = nc.tensor.transpose(pa[:, k, at:at + SAMP], s_nk[:, g * 256 + k * P:g * 256 + (k + 1) * P],
                                            ident[0:SAMP, 0:SAMP])
            m.then_inc(srow_t, 1)
            pe.wait_ge(snorm_ok, 1)
            for g in range(NG):
                for k in range(2):
                    at = (g % 2) * 256 + k * P
                    nc.tensor.transpose(pb[:, g // 2, at:at + P], s_row[:, k, g * P:(g + 1) * P], ident[:])
                    m = nc.tensor.transpose(pa[0:SAMP, g // 2, at:at + P],
                                            s_row[:, k, NG * P + g * SAMP:NG * P + (g + 1) * SAMP], ident[:])
            m.then_inc(pkey_t, 1)

            pe.wait_ge(pkey_ok, 4)
            pe.wait_ge(kv_tok[0], 2 * UNITS["kv"])
            pe.wait_ge(kv_tok[1], 2 * UNITS["kv"])
            for c in range(GC):
                for g in range(NG):
                    at = g * 2 * GW + GW + c * P
                    row = p_nk[:, g * 256:(g + 1) * 256].rearrange("p (b c n) -> p b c n", b=DEC_B, c=GC)
                    m = nc.tensor.matmul(pc[:, 1, c * 64:(c + 1) * 64], kv_n[:, at:at + P], row[:, :, c, :],
                                         start=g == 0, stop=g == NG - 1)
            m.then_inc(snv_done, 1)

            def sample_values(r, s, tiles):
                for t in tiles:
                    if t == 0:
                        pe.wait_ge(value_in[s], 48 * r + 48)
                        pe.wait_ge(pb_ok, 2 * r + s + 1)
                        if s == 0 and not first_turn(r):
                            pe.wait_ge(sv_evac, r)
                    m = nc.tensor.matmul(pd[32 * s:32 * s + 32, 0, :], p_b[s][:, t, :],
                                         v_c0[s][:] if t == 0 else v_c[s][:, t - 1, :],
                                         start=t == 0, stop=t == NCK - 1)
                    if t == NCK - 1:
                        m.then_inc(sv_done, 1)

            def sample_outputs(r):
                pe.wait_ge(sv_evac, r + 1)
                if not first_turn(r):
                    pe.wait_ge(ots_ok, r)
                for c in range(GC):
                    own = ident[0:64, 0:64].rearrange("p (b c n) -> p b c n", b=2, c=GC)[:, :, c, :]
                    m = nc.tensor.matmul(pd[:, 1, c * 16:(c + 1) * 16], o_s[:, c * P:(c + 1) * P], own,
                                         start=True, stop=True)
                m.then_inc(os_t, 1)

            def scores(r, h, first):
                c, lo = h // 2, DH * (h % 2)
                out = pa[:, h % 2, :]
                hd = slice(lo, lo + DH)
                if h >= 2 or not first:
                    pe.wait_ge(s_ok, HEADS * r + h - 1)
                for g in (1, 2):
                    nc.tensor.matmul(out[:, (g + 1) * P:(g + 2) * P], q_r[hd, g * GC + c, :],
                                     k_r[hd, (g - 1) * GC + c, :], start=True, stop=True)
                for b in range(QB):
                    q = q_r[hd, c, 32 * b:32 * b + 32]
                    rows_ = slice(32 * b, 32 * b + 32)
                    if b == 0:
                        for half in range(2):
                            nc.tensor.matmul(out[rows_, half * P:(half + 1) * P], q, kt0[hd, c, 0:P],
                                             start=True, stop=True)
                    else:
                        m = nc.tensor.matmul(out[rows_, 0:256], q, kt0[hd, c, (b - 1) * P:(b + 1) * P],
                                             start=True, stop=True)
                m.then_inc(s_done, 1)

            def turn_probs(r, h, first):
                pe.wait_ge(p_ok, HEADS * r + h + 1)
                if not (first and h < 2):
                    pe.wait_ge(pt_ok, HEADS * r + h - 1)
                for k in range(4):
                    m = nc.tensor.transpose(pb[:, h % 2, k * P:(k + 1) * P], p_p[h % 2][:, k * P:(k + 1) * P], ident[:])
                m.then_inc(pt_done, 1)

            def values(r, h, first):
                pe.wait_ge(pt_ok, HEADS * r + h + 1)
                if h == 0 and not first:
                    pe.wait_ge(on_ok, r)
                out = pc[:, 0, h * DH:(h + 1) * DH]
                pt, cols = pt_p[h % 2], slice(h * DH, (h + 1) * DH)
                for g in (1, 2):
                    nc.tensor.matmul(out, pt[:, (g + 1) * P:(g + 2) * P], v_p[g][:, r, cols], start=g == 1, stop=False,
                                     skip_group_check=True)
                for b in range(QB):
                    rows_ = slice(32 * b, 32 * b + 32)
                    if b:
                        nc.tensor.matmul(out[rows_, :], pt[:, rows_], v_p[0][:, b - 1, cols],
                                         start=False, stop=False, skip_group_check=True)
                    m = nc.tensor.matmul(out[rows_, :], pt[:, P + 32 * b:P + 32 * b + 32], v_p[0][:, b, cols],
                                         start=False, stop=b == QB - 1, skip_group_check=True)
                m.then_inc(pv_done, 1)

            def tile(r, first):
                pe.wait_ge(qk_ok, GC * (r + 1))
                scores(r, 0, first)
                scores(r, 1, first)
                for h in range(HEADS):
                    turn_probs(r, h, first)
                    if h + 2 < HEADS:
                        scores(r, h + 2, first)
                    if first and h == 0:
                        pe.wait_ge(v_in, 16 * NG)
                    if h < 6:
                        sample_values(r, h // 3, range(h % 3 * 3, h % 3 * 3 + 3))
                    values(r, h, first)
                sample_outputs(r)
                pe.wait_ge(on_ok, r + 1)
                if not first:
                    pe.wait_ge(ot_ok, r)
                for c in range(GC):
                    m = nc.tensor.transpose(pc[:, 1, c * P:(c + 1) * P], o_n[:, c * P:(c + 1) * P], ident[:])
                m.then_inc(on_t, 1)

            pe.wait_ge(kt_in, 32)
            pe.wait_ge(snv_ok, 1)
            tile(0, True)
            with pe.Fori(1, QB) as r:
                tile(r, False)
            pe.wait_ge(o_ready, 1)
            linear("wo", lambda k: ohi[:, k, :], lambda k: olo[:, k, :],
                   lambda s, i: pe.wait_ge(res_made, DC * RES.index("wo") + 2 * i - 1 + s))
            norm("wo")
            ready += DC
            up("up3", ready)
            down("down3")
            norm("down3")
            pe.wait_ge(ln_x, DC * RES.index("down3") + DC)
            for j in range(QB + 1):
                if j >= 2:
                    pe.wait_ge(y_ok[0], j - 1)
                    pe.wait_ge(y_ok[1], j - 1)
                n, t0 = (P, j * P) if j < QB else (SAMP, SEQ)
                for c in range(DC):
                    m = nc.tensor.transpose(ps[j % 2][0:n, c // 4, (c % 4) * P:(c % 4 + 1) * P], x[:, c, t0:t0 + n],
                                            ident[:])
                m.then_inc(y_t, 1)

        @block.scalar
        def _(act):
            step = Steps(act_step)

            def round_hi(stage, s, i):
                if stage is None:
                    return
                u = FIRST[stage] + i
                act.wait_ge(raw_in[s], 16 * (u + 1))
                if not (stage == "up0" and first_turn(i)):
                    act.wait_ge(w_used[s], u)
                nc.scalar.activation(whi[s][:, 0:KT[stage], :], raw[s][:, 0:KT[stage], :], ACT.Copy) \
                    .then_inc(hi_made[s], 1)

            def turns(n, stage, body):
                body(0, stage, 1)
                with act.Fori(1, n - 1) as i:
                    body(i, stage, i + 1)
                body(n - 1, AFTER[stage], 0)

            round_hi("up0", 0, 0)
            round_hi("up0", 1, 0)
            act.wait_ge(par_t, 1)
            nc.scalar.activation(par[:], pc[:, 0, 0:NPAR], ACT.Copy).then_inc(par_ok, 1)
            for c in range(DC):
                act.wait_ge(in_t, c + 1)
                nc.scalar.activation(x[:, c, 0:SEQ], ps[c % 2][:, 0, :], ACT.Copy)
                step.add(nc.scalar.activation(x[:, c, SEQ:T], ps[c % 2][:, 1, 0:SAMP], ACT.Copy))
                act.wait_ge(act_step, step.value())
                nc.scalar.activation(xhi[:, c, :], x[:, c, :], ACT.Copy).then_inc(in_evac, 1)
            act.wait_ge(tab_mm, 1)
            for g, src in enumerate((pa[:, 0, :], pa[:, 1, :], pb[:, 0, :])):
                nc.scalar.activation(tab[:, g, :], src[0:HEADS, 0:RP], ACT.Copy).then_inc(tab_evac, 1)
            act.wait_ge(sb_mm, 1)
            nc.scalar.activation(s_bias[:, 0:NG * P], pc[:, 0, 0:NG * P], ACT.Copy).then_inc(sb_evac, 1)
            act.wait_ge(st_t, 1)
            nc.scalar.activation(hist[:].rearrange("p (a c) n -> p a (c n)", a=2), pd[:, :, 0:4 * DEC_B * PAD],
                                 ACT.Copy).then_inc(st_evac, 1)

            def up(stage):
                f, base = int(stage[2]), FIRST[stage]

                def turn(i, nxt, j):
                    act.wait_ge(w_used[0], base + i + 1)
                    if not first_turn(i):
                        act.wait_ge(h_made, FC * f + i)
                    nc.scalar.activation(split(sg[:]), halves(pa), ACT.Silu).then_inc(gate_silu, 1)
                    round_hi(nxt, 0, j)
                    round_hi(nxt, 1, j)
                    act.wait_ge(h_made, FC * f + i + 1)
                    nc.scalar.activation(hhi[:, i, :], hf[:], ACT.Copy).then_inc(h_hi_made, 1)

                turns(FC, stage, turn)

            def square(stage, c, i):
                act.wait_ge(res_made, DC * RES.index(stage) + i + 1)
                if not first_turn(i):
                    act.wait_ge(acc_made, ACCS * RES.index(stage) + 2 * i)
                nc.scalar.activation(sq[:], x[:, c, :], ACT.Square).then_inc(sq_made, 1)

            def root_table():
                nc.scalar.activation(root[:], eps[:], ACT.Sqrt)

            def down(stage):
                def turn(i, nxt, j):
                    round_hi(nxt, 0, j)
                    round_hi(nxt, 1, j)
                    square(stage, i, i)

                root_table()
                turns(DC, stage, turn)

            def norm(stage, k):
                act.wait_ge(stats, 2 * RES.index(stage) + 1)
                nc.scalar.activation(split(var[:]), halves(pc), ACT.Square).then_inc(ln_sq, 1)
                nc.scalar.activation(split(mean[:]), halves(pc), ACT.Copy).then_inc(ln_mean, 1)
                act.wait_ge(ln_var, RES.index(stage) + 1)
                nc.scalar.activation(rstd[:], var[:], ACT.Sqrt, bias=eps[:, 0:1]).then_inc(ln_std, 1)
                for c in range(DC):
                    act.wait_ge(ln_t, DC * RES.index(stage) + c + 1)
                    affine = dict(bias=par[:, PB + k * DC + c:PB + k * DC + c + 1],
                                  scale=par[:, PG + k * DC + c:PG + k * DC + c + 1])
                    if stage != "down3":
                        nc.scalar.activation(xhi[:, c, :], x[:, c, :], ACT.Identity, **affine)
                    nc.scalar.activation(x[:, c, :], x[:, c, :], ACT.Identity, **affine).then_inc(ln_x, 1)

            up("up0")
            down("down0")
            norm("down0", 0)

            def pin(i, nxt, j):
                for s in range(2):
                    c = 2 * i + s
                    act.wait_ge(w_used[s], FIRST["pin"] + i + 1)
                    if i >= 1:
                        act.wait_ge(pooled, 2 * (i - 1) + s + 1)
                    else:
                        act.wait_ge(consts_made, 4)
                    samples = ue[s][:, 16 + SEQ:].rearrange("p (b t) -> p b t", t=20)[:, :, 16:20]
                    nc.scalar.activation(ue[s][:, 16:16 + HALF], ps[s][:, 0, 0:HALF], ACT.Copy)
                    nc.scalar.activation(ue[s][:, 16 + HALF:16 + SEQ], ps[s][:, 1, 0:SEQ - HALF], ACT.Copy)
                    nc.scalar.activation(samples, ps[s][:, 1, SEQ - HALF:HALF].rearrange("p (b t) -> p b t", t=4),
                                         ACT.Copy)
                    nc.scalar.activation(utail[:, c, :], ps[s][:, 1, HALF - PAD - SAMP:HALF], ACT.Copy) \
                        .then_inc(u_evac, 1)
                    round_hi(nxt, s, j)

            for i in range(UNITS["pin"]):
                if i + 1 < UNITS["pin"]:
                    pin(i, "pin", i + 1)
                else:
                    pin(i, "pgrp", 0)
            act.wait_ge(utail_t, 1)
            for b in range(2):
                m = nc.scalar.activation(utok[:, b * 512:(b + 1) * 512], pc[0:PAD + SAMP, b, :], ACT.Copy)
            m.then_inc(utok_ok, 1)

            def pgrp(i, nxt, j):
                for s in range(2):
                    c = 2 * i + s
                    act.wait_ge(w_used[s], FIRST["pgrp"] + i + 1)
                    if c >= 2:
                        act.wait_ge(z_ready, c - 1)
                    zf = (sg, hf)[s]
                    step.add(nc.scalar.activation(split(zf[:]), halves(ps[s]), ACT.Copy,
                                                  scale=par[:, PS + c:PS + c + 1]))
                    z_step = step.value()
                    act.wait_ge(act_step, z_step)
                    nc.scalar.activation(zhi[:, c, :], zf[:], ACT.Copy).then_inc(z_scaled, 1)
                for s in range(2):
                    round_hi(nxt, s, j)

            act.wait_ge(pooled, DC)
            for i in range(4):
                if i < 3:
                    pgrp(i, "pgrp", i + 1)
                else:
                    pgrp(i, "pout", 0)

            def residual_pair(stage):
                def turn(i, nxt, j):
                    for s in range(2):
                        round_hi(nxt, s, j)
                        square(stage, 2 * i + s, 2 * i + s)

                root_table()
                turns(UNITS[stage], stage, turn)

            residual_pair("pout")
            norm("pout", 1)
            act.wait_ge(utok_out, 32)
            up("up1")
            down("down1")
            norm("down1", 2)

            up("up2")
            down("down2")
            act.wait_ge(xs_out, 32)
            norm("down2", 3)

            def q_turn(i, nxt, j):
                for s in range(2):
                    act.wait_ge(w_used[s], FIRST["q"] + i + 1)
                    nc.scalar.activation(split(qt[:, 2 * i + s, :]), halves(ps[s]), ACT.Copy, scale=DH ** -0.5) \
                        .then_inc(q_evac, 1)
                    round_hi(nxt, s, j)

            turns(UNITS["q"], "q", q_turn)
            def kv_chunk(s, i, stored, nxt, j, first=False, keys=None, b=None):
                act.wait_ge(w_used[s], FIRST["kv"] + i + 1)
                if not first:
                    act.wait_ge(kv_t[s], i)
                    act.wait_ge(kt_out[s], 16 * stored)
                if keys is not None:
                    nc.scalar.activation(kn_t[:, bass.ds(keys + s, 1), :], ps[s][:, 1:2, HALF - SAMP:HALF], ACT.Copy)
                if b is not None:
                    g0, n = (0, 2) if s == 0 else (2, 1)
                    nc.scalar.activation(s_sc[:, g0:g0 + n, bass.ds(32 * b, 32)],
                                         ps[s][:, 1, HALF:HALF + 32 * n].rearrange("p (g n) -> p g n", g=n), ACT.Copy)
                nc.scalar.activation(split(kvt[s][:]), halves(ps[s]), ACT.Copy).then_inc(kv_evac[s], 1)
                round_hi(nxt, s, j)

            def kv_tokens(s, i, first=False):
                act.wait_ge(kv_t[s], i + 1)
                if not first:
                    act.wait_ge(kv_out[s], 32 * i)
                nc.scalar.activation(kvp[s][:].rearrange("p j n -> p (j n)"), ps[2 + s][:, 0, :], ACT.Copy) \
                    .then_inc(kv_tok[s], 1)
                nc.scalar.activation(kv_n[:, bass.ds((2 * i + s) * P, P)], pc[SAMP * s:SAMP * (s + 1), 1, 0:P],
                                     ACT.Copy) \
                    .then_inc(kv_tok[s], 1)

            def kv_turn(i, stored, nxt, j, keys=None, b=None):
                kv_chunk(0, i, stored, nxt, j, keys=keys, b=b)
                kv_tokens(1, i - 1)
                kv_chunk(1, i, stored, nxt, j, keys=keys, b=b)
                kv_tokens(0, i)

            kv_chunk(0, 0, 0, "kv", 1, True, keys=0)
            kv_chunk(1, 0, 0, "kv", 1, True, keys=0)
            kv_tokens(0, 0, True)
            kv_chunk(0, 1, 1, "kv", 2, keys=2)
            kv_tokens(1, 0, True)
            kv_chunk(1, 1, 1, "kv", 2, keys=2)
            kv_tokens(0, 1)
            for g in range(NG):
                if g:
                    with act.Fori(0, 2) as i:
                        kv_turn(i + 4 * g, i + 2 * g, "kv", i + 4 * g + 1, keys=2 * i + 4 * g, b=i + 4 * g - 2)
                if g < 2:
                    with act.Fori(0, 2) as i:
                        kv_turn(i + 4 * g + 2, 2 * g + 2, "kv", i + 4 * g + 3, b=i + 4 * g)
            kv_turn(10, 6, "kv", 11)
            kv_turn(11, 6, None, 0)
            kv_tokens(1, 11)

            act.wait_ge(snk_mm, 1)
            nc.scalar.activation(s_nk[:, 0:512], pb[0:SAMP, 0, :], ACT.Copy).then_inc(snk_ok, 1)
            nc.scalar.activation(s_nk[:, 512:768], pb[0:SAMP, 1, 0:256], ACT.Copy).then_inc(snk_ok, 1)
            act.wait_ge(smax_ok, 1)
            for k in range(2):
                nc.scalar.activation(s_row[:, k, :], s_row[:, k, :], ACT.Exp, bias=s_stat[:, 2 + k:3 + k],
                                     accum_out=s_stat[:, 4 + k:5 + k]).then_inc(sexp_ok, 1)
            act.wait_ge(pkey_t, 1)
            for dst, src in ((p_key, pb[:]), (p_nk, pa[0:SAMP])):
                nc.scalar.activation(dst[:, 0:512], src[:, 0, :], ACT.Copy).then_inc(pkey_ok, 1)
                nc.scalar.activation(dst[:, 512:768], src[:, 1, 0:256], ACT.Copy).then_inc(pkey_ok, 1)

            def exps(r, h, first):
                act.wait_ge(s_ok, HEADS * r + h + 1)
                if not (first and h < 2):
                    act.wait_ge(pt_done, HEADS * r + h - 1)
                nc.scalar.activation(p_p[h % 2][:], s_p[h % 2][:], ACT.Exp, bias=a_stat[:, 1, r, h:h + 1],
                                     accum_out=a_stat[:, 2, r, h:h + 1]).then_inc(p_ok, 1)

            def turned(r, h, first):
                act.wait_ge(pt_done, HEADS * r + h + 1)
                if not (first and h < 2):
                    act.wait_ge(pv_done, HEADS * r + h - 1)
                nc.scalar.activation(pt_p[h % 2][:], pb[:, h % 2, :], ACT.Copy).then_inc(pt_ok, 1)

            def tile(r, first):
                exps(r, 0, first)
                for h in range(HEADS):
                    if h + 1 < HEADS:
                        exps(r, h + 1, first)
                    turned(r, h, first)
                act.wait_ge(on_t, r + 1)
                tokens = ot[:, :, 0:SEQ].rearrange("p c (q r) -> p c q r", r=QB)
                nc.scalar.activation(tokens[:, :, :, r], pc[:, 1, :].rearrange("p (c q) -> p c q", c=GC), ACT.Copy) \
                    .then_inc(ot_ok, 1)

            tile(0, True)
            with act.Fori(1, QB) as r:
                tile(r, False)
            round_hi("wo", 0, 0)
            round_hi("wo", 1, 0)
            act.wait_ge(ot_ok, QB)
            act.wait_ge(ots_ok, QB)
            nc.scalar.activation(ohi[:], ot[:], ACT.Copy).then_inc(ohi_ok, 1)
            residual_pair("wo")
            norm("wo", 4)
            up("up3")
            down("down3")
            norm("down3", 5)
            for j in range(QB + 1):
                n = P if j < QB else SAMP
                act.wait_ge(y_t, j + 1)
                nc.scalar.activation(ytok[0:n, j, 0:512], ps[j % 2][0:n, 0, :], ACT.Copy).then_inc(y_ok[0], 1)

        @block.vector
        def _(dve):
            step = Steps(dve_step)

            def round_lo(stage, s, i):
                if stage is None:
                    return
                k = KT[stage]
                dve.wait_ge(hi_made[s], FIRST[stage] + i + 1)
                nc.vector.tensor_tensor(wlo[s][:, 0:k, :], raw[s][:, 0:k, :], whi[s][:, 0:k, :].bitcast(F32),
                                        ALU.subtract).then_inc(lo_made[s], 1)

            def turns(n, stage, body):
                body(0, stage, 1)
                with dve.Fori(1, n - 1) as i:
                    body(i, stage, i + 1)
                body(n - 1, AFTER[stage], 0)

            nc.vector.memset(invd[:], 1.0 / D).then_inc(consts_made, 1)
            nc.vector.memset(eps[:], LN_EPS).then_inc(consts_made, 1)
            nc.vector.memset(rbx[NBUCKET:NBUCKET + 1, :], NEG).then_inc(rb_copied, 1)
            nc.vector.memset(rb_s[:], 0.0).then_inc(rb_copied, 1)
            round_lo("up0", 0, 0)
            round_lo("up0", 1, 0)
            dve.wait_ge(tab_in, 64)
            dve.wait_ge(rb_copied, 2)
            n = NBUCKET + 1
            def heads(g):
                return rbx[:, g * HEADS:(g + 1) * HEADS].rearrange("k (c h) -> k c h", c=GC).unsqueeze(1) \
                    .to_broadcast([n, 4, GC, 2])

            for v in range(6):
                for i in range(DEC_S) if v >= DEC_S else (v,):
                    m = nc.vector.tensor_copy(
                        rb_s[:, v, :].rearrange("k (b c i h) -> k b c i h", b=4, c=GC, h=2)[:, :, :, i, :],
                        heads(max(0, v - 3)))
            m.then_inc(rb_copied, 2)
            for c in range(DC):
                dve.wait_ge(in_evac, c + 1)
                nc.vector.tensor_tensor(xlo[:, c, :], x[:, c, :], xhi[:, c, :].bitcast(F32), ALU.subtract) \
                    .then_inc(x_ready, 1)
            dve.wait_ge(sb_mm, 1)
            nc.vector.tensor_tensor(s_bias[:, NG * P:], pc[:, 1, 0:NG * BW], smask[:], ALU.add).then_inc(sbn_ok, 1)

            def up(stage):
                f, base = int(stage[2]), FIRST[stage]

                def turn(i, nxt, j):
                    round_lo(nxt, 0, j)
                    dve.wait_ge(w_used[1], base + i + 1)
                    dve.wait_ge(gate_silu, FC * f + i + 1)
                    if not first_turn(i):
                        dve.wait_ge(h_lo_made, FC * f + i)
                    nc.vector.tensor_tensor(split(hf[:]), split(sg[:]), halves(pb), ALU.mult).then_inc(h_made, 1)
                    round_lo(nxt, 1, j)
                    dve.wait_ge(h_hi_made, FC * f + i + 1)
                    nc.vector.tensor_tensor(hlo[:, i, :], hf[:], hhi[:, i, :].bitcast(F32), ALU.subtract) \
                        .then_inc(h_lo_made, 1)

                turns(FC, stage, turn)

            def residual(stage, out, c, scale, s, used):
                dve.wait_ge(w_used[s], used)
                nc.vector.scalar_tensor_tensor(out=split(x[:, c, :]), in0=halves(out), scalar=scale,
                                               in1=split(x[:, c, :]), op0=ALU.mult, op1=ALU.add) \
                    .then_inc(res_made, 1)

            def down(stage):
                base = FIRST[stage]

                def pair(i, last):
                    for h in range(2):
                        nxt, j = (AFTER[stage], 0) if last and h else (stage, i + h + 1)
                        round_lo(nxt, 0, j)
                        residual(stage, ps[h], i + h, 0.5 / ALPHA, 1, base + i + h + 1)
                        round_lo(nxt, 1, j)

                with dve.Fori(0, DC - 2, 2) as i:
                    pair(i, False)
                pair(DC - 2, True)

            def norm(stage, last=False):
                dve.wait_ge(stats, 2 * RES.index(stage) + 2)
                dve.wait_ge(ln_sq, RES.index(stage) + 1)
                nc.vector.tensor_tensor(split(var[:]), halves(pd), split(var[:]), ALU.subtract).then_inc(ln_var, 1)
                dve.wait_ge(ln_mean, RES.index(stage) + 1)
                for c in range(EARLY):
                    nc.vector.tensor_tensor(x[:, c, :], x[:, c, :], mean[:], ALU.subtract)
                dve.wait_ge(ln_std, RES.index(stage) + 1)
                step.add(nc.vector.reciprocal(rstd[:], rstd[:]))
                dve.wait_ge(dve_step, step.value())
                for c in range(DC):
                    if c >= EARLY:
                        dve.wait_ge(ln_sub, (DC - EARLY) * RES.index(stage) + c - EARLY + 1)
                    nc.vector.tensor_tensor(x[:, c, :], x[:, c, :], rstd[:], ALU.mult).then_inc(ln_t, 1)
                    if c >= 1 and not last:
                        low(stage, c - 1)
                if not last:
                    low(stage, DC - 1)

            def low(stage, c):
                dve.wait_ge(ln_x, DC * RES.index(stage) + c + 1)
                nc.vector.tensor_tensor(xlo[:, c, :], x[:, c, :], xhi[:, c, :].bitcast(F32), ALU.subtract) \
                    .then_inc(x_ready, 1)

            up("up0")
            down("down0")
            norm("down0")

            for s in range(2):
                nc.vector.memset(ue[s][:, 0:16], 0.0).then_inc(consts_made, 1)
            def pin(i, nxt, j):
                for s in range(2):
                    c = 2 * i + s
                    g = c // 2
                    tail = lambda t: t[:, 16 + SEQ:].rearrange("p (b t) -> p b t", t=20)
                    e = ue[s]
                    if i == 0:
                        dve.wait_ge(st_evac, 1)
                    if c:
                        dve.wait_ge(pooled, c)
                    step.add(nc.vector.tensor_copy(tail(e)[:, :, 1:16], hist[:, c, :].rearrange("p (b t) -> p b t", t=PAD)))
                    dve.wait_ge(dve_step, step.value())
                    dve.wait_ge(u_evac, c + 1)
                    src, w = e, 1
                    for level in range(g + 1):
                        dst = us[level % 2]
                        nc.vector.tensor_tensor(dst[:, 2 * w - 1:16 + SEQ], src[:, 2 * w - 1:16 + SEQ],
                                                src[:, w - 1:16 + SEQ - w], ALU.add)
                        step.add(nc.vector.tensor_tensor(tail(dst)[:, :, 2 * w:20], tail(src)[:, :, 2 * w:20],
                                                         tail(src)[:, :, w:20 - w], ALU.add))
                        dve.wait_ge(dve_step, step.value())
                        src, w = dst, 2 * w
                    mean_, diff = us[(g + 1) % 2], us[g % 2]
                    nc.vector.tensor_tensor(mean_[:, 16:32], src[:, 16:32], inv[:, g, :], ALU.mult)
                    nc.vector.tensor_scalar(mean_[:, 32:16 + SEQ], src[:, 32:16 + SEQ], 1.0 / w, None, ALU.mult)
                    step.add(nc.vector.tensor_scalar(tail(mean_)[:, :, 16:20], tail(src)[:, :, 16:20], 1.0 / w, None,
                                                     ALU.mult))
                    dve.wait_ge(dve_step, step.value())
                    nc.vector.tensor_tensor(diff[:, 0:SEQ], mean_[:, 16:16 + SEQ], e[:, 16:16 + SEQ], ALU.subtract)
                    step.add(nc.vector.tensor_tensor(diff[:, SEQ:T].rearrange("p (b t) -> p b t", t=4),
                                                     tail(mean_)[:, :, 16:20], tail(e)[:, :, 16:20], ALU.subtract))
                    dve.wait_ge(dve_step, step.value())
                    step.add(nc.vector.tensor_copy(phi[:, c, :], diff[:, 0:T]))
                    dve.wait_ge(dve_step, step.value())
                    nc.vector.tensor_tensor(plo[:, c, :], diff[:, 0:T], phi[:, c, :].bitcast(F32), ALU.subtract) \
                        .then_inc(pooled, 1)
                    round_lo(nxt, s, j)

            dve.wait_ge(consts_in, 32)
            for i in range(UNITS["pin"]):
                if i + 1 < UNITS["pin"]:
                    pin(i, "pin", i + 1)
                else:
                    pin(i, "pgrp", 0)

            def pgrp(i, nxt, j):
                for s in range(2):
                    c = 2 * i + s
                    dve.wait_ge(z_scaled, c + 1)
                    nc.vector.tensor_tensor(zlo[:, c, :], (sg, hf)[s][:], zhi[:, c, :].bitcast(F32), ALU.subtract) \
                        .then_inc(z_ready, 1)
                    round_lo(nxt, s, j)

            for i in range(4):
                if i < 3:
                    pgrp(i, "pgrp", i + 1)
                else:
                    pgrp(i, "pout", 0)

            def residual_pair(stage):
                def turn(i, nxt, j):
                    for s in range(2):
                        residual(stage, ps[s], 2 * i + s, 1.0 / ALPHA, s, FIRST[stage] + i + 1)
                        round_lo(nxt, s, j)

                turns(UNITS[stage], stage, turn)

            residual_pair("pout")
            norm("pout")
            dve.wait_ge(utok_out, 32)
            up("up1")
            down("down1")
            norm("down1")

            up("up2")
            down("down2")
            norm("down2")

            def q_turn(i, nxt, j):
                round_lo(nxt, 0, j)
                round_lo(nxt, 1, j)

            turns(UNITS["q"], "q", q_turn)

            def turned_keys(b, tiles):
                for t in tiles:
                    dve.wait_ge(kc_t, NCK * b + t + 1)
                    if t >= 3:
                        dve.wait_ge(kc_used, NCK * b + t - 2)
                    elif t == 0 and not first_turn(b):
                        dve.wait_ge(kc_used, NCK * b)
                    nc.vector.tensor_copy(k_t[t % 3][:], pd[:, 1, :]).then_inc(kc_ok, 1)

            def kv_turn(i, nxt, j, b=None):
                if b is not None:
                    turned_keys(b, range(3))
                round_lo("kv", 1, i)
                if b is not None:
                    turned_keys(b, range(3, NCK))
                round_lo(nxt, 0, j)

            round_lo("kv", 0, 1)
            kv_turn(1, "kv", 2)
            kv_turn(2, "kv", 3, 0)
            with dve.Fori(1, DEC_B) as b:
                kv_turn(b + 2, "kv", b + 3, b)
            kv_turn(10, "kv", 11)
            kv_turn(11, None, 0)

            dve.wait_ge(srow_t, 1)
            dve.wait_ge(sb_evac, 1)
            for k in range(2):
                nc.vector.tensor_tensor(s_row[:, k, 0:NG * P], pa[:, k, 0:NG * P], s_bias[:, 0:NG * P], ALU.add)
                seen = s_bias[:, NG * P:].rearrange("p (g n) -> p g n", g=NG)[:, :, 16 - 16 * k:16 - 16 * k + SAMP]
                m = nc.vector.tensor_tensor(s_row[:, k, NG * P:SK].rearrange("p (g n) -> p g n", g=NG),
                                            pa[:, k, NG * P:SK].rearrange("p (g n) -> p g n", g=NG), seen, ALU.add)
            step.add(m)
            dve.wait_ge(dve_step, step.value())
            step.add(nc.vector.reduce_max(s_stat[:, 0:2], s_row, axis=AX_X))
            dve.wait_ge(dve_step, step.value())
            nc.vector.tensor_scalar(s_stat[:, 2:4], s_stat[:, 0:2], -1.0, None, ALU.mult).then_inc(smax_ok, 1)
            dve.wait_ge(sexp_ok, 2)
            step.add(nc.vector.reciprocal(s_stat[:, 6:8], s_stat[:, 4:6]))
            dve.wait_ge(dve_step, step.value())
            for k in range(2):
                m = nc.vector.tensor_scalar(s_row[:, k, :], s_row[:, k, :], s_stat[:, 6 + k:7 + k], None, ALU.mult)
            m.then_inc(snorm_ok, 1)

            dve.wait_ge(snv_done, 1)
            for h in range(2):
                part = slice(DH * h, DH * h + DH)
                m = nc.vector.tensor_copy(
                    ot[part, :, SEQ:T],
                    pc[part, 1, 0:GC * 2 * SAMP].rearrange("p (c t h) -> p c t h", c=GC, h=2)[:, :, :, h])
            m.then_inc(snv_ok, 1)

            def sample_values(r):
                dve.wait_ge(sv_done, 2 * r + 2)
                if not first_turn(r):
                    dve.wait_ge(os_t, r)
                nc.vector.tensor_copy(o_s, pd[0:64, 0, :]).then_inc(sv_evac, 1)

            def sample_outputs(r):
                dve.wait_ge(os_t, r + 1)
                for h in range(2):
                    part = slice(DH * h, DH * h + DH)
                    dst = ot[part, :, bass.ds(SEQ + 2 * DEC_S * r, 2 * DEC_S)]
                    src = pd[part, 1, 0:GC * 16].rearrange("p (c t h) -> p c t h", c=GC, h=2)
                    m = nc.vector.tensor_tensor(dst, src[:, :, :, h], dst, ALU.add)
                m.then_inc(ots_ok, 1)

            dve.wait_ge(snv_ok, 1)
            dve.wait_ge(kvn_out, 16 * NG)
            for h in range(HEADS):
                m = nc.vector.memset(b0[0:32, h, 0:P], NEG)
            m.then_inc(b0_pad, 1)

            def qk_tile(r, c):
                q = qt[:, :, 0:SEQ].rearrange("p (g c) (q r) -> p g c q r", g=NG, r=QB)
                k = kt12[:].rearrange("p (g c) (q r) -> p g c q r", g=2, r=QB)
                for g in range(NG):
                    nc.vector.tensor_copy(q_r[:, g * GC + c, :], q[:, g, c, :, r])
                for g in range(2):
                    m = nc.vector.tensor_copy(k_r[:, g * GC + c, :], k[:, g, c, :, r])
                m.then_inc(qk_ok, 1)

            def head(r, h):
                dve.wait_ge(s_done, HEADS * r + h + 1)
                dve.wait_ge(b0_in[h // 4], 64 * (r + 1))
                b = h % 2
                if not (first_turn(r) and h < 2):
                    dve.wait_ge(p_ok, HEADS * r + h - 1)
                nc.vector.tensor_tensor(s_p[b][:, 0:256], pa[:, b, 0:256], b0[:, h, :], ALU.add)
                step.add(nc.vector.tensor_tensor(s_p[b][:, 256:512], pa[:, b, 256:512], b12[:, h, :], ALU.add))
                dve.wait_ge(dve_step, step.value())
                step.add(nc.vector.reduce_max(a_stat[:, 0, r, h:h + 1], s_p[b][:], axis=AX_X))
                dve.wait_ge(dve_step, step.value())
                nc.vector.tensor_scalar(a_stat[:, 1, r, h:h + 1], a_stat[:, 0, r, h:h + 1], -1.0, None, ALU.mult) \
                    .then_inc(s_ok, 1)

            def tile(r, last):
                for h in range(HEADS):
                    head(r, h)
                    if h % 2 and not last:
                        qk_tile(r + 1, h // 2)
                dve.wait_ge(p_ok, HEADS * (r + 1))
                step.add(nc.vector.reciprocal(a_stat[:, 3, r, :], a_stat[:, 2, r, :]))
                dve.wait_ge(dve_step, step.value())
                sample_values(r)
                dve.wait_ge(pv_done, HEADS * (r + 1))
                if not first_turn(r):
                    dve.wait_ge(on_t, r)
                nc.vector.tensor_tensor(o_n[:].rearrange("p (h d) -> p h d", d=DH),
                                        pc[:, 0, :].rearrange("p (h d) -> p h d", d=DH),
                                        a_stat[:, 3, r, :].unsqueeze(2).to_broadcast([P, HEADS, DH]), ALU.mult) \
                    .then_inc(on_ok, 1)
                sample_outputs(r)

            dve.wait_ge(kt_in, 32)
            for c in range(GC):
                qk_tile(0, c)
            dve.wait_ge(b12_in, 32)
            tile(0, False)
            with dve.Fori(1, QB - 1) as r:
                step.turn(r - 1, 2 * HEADS + 1)
                tile(r, False)
                step.turns(QB - 2)
            tile(QB - 1, True)
            round_lo("wo", 0, 0)
            round_lo("wo", 1, 0)
            dve.wait_ge(ohi_ok, 1)
            nc.vector.tensor_tensor(olo[:], ot[:], ohi[:].bitcast(F32), ALU.subtract).then_inc(o_ready, 1)
            residual_pair("wo")
            norm("wo")
            up("up3")
            down("down3")
            norm("down3", last=True)
            for j in range(QB + 1):
                n = P if j < QB else SAMP
                dve.wait_ge(y_t, j + 1)
                nc.vector.tensor_copy(ytok[0:n, j, 512:D], ps[j % 2][0:n, 1, :]).then_inc(y_ok[1], 1)

        @block.gpsimd
        def _(pool):
            def sums(stage):
                nc.gpsimd.memset(accs[:], 0.0).then_inc(acc_zero, 1)
                nc.gpsimd.memset(accq[:], 0.0).then_inc(acc_zero, 1)
                pool.wait_ge(acc_zero, 2 * RES.index(stage) + 2)
                base = RES.index(stage)

                def add(c):
                    if not first_turn(c):
                        pool.wait_ge(acc_made, ACCS * base + 2 * c)
                    pool.wait_ge(res_made, DC * base + c + 1)
                    nc.gpsimd.tensor_tensor(accs[:], accs[:], x[:, c, :], ALU.add).then_inc(acc_made, 1)
                    pool.wait_ge(sq_made, DC * base + c + 1)
                    nc.gpsimd.tensor_tensor(accq[:], accq[:], sq[:], ALU.add).then_inc(acc_made, 1)

                add(0)
                with pool.Fori(1, DC - 1) as c:
                    add(c)

            def centre(stage):
                pool.wait_ge(stats, 2 * RES.index(stage) + 2)
                pool.wait_ge(ln_mean, RES.index(stage) + 1)
                for c in range(EARLY, DC):
                    nc.gpsimd.tensor_tensor(x[:, c, :], x[:, c, :], mean[:], ALU.subtract).then_inc(ln_sub, 1)

            sums("down0")
            centre("down0")
            pool.wait_ge(utok_ok, 1)
            pool.dma_start(O["pool_p"][0, 0, :, :], utok[0:PAD, :]).then_inc(utok_out, 16)
            pool.dma_start(O["pool_s"][0, :, PAD - DEC_S:PAD, :], utok[PAD:PAD + SAMP, :]).then_inc(utok_out, 16)
            sums("pout")
            centre("pout")
            sums("down1")
            centre("down1")

            sums("down2")
            centre("down2")

            c0 = A["cache_kv_w128"].rearrange("b p k h d -> b p k (h d)")
            c1 = A["cache_kv_w512"].rearrange("b (p i) k h d -> b p i k (h d)", i=DIL[1])
            c2 = A["cache_kv_w2048"].rearrange("b (p i) k h d -> b p i k (h d)", i=DIL[2])

            def load(b, first, rest, kv, into):
                pool.dma_start(first, c0[b, :, kv, :]).then_inc(into, 16)
                pool.dma_start(rest[:, 0:4, :], c1[b, :, :, kv, :]).then_inc(into, 16)
                pool.dma_start(rest[:, 4:8, :], c2[b, :, 0:DEC_S, kv, :]).then_inc(into, 16)

            def load_keys(b, s):
                if not (isinstance(b, int) and b < 2):
                    pool.wait_ge(kc_t, NCK * b - NCK)
                load(b, cached[s][:, 0, :], cached[s][:, 1:NCK, :], 0, cached_in[s])

            def load_values(b, s):
                load(b, v_c0[s][:], v_c[s], 1, value_in[s])

            def queries(b):
                if not first_turn(b):
                    pool.wait_ge(kc_used, NCK * b)
                nc.gpsimd.tensor_copy(q_b[:], q_bd[:, :, bass.ds(2 * DEC_S * b, 2 * DEC_S)]).then_inc(qb_ok, 1)

            for s in range(2):
                pool.wait_ge(w_used[s], FIRST["kv"])
            load_keys(0, 0)
            load_keys(1, 1)
            nc.gpsimd.memset(q_bd[:], 0.0).then_inc(qbd_ok, 1)
            pool.wait_ge(qbd_ok, 1)
            pool.wait_ge(q_evac, NG * GC)
            for h in range(2):
                part = slice(DH * h, DH * h + DH)
                nc.gpsimd.tensor_copy(q_bd[part].rearrange("p c (t h) -> p c t h", h=2)[:, :, :, h],
                                      qt[part, :, SEQ:T]).then_inc(qbd_ok, 1)
            pool.wait_ge(qbd_ok, 3)
            queries(0)
            with pool.Fori(1, DEC_B // 2) as n:
                load_keys(2 * n, 0)
                queries(2 * n - 1)
                load_keys(2 * n + 1, 1)
                queries(2 * n)
            queries(DEC_B - 1)
            for s in range(2):
                pool.wait_ge(w_used[s], FIRST["wo"])
            load_values(0, 0)
            pool.wait_ge(snk_mm, 1)
            load_values(1, 1)

            def probs(b, s):
                own = p_key.rearrange("p (g n) -> p g n", g=NG)[:, :, bass.ds(32 * b, 32)]
                nc.gpsimd.tensor_copy(p_b[s][:, 0, :], own[:, 0, :])
                own = own.rearrange("p g (c i h) -> p g c i h", c=GC, h=2)
                tiles = p_b[s][:, 1:, :].rearrange("p (g i) n -> p g i n", g=2)
                for i in range(DEC_S):
                    m = nc.gpsimd.tensor_copy(
                        tiles[:, :, i, :].rearrange("p g (c i h) -> p g c i h", c=GC, h=2)[:, :, :, i, :],
                        own[:, 1:, :, i, :])
                m.then_inc(pb_ok, 1)

            pool.wait_ge(srow_t, 1)
            for s in range(2):
                nc.gpsimd.memset(p_b[s], 0.0).then_inc(pb_zero, 1)
            pool.wait_ge(pb_zero, 2)
            pool.wait_ge(pkey_ok, 4)
            probs(0, 0)
            probs(1, 1)
            with pool.Fori(1, DEC_B // 2) as n:
                for s in range(2):
                    pool.wait_ge(sv_done, 2 * n + s - 1)
                    load_values(2 * n + s, s)
                    probs(2 * n + s, s)
            pool.wait_ge(o_ready, 1)
            sums("wo")
            centre("wo")
            sums("down3")
            centre("down3")


OUTPUTS = [("y_p", (1, SEQ, D)), ("y_s", (DEC_B, DEC_S, D)), ("pool_p", (1, 1, PAD, D)), ("pool_s", (1, DEC_B, PAD, D)),
           ("kv_p0", (1, 128, 2, HEADS, DH)), ("kv_p1", (1, SEQ, 2, HEADS, DH)), ("kv_p2", (1, SEQ, 2, HEADS, DH)),
           ("kv_s0", (DEC_B, DEC_S, 2, HEADS, DH)), ("kv_s1", (DEC_B, DEC_S, 2, HEADS, DH)),
           ("kv_s2", (DEC_B, DEC_S, 2, HEADS, DH))]


def kernel(**inputs):
    import concourse.bacc as bacc
    from concourse.bass_utils import run_bass_kernel_spmd

    nc = bacc.Bacc("TRN2", target_bir_lowering=False, num_devices=1)
    arrays, A, O = {}, {}, {}
    for name, a in {**inputs, **shape_constants()}.items():
        a = np.ascontiguousarray(a)
        arrays["in_" + name] = a
        A[name] = nc.dram_tensor("in_" + name, a.shape, mybir.dt.from_np(a.dtype), kind="ExternalInput").ap()
    for name, shape in OUTPUTS:
        O[name] = nc.dram_tensor("out_" + name, shape, F32, kind="ExternalOutput").ap()
    build(nc, A, O)
    r = run_bass_kernel_spmd(nc, [arrays], core_ids=[0])
    return tuple(r.results[0]["out_" + name] for name, _ in OUTPUTS)
```

```python
import math
from contextlib import ExitStack

import concourse.bass as bass
import numpy as np
from concourse import mybir

F32 = mybir.dt.float32
F32R = mybir.dt.float32r
ACT = mybir.ActivationFunctionType
ALU = mybir.AluOpType
AX_X = mybir.AxisListType.X

P = 128
D, SEQ, DEC_B, DEC_S = 1024, 512, 8, 4
SAMP = DEC_B * DEC_S
T = SEQ + SAMP
HALF = T // 2
DC = D // P
FF = 2816
FC = FF // P
KH = FC // 2
PAD = 15
DH = 64
HEADS = 8
GW = HEADS * DH
GC = GW // P
NG = 3
DIL = (1, 4, 16)
WIN = (128, 512, 2048)
NKEY = 129
NBUCKET, MAXDIST = 32, 2048
QB = SEQ // P
ALPHA = (2.0 * 2) ** 0.25
LN_EPS = 1e-5 / ALPHA ** 2
NEG = -1e30
RP = 384
SK = NG * (P + SAMP)
NCK = 9
BW = 16 + SAMP

PG, PB, PS = 0, 48, 96
NPAR = 104

STAGES = [("up0", 22, 8), ("down0", 8, 11), ("pin", 4, 8), ("pgrp", 1, 8), ("pout", 4, 8),
          ("up1", 22, 8), ("down1", 8, 11), ("up2", 22, 8), ("down2", 8, 11),
          ("q", 6, 8), ("kv", 12, 8), ("wo", 4, 4), ("up3", 22, 8), ("down3", 8, 11)]
EARLY = 3
ACCS = 2 * (DC - 1)
RES = ("down0", "pout", "down1", "down2", "wo", "down3")
UNITS = {n: u for n, u, _ in STAGES}
KT = {n: k for n, _, k in STAGES}
FIRST, AFTER = {}, {}
_at = 0
for _j, (_n, _u, _k) in enumerate(STAGES):
    FIRST[_n] = _at
    _at += _u
    AFTER[_n] = STAGES[_j + 1][0] if _j + 1 < len(STAGES) else None


def t5_bucket(dist):
    exact = NBUCKET // 2
    if dist < exact:
        return dist
    return min(exact + int(math.log(dist / exact) / math.log(MAXDIST / exact) * (NBUCKET - exact)), NBUCKET - 1)


def shape_constants():
    table = np.zeros((NBUCKET + 1, NG, RP), np.float32)
    for x in range(RP):
        for g in range(NG):
            if g == 0:
                d = 255 - x
                ok, j = 0 <= d < NKEY, d
            else:
                d = 127 - x
                step = DIL[g] // DIL[1]
                ok, j = d >= 0 and d % step == 0 and d // step < NKEY, d // step
            table[t5_bucket(j * DIL[g]) if ok else NBUCKET, g, x] = 1.0
    samp = np.zeros((NBUCKET + 1, 6, NG * (P + BW)), np.float32)
    for i in range(DEC_S):
        for r in range(P):
            samp[t5_bucket(P + i - r) if P + i - r < NKEY else NBUCKET, i, r] = 1.0
        for k in range(BW):
            samp[t5_bucket(i - k % DEC_S) if k % DEC_S <= i else NBUCKET, i, NG * P + k] = 1.0
    for g in (1, 2):
        for r in range(P):
            samp[t5_bucket((P - r) * DIL[g]), 3 + g, g * P + r] = 1.0
        samp[t5_bucket(0), 3 + g, NG * P + g * BW:NG * P + (g + 1) * BW] = 1.0
    mask = np.full((4, GC, DEC_S, 2, NG, BW), NEG, np.float32)
    for b in range(4):
        for i in range(DEC_S):
            mask[b, :, i, :, 0, 16 + DEC_S * b:16 + DEC_S * (b + 1)] = 0.0
            mask[b, :, i, :, 1:, 16 + DEC_S * b + i] = 0.0
    inv = np.zeros((4, 16), np.float32)
    for g in range(4):
        for t in range(16):
            inv[g, t] = 1.0 / min(t + 1, 2 ** (g + 1))
    return {"c_table": table, "c_samp": samp, "c_mask": mask.reshape(P, NG * BW), "c_inv": inv.reshape(1, 64),
            "c_ident": np.eye(P, dtype=np.float32)}


def first_turn(i):
    return isinstance(i, int) and i == 0


class Steps:

    def __init__(self, sem):
        self.sem, self.n, self.i, self.start = sem, 0, None, 0

    def add(self, instruction, k=1):
        instruction.then_inc(self.sem, k)
        self.n += k

    def value(self):
        if self.i is None:
            return self.n
        return self.start + self.per * self.i + (self.n - self.start)

    def turn(self, i, per):
        self.i, self.per, self.start = i, per, self.n

    def turns(self, count):
        assert self.n - self.start == self.per, (self.n - self.start, self.per)
        self.n, self.i = self.start + count * self.per, None


def build(nc, A, O):
    ctx = ExitStack()

    def sb(where, name, shape, dt=F32):
        return where.enter_context(nc.sbuf_tensor("t_" + name, shape, dt))

    def sem(name):
        return ctx.enter_context(nc.semaphore(name))

    with ctx:
        x = sb(ctx, "stream", [P, DC, T])
        rw = ExitStack()
        v_c = [sb(rw, f"cached_v{s}", [P, NCK - 1, GW]) for s in range(2)]
        rw.close()
        raw = [sb(ctx, f"w_raw{s}", [P, KH, P]) for s in range(2)]
        whi = [sb(ctx, f"w_hi{s}", [P, KH, P], F32R) for s in range(2)]
        wlo = [sb(ctx, f"w_lo{s}", [P, KH, P], F32R) for s in range(2)]
        ident = sb(ctx, "ident", [P, P])
        invd = sb(ctx, "inv_d", [P, P])
        par = sb(ctx, "params", [P, NPAR])
        eps = sb(ctx, "eps", [P, 1])
        root = sb(ctx, "root", [P, 1])
        rq = ExitStack()
        q_hi = sb(rq, "q_rows_hi", [SAMP, 2 * GW], F32R)
        sel = [sb(rq, "one_hot0", [SAMP, DEC_S, P], F32R)]
        rq.close()
        elem = sb(ctx, "elementwise", [P, 3 * T])
        sg, hf, sq = (elem[:, j * T:(j + 1) * T] for j in range(3))
        tab = sb(ctx, "bias_rows", [HEADS, NG, RP])
        s_bias = sb(ctx, "samp_bias", [P, NG * (P + BW)])
        s_sc = sb(rq, "samp_scores", [P, NG, 256])
        q_lo = sb(rq, "q_rows_lo", [SAMP, 2 * GW], F32R)
        sel += [sb(rq, "one_hot1", [SAMP, DEC_S, P], F32R)]
        rq.close()
        work = sb(ctx, "work", [P, 5 * T])
        accs, accq, mean, var, rstd = (work[:, j * T:(j + 1) * T] for j in range(5))
        s_row = work[:, 768:768 + 2 * SK].rearrange("p (k n) -> p k n", k=2)
        p_b = [work[:, n * NCK * 32:(n + 1) * NCK * 32].rearrange("p (t n) -> p t n", t=NCK) for n in range(2)]
        o_s = work[0:2 * 32, 768:768 + GW]
        s_stat = work[:, 1920:1928]
        s_nk = work[0:SAMP, 1928:1928 + NG * 256]
        p_key = elem[:, 0:NG * 256]
        p_nk = elem[0:SAMP, NG * 256:2 * NG * 256]
        hist = sb(ctx, "history", [P, DC, DEC_B * PAD])
        inv = sb(ctx, "inv_count", [P, 4, 16])

        rx = ExitStack()
        xhi = sb(rx, "x_hi", [P, DC, T], F32R)
        xlo = sb(rx, "x_lo", [P, DC, T], F32R)
        rh = ExitStack()
        hhi = sb(rh, "h_hi", [P, FC, T], F32R)
        hlo = sb(rh, "h_lo", [P, FC, T], F32R)
        rh.close()
        xtok = sb(rh, "x_tok", [P, 5, D])
        ptok = sb(rh, "par_tok", [NPAR, P])
        sttok = sb(rh, "state_tok", [DEC_B * PAD, D])
        oh_t = sb(rh, "onehot_table", [NBUCKET + 1, NG, RP])
        oh_s = sb(rh, "onehot_samp", [NBUCKET + 1, 6, NG * (P + BW)])
        rbx = sb(rh, "bucket_bias", [NBUCKET + 1, NG * HEADS])
        rb_s = sb(rh, "bucket_bias_samp", [NBUCKET + 1, 6, P])
        smask = sb(rh, "samp_mask", [P, NG * BW])
        rh.close()
        phi = sb(rh, "pool_hi", [P, DC, T], F32R)
        plo = sb(rh, "pool_lo", [P, DC, T], F32R)
        ue = [sb(rh, f"u_ext{s}", [P, 16 + SEQ + DEC_B * 20]) for s in range(2)]
        us = [sb(rh, f"u_sum{s}", [P, 16 + SEQ + DEC_B * 20]) for s in range(2)]
        utail = sb(rh, "u_tail", [P, DC, PAD + SAMP])
        utok = sb(rh, "u_tok", [PAD + SAMP, D])
        zhi = sb(rh, "z_hi", [P, DC, T], F32R)
        zlo = sb(rh, "z_lo", [P, DC, T], F32R)
        rh.close()
        qt = sb(rh, "q_feat", [P, NG * GC, T])
        hq = ExitStack()
        yhi = sb(hq, "kv_in_hi", [P, DC, T], F32R)
        ylo = sb(hq, "kv_in_lo", [P, DC, T], F32R)
        cached_odd = sb(hq, "cached1", [P, NCK, GW])
        kvt = [sb(hq, f"kv_feat{s}", [P, T]) for s in range(2)]
        kvp = [sb(hq, f"kv_tok{s}", [P, QB, P]) for s in range(2)]
        q_bd = sb(hq, "q_blocks", [P, NG * GC, 2 * SAMP])
        q_b = [sb(hq, f"q_blocks_b{s}", [P, GC, 2 * DEC_S]) for s in range(2)]
        kn_t = sb(hq, "k_new_feat", [P, NG * GC, SAMP])
        k_t = sb(hq, "k_turned", [P, GW])
        hq.close()
        ot = sb(hq, "o_feat", [P, GC, T])
        q_r = sb(hq, "q_tile", [P, NG * GC, P])
        k_r = sb(hq, "k_tile", [P, 2 * GC, P])
        v_p = [sb(hq, "v_prompt0", [P, QB, GW])]
        b12 = sb(hq, "bias12", [P, HEADS, 256])
        sb(hq, "not_used", [P, 3 * P])
        kt12 = sb(hq, "k_feat12", [P, 2 * GC, SEQ])
        v_p += [sb(hq, f"v_prompt{g}", [P, QB, GW]) for g in (1, 2)]
        hq.close()
        rh.close()
        ohi = sb(rh, "o_hi", [P, GC, T], F32R)
        olo = sb(rh, "o_lo", [P, GC, T], F32R)
        rh.close()
        ytok = sb(rh, "y_tok", [P, QB + 1, D])
        rh.close()
        rx.close()
        cached = [sb(rx, "cached0", [P, NCK, GW]), cached_odd]
        kv_n = sb(rx, "kv_new", [SAMP, NG * 2 * GW])
        kq = [sb(rx, f"k_times_q{s}", [P, GW]) for s in range(2)]
        rx.close()
        b0 = sb(rx, "bias0", [P, HEADS, 256])
        kt0 = sb(rx, "k_feat0", [P, GC, SEQ])
        s_p = [sb(rx, f"s_prompt{s}", [P, 512]) for s in range(2)]
        p_p = [sb(rx, f"p_prompt{s}", [P, 512]) for s in range(2)]
        pt_p = [sb(rx, f"pt_prompt{s}", [P, 512]) for s in range(2)]
        o_n = sb(rx, "o_tok", [P, GW])
        a_stat = sb(rx, "a_stats", [P, 4, QB, HEADS])
        v_c0 = [hist[:].rearrange("p c n -> p (c n)")[:, 0:GW], sb(rx, "cached_v_g0", [P, GW])]
        rx.close()

        ps = [ctx.enter_context(nc.psum_tensor(f"pair{j}", [P, 2, 512], F32)) for j in range(4)]
        pa, pb, pc, pd = ps

        def halves(t):
            return t[:, :, 0:HALF]

        def split(t):
            return t.rearrange("p (a n) -> p a n", a=2)

        kt_d = nc.dram_tensor("scratch_kt", [NG * GC, P, SEQ], F32)
        kv0_d = nc.dram_tensor("scratch_kv0", [SEQ, 2 * GW], F32)
        xs_d = nc.dram_tensor("scratch_x_parts", [2, P, DC * T], F32)
        tab_d = nc.dram_tensor("scratch_bias_rows", [NG, HEADS, P, RP], F32)

        raw_in = [sem(f"raw_in{s}") for s in range(2)]
        hi_made = [sem(f"hi_made{s}") for s in range(2)]
        lo_made = [sem(f"lo_made{s}") for s in range(2)]
        w_used = [sem(f"w_used{s}") for s in range(2)]
        consts_in = sem("consts_in")
        xtok_in = sem("xtok_in")
        ptok_in = sem("ptok_in")
        consts_made = sem("consts_made")
        par_t = sem("par_transposed")
        par_ok = sem("par_ready")
        in_t = sem("in_transposed")
        in_evac = sem("in_evacuated")
        x_ready = sem("x_parts_ready")
        act_step = sem("act_step")
        dve_step = sem("dve_step")
        pool_step = sem("pool_step")
        res_made = sem("residual_made")
        sq_made = sem("squares_made")
        acc_made = sem("sums_made")
        acc_zero = sem("sums_zero")
        stats = sem("norm_sums")
        ln_mean = sem("norm_mean")
        ln_sq = sem("norm_mean_squared")
        ln_var = sem("norm_var")
        ln_std = sem("norm_std")
        ln_sub = sem("norm_centred")
        ln_t = sem("norm_scaled")
        ln_x = sem("norm_out")
        gate_silu = sem("gate_silu")
        h_made = sem("hidden_made")
        h_hi_made = sem("hidden_hi_made")
        h_lo_made = sem("hidden_lo_made")
        u_evac = sem("u_evacuated")
        st_in = sem("state_in")
        st_t = sem("state_transposed")
        st_evac = sem("state_evacuated")
        pooled = sem("pooled")
        utail_t = sem("u_tail_transposed")
        utok_ok = sem("u_tok_ready")
        z_scaled = sem("z_scaled")
        z_done = sem("z_products")
        z_ready = sem("z_parts_ready")
        kv_evac = [sem(f"kv_evacuated{s}") for s in range(2)]
        kv_t = [sem(f"kv_transposed{s}") for s in range(2)]
        kv_tok = [sem(f"kv_tok_ready{s}") for s in range(2)]
        kt_out = [sem(f"kt_stored{s}") for s in range(2)]
        kv_out = [sem(f"kv_stored{s}") for s in range(2)]
        utok_out = sem("u_tok_stored")
        tab_in = sem("tab_in")
        rb_copied = sem("rb_copied")
        tab_mm = sem("tab_mm")
        tab_evac = sem("tab_evac")
        sb_mm = sem("sb_mm")
        sb_evac = sem("sb_evac")
        sbn_ok = sem("samp_bias_new")
        tab_out = sem("tab_out")
        xs_out = sem("xs_out")
        xs_in = sem("xs_in")
        q_evac = sem("q_evac")
        kvn_out = sem("kv_new_stored")
        cached_in = [sem(f"cached_in{s}") for s in range(2)]
        value_in = [sem(f"value_in{s}") for s in range(2)]
        pb_zero = sem("samp_probs_zero")
        os_t = sem("samp_outputs_turned")
        qbd_ok = sem("q_blocks_ready")
        qb_ok = sem("q_blocks_b_ready")
        kc_t = sem("cached_keys_turned")
        kc_ok = sem("cached_keys_evacuated")
        kc_used = sem("cached_keys_used")
        qrow_t = sem("q_rows_turned")
        qhi_ok = sem("q_rows_hi")
        qlo_ok = sem("q_rows_lo")
        q_cast = sem("q_on_all_partitions")
        kq_used = sem("cached_keys_summed")
        kq_made = sem("cached_keys_times_q")
        snk_mm = sem("samp_new_scores")
        snk_ok = sem("samp_new_scores_evacuated")
        srow_t = sem("samp_rows_turned")
        srow_ok = sem("samp_rows_evacuated")
        smax_ok = sem("samp_max")
        sexp_ok = sem("samp_exp")
        snorm_ok = sem("samp_probs")
        pkey_t = sem("samp_probs_turned")
        pkey_ok = sem("samp_probs_evacuated")
        pb_ok = sem("samp_probs_b")
        snv_done = sem("samp_new_values")
        snv_ok = sem("samp_new_values_evacuated")
        sv_done = sem("samp_values")
        sv_evac = sem("samp_values_evacuated")
        ots_ok = sem("samp_outputs_added")
        kt_in = sem("kt_in")
        v_in = sem("v_in")
        b12_in = sem("b12_in")
        b0_pad = sem("b0_pad")
        qk_ok = sem("qk_ok")
        s_done = sem("s_done")
        s_ok = sem("s_ok")
        p_ok = sem("p_ok")
        pt_done = sem("pt_done")
        pt_ok = sem("pt_ok")
        pv_done = sem("pv_done")
        on_ok = sem("on_ok")
        on_t = sem("on_t")
        ot_ok = sem("ot_ok")
        o_ready = sem("o_ready")
        ohi_ok = sem("ohi_ok")
        y_t = sem("y_t")
        y_ok = [sem(f"y_ok{s}") for s in range(2)]
        y_out = sem("y_out")
        b0_in = [sem(f"b0_in{h}") for h in range(2)]
        done = sem("outputs_done")

        def rows(w):
            return w.rearrange("(k p) n -> p k n", p=P)

        w13 = [rows(A["ffn_w13"][f // 2, f % 2]) for f in range(4)]
        w2 = [rows(A["ffn_w2"][f // 2, f % 2]) for f in range(4)]
        w_pin, w_pout = rows(A["pool_w_in"][0]), rows(A["pool_w_out"][0])
        w_grp = A["pool_w_grp"][0].rearrange("g (k p) n -> p (g k) n", p=P)
        w_kv, w_q, w_o = rows(A["attn_w_kv"]), rows(A["attn_w_q"][0]), rows(A["attn_w_o"][0])

        def unit_source(stage, s, i):
            if stage[:2] == "up":
                return w13[int(stage[2])][:, :, bass.ds(FF * s + i * P, P)]
            if stage[:4] == "down":
                return w2[int(stage[4])][:, KH * s:KH * (s + 1), bass.ds(i * P, P)]
            if stage == "pgrp":
                return w_grp[:, :, s * P:(s + 1) * P]
            w = {"pin": w_pin, "pout": w_pout, "kv": w_kv, "q": w_q, "wo": w_o}[stage]
            return w[:, :, bass.ds(2 * i * P + s * P, P)]

        block = ctx.enter_context(nc.Block())

        @block.sync
        def _(sp):
            def load(dst, src, s, k=16):
                sp.dma_start(dst, src).then_inc(s, k)

            load(ident[:], A["c_ident"], consts_in)
            load(inv[:].rearrange("p g t -> p (g t)"), A["c_inv"].partition_broadcast(P).rearrange("q a n -> q (a n)"),
                 consts_in)
            load(xtok[:, 0:4, :], A["x_prompt"][0].rearrange("(j p) d -> p j d", p=P), xtok_in)
            load(xtok[0:SAMP, 4, :], A["x_sample"].rearrange("b s d -> (b s) d"), xtok_in)
            load(ptok[PG:PB, :], A["ln_g"].rearrange("l s (c p) -> (l s c) p", p=P), ptok_in)
            load(ptok[PB:PS, :], A["ln_b"].rearrange("l s (c p) -> (l s c) p", p=P), ptok_in)
            load(ptok[PS:NPAR, :], A["pool_scale"][0].rearrange("(c p) -> c p", p=P), ptok_in)

            load(sttok[:], A["state_pool"][0].rearrange("b t d -> (b t) d"), st_in)
            load(oh_t[:], A["c_table"], tab_in)
            load(oh_s[:], A["c_samp"], tab_in)
            load(smask[:], A["c_mask"], tab_in)
            sp.wait_ge(rb_copied, 1)
            load(rbx[0:NBUCKET, :], A["rel_bias"], tab_in)

            def stream(stage, i):
                for s in range(2):
                    if not (stage == "up0" and first_turn(i)):
                        sp.wait_ge(lo_made[s], FIRST[stage] + i)
                    sp.dma_start(raw[s][:, 0:KT[stage], :], unit_source(stage, s, i)).then_inc(raw_in[s], 16)

            def stream_all(stage, start=0):
                with sp.Fori(start, UNITS[stage]) as i:
                    stream(stage, i)

            stream("up0", 0)
            stream("up0", 1)
            stream("up0", 2)
            sp.wait_ge(tab_evac, NG)
            for g in range(NG):
                sp.dma_start(tab_d.ap()[g],
                             tab[:, g, :].unsqueeze(1).to_broadcast([HEADS, P, RP])).then_inc(tab_out, 16)
                stream("up0", 3 + g)
            sp.dma_start(O["pool_s"][0, :, 0:PAD - DEC_S, :], A["state_pool"][0, :, DEC_S:PAD, :]).then_inc(done, 16)
            stream_all("up0", 3 + NG)
            for stage in ("down0", "pin", "pgrp", "pout", "up1", "down1"):
                stream_all(stage)
            stream("up2", 0)
            stream("up2", 1)
            sp.wait_ge(x_ready, 4 * DC)
            for n, part in enumerate((xhi, xlo)):
                sp.dma_start(xs_d.ap()[n], part[:].rearrange("p c t -> p (c t)").bitcast(F32)).then_inc(xs_out, 16)
            stream_all("up2", 2)
            stream_all("down2")
            stream("q", 0)
            sp.wait_ge(res_made, DC * RES.index("down2") + DC)
            sp.wait_ge(xs_out, 32)
            for n, part in enumerate((yhi, ylo)):
                sp.dma_start(part[:].rearrange("p c t -> p (c t)").bitcast(F32), xs_d.ap()[n]).then_inc(xs_in, 16)
            stream_all("q", 1)

            def kt_store(i, s):
                g, j = i // 4, i % 4
                if j < 2:
                    sp.wait_ge(kv_evac[s], i + 1)
                    sp.dma_start(kt_d.ap()[g * GC + 2 * j + s], kvt[s][:, 0:SEQ]).then_inc(kt_out[s], 16)

            def kv_store(i, s):
                g, col = i // 4, ((i % 4) * 2 + s) * P
                sp.wait_ge(kv_tok[s], 2 * i + 2)
                if g == 0:
                    sp.dma_start(kv0_d.ap().rearrange("(j p) n -> p j n", p=P)[:, :, col:col + P],
                                 kvp[s][:]).then_inc(kv_out[s], 16)
                    sp.dma_start(O["kv_p0"].rearrange("b w k h d -> (b w) (k h d)")[:, col:col + P],
                                 kvp[s][:, QB - 1, :]).then_inc(kv_out[s], 16)
                else:
                    view = O[f"kv_p{g}"].rearrange("b (j p) k h d -> p (b j) (k h d)", p=P)
                    for h in range(2):
                        sp.dma_start(view[:, 2 * h:2 * h + 2, col:col + P],
                                     kvp[s][:, 2 * h:2 * h + 2, :]).then_inc(kv_out[s], 16)

            def bias0(r, h, first=False):
                if not first:
                    sp.wait_ge(s_ok, HEADS * (r - 1) + 4 * h + 4)
                for c in range(QB):
                    k0 = P if c == 0 else 0
                    sp.dma_start(b0[32 * c:32 * c + 32, 4 * h:4 * h + 4, k0:256],
                                 bass.AP(tensor=tab_d, offset=4 * h * P * RP + P - 1 - r + k0,
                                         ap=[[RP - 4, 32], [P * RP, 4], [1, 256 - k0]])).then_inc(b0_in[h], 16)

            for i in range(UNITS["kv"]):
                stream("kv", i)
                if i >= 1:
                    kt_store(i - 1, 0)
                    if i >= 2:
                        kv_store(i - 2, 1)
                    kt_store(i - 1, 1)
                    kv_store(i - 1, 0)
            for s in range(2):
                sp.wait_ge(kt_out[s], 16 * UNITS["kv"] // 2)
            sp.wait_ge(kq_made, (NCK - 1) * DEC_B)
            load(kt12[:], kt_d.ap()[GC:NG * GC].rearrange("c p t -> p c t"), kt_in)
            load(kt0[:], kt_d.ap()[0:GC].rearrange("c p t -> p c t"), kt_in)
            sp.wait_ge(tab_out, 16 * NG)
            sp.wait_ge(b0_pad, 1)
            bias0(0, 0, True)
            bias0(0, 1, True)
            kv_store(UNITS["kv"] - 2, 1)
            kv_store(UNITS["kv"] - 1, 0)
            kv_store(UNITS["kv"] - 1, 1)
            for g in range(NG):
                sp.dma_start(O[f"kv_s{g}"].rearrange("b t k h d -> (b t) (k h d)"),
                             kv_n[:, g * 2 * GW:(g + 1) * 2 * GW]).then_inc(kvn_out, 16)

            for s in range(2):
                sp.wait_ge(w_used[s], FIRST["wo"])
            for s in range(2):
                sp.wait_ge(kv_out[s], 32 * UNITS["kv"])
            sp.wait_ge(snk_mm, 1)
            load(v_p[0][:], kv0_d.ap().rearrange("(c p) n -> p c n", p=P)[:, :, GW:2 * GW], v_in)
            for g in (1, 2):
                load(v_p[g][:], O[f"kv_p{g}"].rearrange("b (p r) k h d -> p (b r) k (h d)", r=QB)[:, :, 1, :], v_in)
            for g in (1, 2):
                load(b12[:, :, (g - 1) * P:g * P],
                     bass.AP(tensor=tab_d, offset=g * HEADS * P * RP + P - 1, ap=[[RP - 1, P], [P * RP, HEADS], [1, P]]),
                     b12_in)

            for r in range(1, QB):
                bias0(r, 0)
                bias0(r, 1)
            sp.wait_ge(sv_done, DEC_B)
            stream_all("wo")
            stream_all("up3")
            stream_all("down3")

            out_p = O["y_p"].rearrange("b (j p) d -> p (b j) d", p=P)
            for j in range(QB):
                sp.wait_ge(y_ok[0], j + 1)
                sp.wait_ge(y_ok[1], j + 1)
                sp.dma_start(out_p[:, j, :], ytok[:, j, :]).then_inc(y_out, 16)
            sp.wait_ge(y_ok[0], QB + 1)
            sp.wait_ge(y_ok[1], QB + 1)
            sp.dma_start(O["y_s"].rearrange("b t d -> (b t) d"), ytok[0:SAMP, QB, :]).then_inc(y_out, 16)
            sp.wait_ge(y_out, 16 * (QB + 1))
            sp.wait_ge(done, 16)
            sp.wait_ge(utok_out, 32)
            for s in range(2):
                sp.wait_ge(kv_out[s], 32 * UNITS["kv"])
                sp.wait_ge(kt_out[s], 16 * UNITS["kv"] // 2)
            sp.wait_ge(kvn_out, 16 * NG)

        @block.tensor
        def _(pe):
            def products(out, s, kt, hi, lo, first=True, last=True, each=None, at=0):
                for k in range(kt):
                    if each:
                        each(k)
                    for n, (w, a) in enumerate(((whi[s], hi), (whi[s], lo), (wlo[s], hi))):
                        for j in range(2):
                            m = nc.tensor.matmul(out[:, j, 0:HALF], w[:, at + k, :], a(k)[:, j * HALF:(j + 1) * HALF],
                                                 start=first and k == 0 and n == 0,
                                                 stop=last and k == kt - 1 and n == 2)
                return m

            def stream_x(k):
                return xhi[:, k, :]

            def stream_xl(k):
                return xlo[:, k, :]

            def first_units(stage, count):
                for s in range(2):
                    pe.wait_ge(lo_made[s], FIRST[stage] + 1)
                for k in range(DC):
                    pe.wait_ge(x_ready, count - DC + k + 1)
                    for s in range(2):
                        for n, (w, a) in enumerate(((whi[s], xhi), (whi[s], xlo), (wlo[s], xhi))):
                            for j in range(2):
                                m = nc.tensor.matmul(ps[s][:, j, 0:HALF], w[:, k, :],
                                                     a[:, k, j * HALF:(j + 1) * HALF],
                                                     start=k == 0 and n == 0, stop=k == DC - 1 and n == 2)
                        if k == DC - 1:
                            m.then_inc(w_used[s], 1)

            pe.wait_ge(consts_in, 32)
            pe.wait_ge(xtok_in, 32)
            for c in range(DC):
                if c >= 2:
                    pe.wait_ge(in_evac, c - 1)
                for j in range(QB):
                    nc.tensor.transpose(ps[c % 2][:, 0, j * P:(j + 1) * P], xtok[:, j, c * P:(c + 1) * P], ident[:])
                nc.tensor.transpose(ps[c % 2][:, 1, 0:SAMP], xtok[0:SAMP, 4, c * P:(c + 1) * P],
                                    ident[0:SAMP, 0:SAMP]).then_inc(in_t, 1)

            pe.wait_ge(ptok_in, 48)
            nc.tensor.transpose(pc[:, 0, 0:NPAR], ptok[:], ident[0:NPAR, 0:NPAR]).then_inc(par_t, 1)

            def up(stage, ready):
                f, base = int(stage[2]), FIRST[stage]

                def turn(i):
                    pe.wait_ge(lo_made[0], base + i + 1)
                    pe.wait_ge(gate_silu, FC * f + i)
                    products(pa, 0, DC, stream_x, stream_xl).then_inc(w_used[0], 1)
                    pe.wait_ge(lo_made[1], base + i + 1)
                    pe.wait_ge(h_made, FC * f + i)
                    products(pb, 1, DC, stream_x, stream_xl).then_inc(w_used[1], 1)

                first_units(stage, ready)
                with pe.Fori(1, FC) as i:
                    turn(i)

            def down(stage):
                f, base = int(stage[4]), FIRST[stage]

                def chunk(i, out, first=False):
                    for s in range(2):
                        pe.wait_ge(lo_made[s], base + i + 1)
                        if first:
                            pe.wait_ge(h_lo_made, FC * f + (KH if s == 0 else FC))
                        elif s == 0:
                            pe.wait_ge(res_made, DC * RES.index(stage) + i - 1)
                        products(out, s, KH, lambda k: hhi[:, KH * s + k, :], lambda k: hlo[:, KH * s + k, :],
                                 first=s == 0, last=s == 1).then_inc(w_used[s], 1)

                chunk(0, pa, True)
                chunk(1, pb, True)
                with pe.Fori(2, DC, 2) as i:
                    chunk(i, pa)
                    chunk(i + 1, pb)

            def linear(stage, hi, lo, evac, ready=None, each=None):
                base = FIRST[stage]

                def turn(i, first):
                    for s in range(2):
                        pe.wait_ge(lo_made[s], base + i + 1)
                        if not first:
                            evac(s, i)
                        products(ps[s], s, KT[stage], hi, lo, each=each if first and s == 0 else None) \
                            .then_inc(w_used[s], 1)

                if ready:
                    first_units(stage, ready)
                else:
                    turn(0, True)
                with pe.Fori(1, UNITS[stage]) as i:
                    turn(i, False)

            def norm(stage):
                n = RES.index(stage)

                def add(out, a, first):
                    for j in range(2):
                        m = nc.tensor.matmul(out[:, j, 0:HALF], invd[:], a[:, j * HALF:(j + 1) * HALF],
                                             start=first, stop=not first)
                    return m

                pe.wait_ge(acc_made, ACCS * (n + 1))
                add(pc, accs, True)
                add(pd, accq, True)
                pe.wait_ge(res_made, DC * (n + 1))
                add(pc, x[:, DC - 1, :], False).then_inc(stats, 1)
                pe.wait_ge(sq_made, DC * (n + 1))
                add(pd, sq, False).then_inc(stats, 1)

            pe.wait_ge(st_in, 16)
            for c in range(DC):
                n = DEC_B * PAD
                m = nc.tensor.transpose(pd[:, c // 4, (c % 4) * n:(c % 4 + 1) * n], sttok[:, c * P:(c + 1) * P],
                                        ident[0:n, 0:n])
            m.then_inc(st_t, 1)
            pe.wait_ge(tab_in, 64)
            pe.wait_ge(rb_copied, 4)
            pe.wait_ge(par_ok, 1)
            pe.wait_ge(in_evac, DC)
            for g, out in enumerate((pa[:, 0, :], pa[:, 1, :], pb[:, 0, :])):
                m = nc.tensor.matmul(out[0:HEADS, 0:RP], rbx[:, g * HEADS:(g + 1) * HEADS], oh_t[:, g, :],
                                     start=True, stop=True)
            m.then_inc(tab_mm, 1)
            for v in range(6):
                for half, cols in enumerate((slice(0, NG * P), slice(NG * P, NG * (P + BW)))):
                    m = nc.tensor.matmul(pc[:, half, 0:cols.stop - cols.start], rb_s[:, v, :], oh_s[:, v, cols],
                                         start=v == 0, stop=v == 5)
            m.then_inc(sb_mm, 1)
            pe.wait_ge(tab_evac, NG)
            pe.wait_ge(consts_made, 2)
            pe.wait_ge(in_evac, DC)
            ready = DC
            up("up0", ready)
            down("down0")
            norm("down0")
            ready += DC
            linear("pin", stream_x, stream_xl, lambda s, i: pe.wait_ge(u_evac, 2 * i - 1 + s), ready)
            pe.wait_ge(u_evac, DC)
            for c in range(DC):
                m = nc.tensor.transpose(pc[0:PAD + SAMP, c // 4, (c % 4) * P:(c % 4 + 1) * P], utail[:, c, :], ident[:])
            m.then_inc(utail_t, 1)
            for g in range(4):
                for s in range(2):
                    if g == 0:
                        pe.wait_ge(lo_made[s], FIRST["pgrp"] + 1)
                    pe.wait_ge(pooled, 2 * g + 2)
                    if g >= 1:
                        pe.wait_ge(z_scaled, 2 * g - 1 + s)
                    m = products(ps[s], s, 2, lambda k: phi[:, 2 * g + k, :], lambda k: plo[:, 2 * g + k, :], at=2 * g)
                    m.then_inc(w_used[s] if g == 3 else z_done, 1)
            pe.wait_ge(z_ready, DC)
            linear("pout", lambda k: zhi[:, k, :], lambda k: zlo[:, k, :],
                   lambda s, i: pe.wait_ge(res_made, DC * RES.index("pout") + 2 * i - 1 + s))
            norm("pout")
            ready += DC
            up("up1", ready)
            down("down1")
            norm("down1")
            ready += DC

            up("up2", ready)
            down("down2")
            norm("down2")
            ready += DC
            linear("q", stream_x, stream_xl, lambda s, i: pe.wait_ge(q_evac, 2 * i - 1 + s), ready)
            def kv_units(s, i, first=False, each=None):
                pe.wait_ge(lo_made[s], FIRST["kv"] + i + 1)
                if not first:
                    pe.wait_ge(kv_evac[s], i)
                products(ps[s], s, DC, lambda k: yhi[:, k, :], lambda k: ylo[:, k, :], each=each) \
                    .then_inc(w_used[s], 1)

            def kv_transposes(s, i, first=False):
                pe.wait_ge(kv_evac[s], i + 1)
                if not first:
                    pe.wait_ge(kv_tok[s], 2 * i)
                for j in range(QB):
                    nc.tensor.transpose(ps[2 + s][:, 0, j * P:(j + 1) * P], kvt[s][:, j * P:(j + 1) * P], ident[:])
                nc.tensor.matmul(pc[SAMP * s:SAMP * (s + 1), 1, 0:P], kvt[s][:, SEQ:T], ident[:], start=True,
                                 stop=True).then_inc(kv_t[s], 1)

            def turn_keys(b, s):
                pe.wait_ge(cached_in[s], 24 * (b - s) + 48)
                if not first_turn(b):
                    pe.wait_ge(kq_made, (NCK - 1) * b)
                for c in range(GC):
                    m = nc.tensor.transpose(pd[:, 1, c * P:(c + 1) * P], cached[s][:, 0, c * P:(c + 1) * P], ident[:])
                m.then_inc(kc_t, 1)

            def key_scores(b, s):
                pe.wait_ge(qb_ok, b + 1)
                pe.wait_ge(kc_ok, b + 1)
                for c in range(GC):
                    at = HALF + c * 2 * DEC_S
                    m = nc.tensor.matmul(pa[:, 1, at:at + 2 * DEC_S], k_t[:, c * P:(c + 1) * P], q_b[s][:, c, :],
                                         start=False, stop=False,
                                         skip_group_check=True)
                m.then_inc(kc_used, 1)

            def cast_queries(b, s, t):
                g, i = (t - 1) // 4, (t - 1) % 4
                if t == 1:
                    pe.wait_ge(qb_ok, b + 1)
                    pe.wait_ge(kc_ok, b + 1)
                else:
                    pe.wait_ge(kq_made, (NCK - 1) * b + t - 1)
                for n, part in enumerate((q_hi, q_lo)):
                    m = nc.tensor.matmul(pd[:, 1, :], sel[s][:, i, :], part[:, g * GW:(g + 1) * GW], start=n == 0,
                                         stop=n == 1)
                m.then_inc(q_cast, 1)

            def kv_turn(i, b=None, s=0):
                def each0(k):
                    if k == 0:
                        turn_keys(b, s)
                    if k == 2:
                        key_scores(b, s)
                    if k % 2:
                        cast_queries(b, s, (k + 1) // 2)

                def each1(k):
                    if k % 2:
                        cast_queries(b, s, (k + 1) // 2 + 4)

                kv_units(0, i, each=None if b is None else each0)
                kv_transposes(1, i - 1)
                kv_units(1, i, each=None if b is None else each1)
                kv_transposes(0, i)

            pe.wait_ge(q_evac, NG * GC)
            for g in range(2):
                for c in range(GC):
                    m = nc.tensor.transpose(pc[0:SAMP, g, c * P:(c + 1) * P], qt[:, (g + 1) * GC + c, SEQ:T], ident[:])
            m.then_inc(qrow_t, 1)
            pe.wait_ge(xs_in, 32)
            kv_units(0, 0, True)
            kv_units(1, 0, True)
            pe.wait_ge(qlo_ok, 1)
            kv_transposes(0, 0, True)
            kv_units(0, 1)
            kv_transposes(1, 0, True)
            kv_units(1, 1)
            kv_transposes(0, 1)
            kv_turn(2, 0, 0)
            kv_turn(3, 1, 1)
            with pe.Fori(1, DEC_B // 2) as n:
                kv_turn(2 * n + 2, 2 * n, 0)
                kv_turn(2 * n + 3, 2 * n + 1, 1)
            kv_turn(10)
            kv_turn(11)
            kv_transposes(1, UNITS["kv"] - 1)

            def scores(r, h, first):
                c, lo = h // 2, DH * (h % 2)
                out = pa[:, h % 2, :]
                hd = slice(lo, lo + DH)
                if h % 2 == 0:
                    pe.wait_ge(qk_ok, GC * r + c + 1)
                if h >= 2 or not first:
                    pe.wait_ge(s_ok, HEADS * r + h - 1)
                for g in (1, 2):
                    nc.tensor.matmul(out[:, (g + 1) * P:(g + 2) * P], q_r[hd, g * GC + c, :],
                                     k_r[hd, (g - 1) * GC + c, :], start=True, stop=True)
                for b in range(QB):
                    q = q_r[hd, c, 32 * b:32 * b + 32]
                    rows_ = slice(32 * b, 32 * b + 32)
                    if b == 0:
                        for half in range(2):
                            nc.tensor.matmul(out[rows_, half * P:(half + 1) * P], q, kt0[hd, c, 0:P],
                                             start=True, stop=True)
                    else:
                        m = nc.tensor.matmul(out[rows_, 0:256], q, kt0[hd, c, (b - 1) * P:(b + 1) * P],
                                             start=True, stop=True)
                m.then_inc(s_done, 1)

            pe.wait_ge(kv_evac[1], UNITS["kv"])
            pe.wait_ge(qbd_ok, 3)
            for g in range(NG):
                for c in range(GC):
                    row = pb[0:SAMP, g // 2, (g % 2) * 256:(g % 2 + 1) * 256]
                    m = nc.tensor.matmul(row.rearrange("p (b c n) -> p b c n", b=DEC_B, c=GC)[:, :, c, :],
                                         kn_t[:, g * GC + c, :],
                                         q_bd[:, g * GC + c, :].rearrange("p (b n) -> p b n", b=DEC_B),
                                         start=True, stop=True)
            m.then_inc(snk_mm, 1)
            pe.wait_ge(kq_used, (NCK - 1) * DEC_B)
            pe.wait_ge(kv_evac[0], UNITS["kv"])
            for k in range(2):
                for g in range(NG):
                    nc.tensor.transpose(pa[:, k, g * P:(g + 1) * P], s_sc[:, g, k * P:(k + 1) * P], ident[:])
            pe.wait_ge(snk_ok, 2)
            for k in range(2):
                for g in range(NG):
                    at = NG * P + g * SAMP
                    m = nc.tensor.transpose(pa[:, k, at:at + SAMP], s_nk[:, g * 256 + k * P:g * 256 + (k + 1) * P],
                                            ident[0:SAMP, 0:SAMP])
            m.then_inc(srow_t, 1)
            pe.wait_ge(kt_in, 32)
            pe.wait_ge(srow_ok, 1)
            scores(0, 0, True)
            scores(0, 1, True)
            pe.wait_ge(snorm_ok, 1)
            for s in range(2):
                pe.wait_ge(kv_tok[s], 2 * UNITS["kv"])
            for g in range(NG):
                for k in range(2):
                    at = (g % 2) * 256 + k * P
                    nc.tensor.transpose(pb[:, g // 2, at:at + P], s_row[:, k, g * P:(g + 1) * P], ident[:])
                    m = nc.tensor.transpose(pd[0:SAMP, g // 2, at:at + P],
                                            s_row[:, k, NG * P + g * SAMP:NG * P + (g + 1) * SAMP], ident[:])
            m.then_inc(pkey_t, 1)

            pe.wait_ge(pkey_ok, 4)
            for c in range(GC):
                for g in range(NG):
                    at = g * 2 * GW + GW + c * P
                    row = p_nk[:, g * 256:(g + 1) * 256].rearrange("p (b c n) -> p b c n", b=DEC_B, c=GC)
                    m = nc.tensor.matmul(pc[:, 1, c * 64:(c + 1) * 64], kv_n[:, at:at + P], row[:, :, c, :],
                                         start=g == 0, stop=g == NG - 1)
            m.then_inc(snv_done, 1)

            def sample_values(r, s, tiles):
                for t in tiles:
                    if t == 0:
                        pe.wait_ge(value_in[s], 48 * r + 48)
                        pe.wait_ge(pb_ok, 2 * r + s + 1)
                        if s == 0 and not first_turn(r):
                            pe.wait_ge(sv_evac, r)
                    m = nc.tensor.matmul(pd[32 * s:32 * s + 32, 0, :], p_b[s][:, t, :],
                                         v_c0[s][:] if t == 0 else v_c[s][:, t - 1, :],
                                         start=t == 0, stop=t == NCK - 1)
                    if t == NCK - 1:
                        m.then_inc(sv_done, 1)

            def sample_outputs(r):
                pe.wait_ge(sv_evac, r + 1)
                if not first_turn(r):
                    pe.wait_ge(ots_ok, r)
                for c in range(GC):
                    own = ident[0:64, 0:64].rearrange("p (b c n) -> p b c n", b=2, c=GC)[:, :, c, :]
                    m = nc.tensor.matmul(pd[:, 1, c * 16:(c + 1) * 16], o_s[:, c * P:(c + 1) * P], own,
                                         start=True, stop=True)
                m.then_inc(os_t, 1)

            def turn_probs(r, h, first):
                pe.wait_ge(p_ok, HEADS * r + h + 1)
                if not (first and h < 2):
                    pe.wait_ge(pt_ok, HEADS * r + h - 1)
                for k in range(4):
                    m = nc.tensor.transpose(pb[:, h % 2, k * P:(k + 1) * P], p_p[h % 2][:, k * P:(k + 1) * P], ident[:])
                m.then_inc(pt_done, 1)

            def values(r, h, first):
                pe.wait_ge(pt_ok, HEADS * r + h + 1)
                if h == 0 and not first:
                    pe.wait_ge(on_ok, r)
                out = pc[:, 0, h * DH:(h + 1) * DH]
                pt, cols = pt_p[h % 2], slice(h * DH, (h + 1) * DH)
                for g in (1, 2):
                    nc.tensor.matmul(out, pt[:, (g + 1) * P:(g + 2) * P], v_p[g][:, r, cols], start=g == 1, stop=False,
                                     skip_group_check=True)
                for b in range(QB):
                    rows_ = slice(32 * b, 32 * b + 32)
                    if b:
                        nc.tensor.matmul(out[rows_, :], pt[:, rows_], v_p[0][:, b - 1, cols],
                                         start=False, stop=False, skip_group_check=True)
                    m = nc.tensor.matmul(out[rows_, :], pt[:, P + 32 * b:P + 32 * b + 32], v_p[0][:, b, cols],
                                         start=False, stop=b == QB - 1, skip_group_check=True)
                m.then_inc(pv_done, 1)

            def tile(r, first, last):
                lag = 2 if first else 0
                for h in range(HEADS):
                    turn_probs(r, h, first)
                    if h + 2 < HEADS:
                        scores(r, h + 2, first)
                    elif not last:
                        scores(r + 1, h + 2 - HEADS, False)
                    if first and h == 0:
                        pe.wait_ge(v_in, 16 * NG)
                    if lag <= h < lag + 6:
                        n = h - lag
                        sample_values(r, n // 3, range(n % 3 * 3, n % 3 * 3 + 3))
                    values(r, h, first)
                sample_outputs(r)
                pe.wait_ge(on_ok, r + 1)
                if not first:
                    pe.wait_ge(ot_ok, r)
                for c in range(GC):
                    m = nc.tensor.transpose(pc[:, 1, c * P:(c + 1) * P], o_n[:, c * P:(c + 1) * P], ident[:])
                m.then_inc(on_t, 1)

            pe.wait_ge(snv_ok, 1)
            tile(0, True, False)
            with pe.Fori(1, QB - 1) as r:
                tile(r, False, False)
            tile(QB - 1, False, True)
            linear("wo", lambda k: ohi[:, k, :], lambda k: olo[:, k, :],
                   lambda s, i: pe.wait_ge(res_made, DC * RES.index("wo") + 2 * i - 1 + s),
                   each=lambda k: pe.wait_ge(o_ready, k + 1))
            norm("wo")
            ready += DC
            up("up3", ready)
            down("down3")
            norm("down3")
            for c in range(DC):
                pe.wait_ge(ln_x, DC * RES.index("down3") + c + 1)
                for j in range(QB):
                    m = nc.tensor.transpose(ps[j][:, c // 4, (c % 4) * P:(c % 4 + 1) * P], x[:, c, j * P:(j + 1) * P],
                                            ident[:])
                    if c == DC - 1:
                        m.then_inc(y_t, 1)
            for s in range(2):
                pe.wait_ge(y_ok[s], 1)
            for c in range(DC):
                m = nc.tensor.transpose(pa[0:SAMP, c // 4, (c % 4) * P:(c % 4 + 1) * P], x[:, c, SEQ:T], ident[:])
            m.then_inc(y_t, 1)

        @block.scalar
        def _(act):
            step = Steps(act_step)

            def round_hi(stage, s, i):
                if stage is None:
                    return
                u = FIRST[stage] + i
                act.wait_ge(raw_in[s], 16 * (u + 1))
                if not (stage == "up0" and first_turn(i)):
                    act.wait_ge(w_used[s], u)
                nc.scalar.activation(whi[s][:, 0:KT[stage], :], raw[s][:, 0:KT[stage], :], ACT.Copy) \
                    .then_inc(hi_made[s], 1)

            def turns(n, stage, body):
                body(0, stage, 1)
                with act.Fori(1, n - 1) as i:
                    body(i, stage, i + 1)
                body(n - 1, AFTER[stage], 0)

            for c in range(DC):
                if c == 4:
                    round_hi("up0", 0, 0)
                    round_hi("up0", 1, 0)
                act.wait_ge(in_t, c + 1)
                nc.scalar.activation(x[:, c, 0:SEQ], ps[c % 2][:, 0, :], ACT.Copy)
                step.add(nc.scalar.activation(x[:, c, SEQ:T], ps[c % 2][:, 1, 0:SAMP], ACT.Copy))
                act.wait_ge(act_step, step.value())
                nc.scalar.activation(xhi[:, c, :], x[:, c, :], ACT.Copy).then_inc(in_evac, 1)
            act.wait_ge(par_t, 1)
            nc.scalar.activation(par[:], pc[:, 0, 0:NPAR], ACT.Copy).then_inc(par_ok, 1)
            act.wait_ge(tab_mm, 1)
            for g, src in enumerate((pa[:, 0, :], pa[:, 1, :], pb[:, 0, :])):
                nc.scalar.activation(tab[:, g, :], src[0:HEADS, 0:RP], ACT.Copy).then_inc(tab_evac, 1)
            act.wait_ge(sb_mm, 1)
            nc.scalar.activation(s_bias[:, 0:NG * P], pc[:, 0, 0:NG * P], ACT.Copy).then_inc(sb_evac, 1)
            act.wait_ge(st_t, 1)
            nc.scalar.activation(hist[:].rearrange("p (a c) n -> p a (c n)", a=2), pd[:, :, 0:4 * DEC_B * PAD],
                                 ACT.Copy).then_inc(st_evac, 1)

            def up(stage):
                f, base = int(stage[2]), FIRST[stage]

                def turn(i, nxt, j):
                    if first_turn(i):
                        round_hi(nxt, 0, j)
                    act.wait_ge(w_used[0], base + i + 1)
                    if not first_turn(i):
                        act.wait_ge(h_made, FC * f + i)
                    nc.scalar.activation(split(sg[:]), halves(pa), ACT.Silu).then_inc(gate_silu, 1)
                    if not first_turn(i):
                        round_hi(nxt, 0, j)
                    round_hi(nxt, 1, j)
                    act.wait_ge(h_made, FC * f + i + 1)
                    nc.scalar.activation(hhi[:, i, :], hf[:], ACT.Copy).then_inc(h_hi_made, 1)

                turns(FC, stage, turn)

            def square(stage, c, i):
                act.wait_ge(res_made, DC * RES.index(stage) + i + 1)
                if not first_turn(i):
                    act.wait_ge(acc_made, ACCS * RES.index(stage) + 2 * i)
                nc.scalar.activation(sq[:], x[:, c, :], ACT.Square).then_inc(sq_made, 1)

            def root_table():
                nc.scalar.activation(root[:], eps[:], ACT.Sqrt)

            def down(stage):
                def turn(i, nxt, j):
                    round_hi(nxt, 0, j)
                    round_hi(nxt, 1, j)
                    square(stage, i, i)

                root_table()
                turns(DC, stage, turn)

            def norm(stage, k):
                act.wait_ge(stats, 2 * RES.index(stage) + 1)
                nc.scalar.activation(split(var[:]), halves(pc), ACT.Square).then_inc(ln_sq, 1)
                nc.scalar.activation(split(mean[:]), halves(pc), ACT.Copy).then_inc(ln_mean, 1)
                act.wait_ge(ln_var, RES.index(stage) + 1)
                nc.scalar.activation(rstd[:], var[:], ACT.Sqrt, bias=eps[:, 0:1]).then_inc(ln_std, 1)
                for c in range(DC):
                    act.wait_ge(ln_t, DC * RES.index(stage) + c + 1)
                    affine = dict(bias=par[:, PB + k * DC + c:PB + k * DC + c + 1],
                                  scale=par[:, PG + k * DC + c:PG + k * DC + c + 1])
                    if stage != "down3":
                        nc.scalar.activation(xhi[:, c, :], x[:, c, :], ACT.Identity, **affine)
                    nc.scalar.activation(x[:, c, :], x[:, c, :], ACT.Identity, **affine).then_inc(ln_x, 1)
                if (AFTER[stage] or "")[:2] == "up":
                    nc.scalar.activation(root[:], eps[:], ACT.Silu)

            up("up0")
            down("down0")
            norm("down0", 0)

            def pin(i, nxt, j):
                for s in range(2):
                    c = 2 * i + s
                    round_hi(nxt, s, j)
                    act.wait_ge(w_used[s], FIRST["pin"] + i + 1)
                    if i >= 1:
                        act.wait_ge(pooled, 2 * (i - 1) + s + 1)
                    else:
                        act.wait_ge(consts_made, 4)
                    samples = ue[s][:, 16 + SEQ:].rearrange("p (b t) -> p b t", t=20)[:, :, 16:20]
                    nc.scalar.activation(ue[s][:, 16:16 + HALF], ps[s][:, 0, 0:HALF], ACT.Copy)
                    nc.scalar.activation(ue[s][:, 16 + HALF:16 + SEQ], ps[s][:, 1, 0:SEQ - HALF], ACT.Copy)
                    nc.scalar.activation(samples, ps[s][:, 1, SEQ - HALF:HALF].rearrange("p (b t) -> p b t", t=4),
                                         ACT.Copy)
                    nc.scalar.activation(utail[:, c, :], ps[s][:, 1, HALF - PAD - SAMP:HALF], ACT.Copy) \
                        .then_inc(u_evac, 1)

            for i in range(UNITS["pin"]):
                if i + 1 < UNITS["pin"]:
                    pin(i, "pin", i + 1)
                else:
                    pin(i, "pgrp", 0)
            act.wait_ge(utail_t, 1)
            for b in range(2):
                m = nc.scalar.activation(utok[:, b * 512:(b + 1) * 512], pc[0:PAD + SAMP, b, :], ACT.Copy)
            m.then_inc(utok_ok, 1)

            for c in range(DC):
                s = c % 2
                if c < DC - 2:
                    act.wait_ge(z_done, c + 1)
                else:
                    act.wait_ge(w_used[s], FIRST["pgrp"] + 1)
                if c >= 2:
                    act.wait_ge(z_ready, c - 1)
                zf = (sg, hf)[s]
                step.add(nc.scalar.activation(split(zf[:]), halves(ps[s]), ACT.Copy, scale=par[:, PS + c:PS + c + 1]))
                act.wait_ge(act_step, step.value())
                nc.scalar.activation(zhi[:, c, :], zf[:], ACT.Copy).then_inc(z_scaled, 1)
                if c >= DC - 2:
                    round_hi("pout", s, 0)

            def residual_pair(stage):
                def turn(i, nxt, j):
                    for s in range(2):
                        round_hi(nxt, s, j)
                        square(stage, 2 * i + s, 2 * i + s)

                root_table()
                turns(UNITS[stage], stage, turn)

            residual_pair("pout")
            norm("pout", 1)
            act.wait_ge(utok_out, 32)
            up("up1")
            down("down1")
            norm("down1", 2)

            up("up2")
            down("down2")
            act.wait_ge(xs_out, 32)
            norm("down2", 3)

            def q_turn(i, nxt, j):
                for s in range(2):
                    act.wait_ge(w_used[s], FIRST["q"] + i + 1)
                    nc.scalar.activation(split(qt[:, 2 * i + s, :]), halves(ps[s]), ACT.Copy, scale=DH ** -0.5) \
                        .then_inc(q_evac, 1)
                    round_hi(nxt, s, j)

            turns(UNITS["q"], "q", q_turn)
            def kv_chunk(s, i, stored, nxt, j, first=False, keys=None, b=None):
                act.wait_ge(w_used[s], FIRST["kv"] + i + 1)
                if not first:
                    act.wait_ge(kv_t[s], i)
                    act.wait_ge(kt_out[s], 16 * stored)
                if keys is not None:
                    nc.scalar.activation(kn_t[:, bass.ds(keys + s, 1), :], ps[s][:, 1:2, HALF - SAMP:HALF], ACT.Copy)
                if b is not None and s == 0:
                    nc.scalar.activation(s_sc[:, 0, bass.ds(32 * b, 32)], pa[:, 1, HALF:HALF + 32], ACT.Copy)
                nc.scalar.activation(split(kvt[s][:]), halves(ps[s]), ACT.Copy).then_inc(kv_evac[s], 1)
                round_hi(nxt, s, j)

            def kv_tokens(s, i, first=False):
                act.wait_ge(kv_t[s], i + 1)
                if not first:
                    act.wait_ge(kv_out[s], 32 * i)
                nc.scalar.activation(kvp[s][:].rearrange("p j n -> p (j n)"), ps[2 + s][:, 0, :], ACT.Copy) \
                    .then_inc(kv_tok[s], 1)
                nc.scalar.activation(kv_n[:, bass.ds((2 * i + s) * P, P)], pc[SAMP * s:SAMP * (s + 1), 1, 0:P],
                                     ACT.Copy) \
                    .then_inc(kv_tok[s], 1)

            def kv_turn(i, stored, nxt, j, keys=None, b=None):
                kv_chunk(0, i, stored, nxt, j, keys=keys, b=b)
                kv_tokens(1, i - 1)
                kv_chunk(1, i, stored, nxt, j, keys=keys, b=b)
                kv_tokens(0, i)

            act.wait_ge(qrow_t, 1)
            nc.scalar.activation(q_hi[:], pc[0:SAMP].rearrange("p a n -> p (a n)"), ACT.Copy).then_inc(qhi_ok, 1)
            kv_chunk(0, 0, 0, "kv", 1, True, keys=0)
            kv_chunk(1, 0, 0, "kv", 1, True, keys=0)
            kv_tokens(0, 0, True)
            kv_chunk(0, 1, 1, "kv", 2, keys=2)
            kv_tokens(1, 0, True)
            kv_chunk(1, 1, 1, "kv", 2, keys=2)
            kv_tokens(0, 1)
            for g in range(NG):
                if g:
                    with act.Fori(0, 2) as i:
                        kv_turn(i + 4 * g, i + 2 * g, "kv", i + 4 * g + 1, keys=2 * i + 4 * g, b=i + 4 * g - 2)
                if g < 2:
                    with act.Fori(0, 2) as i:
                        kv_turn(i + 4 * g + 2, 2 * g + 2, "kv", i + 4 * g + 3, b=i + 4 * g)
            kv_turn(10, 6, "kv", 11)
            kv_turn(11, 6, None, 0)
            kv_tokens(1, 11)

            act.wait_ge(snk_mm, 1)
            nc.scalar.activation(s_nk[:, 0:512], pb[0:SAMP, 0, :], ACT.Copy).then_inc(snk_ok, 1)
            nc.scalar.activation(s_nk[:, 512:768], pb[0:SAMP, 1, 0:256], ACT.Copy).then_inc(snk_ok, 1)
            act.wait_ge(smax_ok, 1)
            for k in range(2):
                nc.scalar.activation(s_row[:, k, :], s_row[:, k, :], ACT.Exp, bias=s_stat[:, 2 + k:3 + k],
                                     accum_out=s_stat[:, 4 + k:5 + k]).then_inc(sexp_ok, 1)
            act.wait_ge(pkey_t, 1)
            for dst, src in ((p_key, pb[:]), (p_nk, pd[0:SAMP])):
                nc.scalar.activation(dst[:, 0:512], src[:, 0, :], ACT.Copy).then_inc(pkey_ok, 1)
                nc.scalar.activation(dst[:, 512:768], src[:, 1, 0:256], ACT.Copy).then_inc(pkey_ok, 1)

            def exps(r, h, first):
                act.wait_ge(s_ok, HEADS * r + h + 1)
                if not (first and h < 2):
                    act.wait_ge(pt_done, HEADS * r + h - 1)
                nc.scalar.activation(p_p[h % 2][:], s_p[h % 2][:], ACT.Exp, bias=a_stat[:, 1, r, h:h + 1],
                                     accum_out=a_stat[:, 2, r, h:h + 1]).then_inc(p_ok, 1)

            def turned(r, h, first):
                act.wait_ge(pt_done, HEADS * r + h + 1)
                if not (first and h < 2):
                    act.wait_ge(pv_done, HEADS * r + h - 1)
                nc.scalar.activation(pt_p[h % 2][:], pb[:, h % 2, :], ACT.Copy).then_inc(pt_ok, 1)

            def tile(r, first):
                exps(r, 0, first)
                for h in range(HEADS):
                    if isinstance(r, int) and r == QB - 1 and h == HEADS - 1:
                        round_hi("wo", 0, 0)
                        round_hi("wo", 1, 0)
                    if h + 1 < HEADS:
                        exps(r, h + 1, first)
                    turned(r, h, first)
                act.wait_ge(on_t, r + 1)
                tokens = ot[:, :, 0:SEQ].rearrange("p c (q r) -> p c q r", r=QB)
                nc.scalar.activation(tokens[:, :, :, r], pc[:, 1, :].rearrange("p (c q) -> p c q", c=GC), ACT.Copy) \
                    .then_inc(ot_ok, 1)

            tile(0, True)
            with act.Fori(1, QB - 1) as r:
                tile(r, False)
            tile(QB - 1, False)
            act.wait_ge(ot_ok, QB)
            act.wait_ge(ots_ok, QB)
            for c in range(GC):
                nc.scalar.activation(ohi[:, c, :], ot[:, c, :], ACT.Copy).then_inc(ohi_ok, 1)
            residual_pair("wo")
            norm("wo", 4)
            up("up3")
            down("down3")
            norm("down3", 5)
            for j in range(QB + 1):
                n = P if j < QB else SAMP
                act.wait_ge(y_t, j + 1)
                nc.scalar.activation(ytok[0:n, j, 0:512], ps[j % QB][0:n, 0, :], ACT.Copy).then_inc(y_ok[0], 1)

        @block.vector
        def _(dve):
            step = Steps(dve_step)

            def round_lo(stage, s, i):
                if stage is None:
                    return
                k = KT[stage]
                dve.wait_ge(hi_made[s], FIRST[stage] + i + 1)
                nc.vector.tensor_tensor(wlo[s][:, 0:k, :], raw[s][:, 0:k, :], whi[s][:, 0:k, :].bitcast(F32),
                                        ALU.subtract).then_inc(lo_made[s], 1)

            def turns(n, stage, body):
                body(0, stage, 1)
                with dve.Fori(1, n - 1) as i:
                    body(i, stage, i + 1)
                body(n - 1, AFTER[stage], 0)

            nc.vector.memset(invd[:], 1.0 / D).then_inc(consts_made, 1)
            nc.vector.memset(eps[:], LN_EPS).then_inc(consts_made, 1)
            nc.vector.memset(rbx[NBUCKET:NBUCKET + 1, :], NEG).then_inc(rb_copied, 1)
            nc.vector.memset(rb_s[:], 0.0).then_inc(rb_copied, 1)

            def x_low(chunks):
                for c in chunks:
                    dve.wait_ge(in_evac, c + 1)
                    nc.vector.tensor_tensor(xlo[:, c, :], x[:, c, :], xhi[:, c, :].bitcast(F32), ALU.subtract) \
                        .then_inc(x_ready, 1)

            x_low(range(4))
            round_lo("up0", 0, 0)
            round_lo("up0", 1, 0)
            dve.wait_ge(tab_in, 64)
            dve.wait_ge(rb_copied, 2)
            n = NBUCKET + 1
            def heads(g):
                return rbx[:, g * HEADS:(g + 1) * HEADS].rearrange("k (c h) -> k c h", c=GC).unsqueeze(1) \
                    .to_broadcast([n, 4, GC, 2])

            for v in range(6):
                for i in range(DEC_S) if v >= DEC_S else (v,):
                    m = nc.vector.tensor_copy(
                        rb_s[:, v, :].rearrange("k (b c i h) -> k b c i h", b=4, c=GC, h=2)[:, :, :, i, :],
                        heads(max(0, v - 3)))
            m.then_inc(rb_copied, 2)
            x_low(range(4, DC))
            dve.wait_ge(sb_mm, 1)
            nc.vector.tensor_tensor(s_bias[:, NG * P:], pc[:, 1, 0:NG * BW], smask[:], ALU.add).then_inc(sbn_ok, 1)

            def up(stage):
                f, base = int(stage[2]), FIRST[stage]

                def turn(i, nxt, j):
                    round_lo(nxt, 0, j)
                    dve.wait_ge(w_used[1], base + i + 1)
                    dve.wait_ge(gate_silu, FC * f + i + 1)
                    if not first_turn(i):
                        dve.wait_ge(h_lo_made, FC * f + i)
                    nc.vector.tensor_tensor(split(hf[:]), split(sg[:]), halves(pb), ALU.mult).then_inc(h_made, 1)
                    round_lo(nxt, 1, j)
                    dve.wait_ge(h_hi_made, FC * f + i + 1)
                    nc.vector.tensor_tensor(hlo[:, i, :], hf[:], hhi[:, i, :].bitcast(F32), ALU.subtract) \
                        .then_inc(h_lo_made, 1)

                turns(FC, stage, turn)

            def residual(stage, out, c, scale, s, used):
                dve.wait_ge(w_used[s], used)
                nc.vector.scalar_tensor_tensor(out=split(x[:, c, :]), in0=halves(out), scalar=scale,
                                               in1=split(x[:, c, :]), op0=ALU.mult, op1=ALU.add) \
                    .then_inc(res_made, 1)

            def down(stage):
                base = FIRST[stage]

                def pair(i, last):
                    for h in range(2):
                        nxt, j = (AFTER[stage], 0) if last and h else (stage, i + h + 1)
                        round_lo(nxt, 0, j)
                        residual(stage, ps[h], i + h, 0.5 / ALPHA, 1, base + i + h + 1)
                        round_lo(nxt, 1, j)

                with dve.Fori(0, DC - 2, 2) as i:
                    pair(i, False)
                pair(DC - 2, True)

            def norm(stage, last=False):
                dve.wait_ge(stats, 2 * RES.index(stage) + 2)
                dve.wait_ge(ln_sq, RES.index(stage) + 1)
                nc.vector.tensor_tensor(split(var[:]), halves(pd), split(var[:]), ALU.subtract).then_inc(ln_var, 1)
                dve.wait_ge(ln_mean, RES.index(stage) + 1)
                for c in range(EARLY):
                    nc.vector.tensor_tensor(x[:, c, :], x[:, c, :], mean[:], ALU.subtract)
                dve.wait_ge(ln_std, RES.index(stage) + 1)
                step.add(nc.vector.reciprocal(rstd[:], rstd[:]))
                dve.wait_ge(dve_step, step.value())
                for c in range(DC):
                    if c >= EARLY:
                        dve.wait_ge(ln_sub, (DC - EARLY) * RES.index(stage) + c - EARLY + 1)
                    nc.vector.tensor_tensor(x[:, c, :], x[:, c, :], rstd[:], ALU.mult).then_inc(ln_t, 1)
                    if c >= 1 and not last:
                        low(stage, c - 1)
                if not last:
                    low(stage, DC - 1)

            def low(stage, c):
                dve.wait_ge(ln_x, DC * RES.index(stage) + c + 1)
                nc.vector.tensor_tensor(xlo[:, c, :], x[:, c, :], xhi[:, c, :].bitcast(F32), ALU.subtract) \
                    .then_inc(x_ready, 1)

            up("up0")
            down("down0")
            norm("down0")

            for s in range(2):
                nc.vector.memset(ue[s][:, 0:16], 0.0).then_inc(consts_made, 1)
            def pin(i, nxt, j):
                for s in range(2):
                    c = 2 * i + s
                    g = c // 2
                    tail = lambda t: t[:, 16 + SEQ:].rearrange("p (b t) -> p b t", t=20)
                    e = ue[s]
                    round_lo(nxt, s, j)
                    if i == 0:
                        dve.wait_ge(st_evac, 1)
                    if c:
                        dve.wait_ge(pooled, c)
                    step.add(nc.vector.tensor_copy(tail(e)[:, :, 1:16], hist[:, c, :].rearrange("p (b t) -> p b t", t=PAD)))
                    dve.wait_ge(dve_step, step.value())
                    dve.wait_ge(u_evac, c + 1)
                    src, w = e, 1
                    for level in range(g + 1):
                        dst = us[level % 2]
                        nc.vector.tensor_tensor(dst[:, 2 * w - 1:16 + SEQ], src[:, 2 * w - 1:16 + SEQ],
                                                src[:, w - 1:16 + SEQ - w], ALU.add)
                        step.add(nc.vector.tensor_tensor(tail(dst)[:, :, 2 * w:20], tail(src)[:, :, 2 * w:20],
                                                         tail(src)[:, :, w:20 - w], ALU.add))
                        dve.wait_ge(dve_step, step.value())
                        src, w = dst, 2 * w
                    mean_, diff = us[(g + 1) % 2], us[g % 2]
                    nc.vector.tensor_tensor(mean_[:, 16:32], src[:, 16:32], inv[:, g, :], ALU.mult)
                    nc.vector.tensor_scalar(mean_[:, 32:16 + SEQ], src[:, 32:16 + SEQ], 1.0 / w, None, ALU.mult)
                    step.add(nc.vector.tensor_scalar(tail(mean_)[:, :, 16:20], tail(src)[:, :, 16:20], 1.0 / w, None,
                                                     ALU.mult))
                    dve.wait_ge(dve_step, step.value())
                    nc.vector.tensor_tensor(diff[:, 0:SEQ], mean_[:, 16:16 + SEQ], e[:, 16:16 + SEQ], ALU.subtract)
                    step.add(nc.vector.tensor_tensor(diff[:, SEQ:T].rearrange("p (b t) -> p b t", t=4),
                                                     tail(mean_)[:, :, 16:20], tail(e)[:, :, 16:20], ALU.subtract))
                    dve.wait_ge(dve_step, step.value())
                    step.add(nc.vector.tensor_copy(phi[:, c, :], diff[:, 0:T]))
                    dve.wait_ge(dve_step, step.value())
                    nc.vector.tensor_tensor(plo[:, c, :], diff[:, 0:T], phi[:, c, :].bitcast(F32), ALU.subtract) \
                        .then_inc(pooled, 1)

            dve.wait_ge(consts_in, 32)
            for i in range(UNITS["pin"]):
                if i + 1 < UNITS["pin"]:
                    pin(i, "pin", i + 1)
                else:
                    pin(i, "pgrp", 0)

            for c in range(DC):
                dve.wait_ge(z_scaled, c + 1)
                nc.vector.tensor_tensor(zlo[:, c, :], (sg, hf)[c % 2][:], zhi[:, c, :].bitcast(F32), ALU.subtract) \
                    .then_inc(z_ready, 1)
                if c >= DC - 2:
                    round_lo("pout", c % 2, 0)

            def residual_pair(stage):
                def turn(i, nxt, j):
                    for s in range(2):
                        residual(stage, ps[s], 2 * i + s, 1.0 / ALPHA, s, FIRST[stage] + i + 1)
                        round_lo(nxt, s, j)

                turns(UNITS[stage], stage, turn)

            residual_pair("pout")
            norm("pout")
            dve.wait_ge(utok_out, 32)
            up("up1")
            down("down1")
            norm("down1")

            up("up2")
            down("down2")
            norm("down2")

            def q_turn(i, nxt, j):
                round_lo(nxt, 0, j)
                round_lo(nxt, 1, j)

            turns(UNITS["q"], "q", q_turn)

            dve.wait_ge(qhi_ok, 1)
            nc.vector.tensor_tensor(q_lo[:], pc[0:SAMP].rearrange("p a n -> p (a n)"), q_hi[:].bitcast(F32), ALU.subtract) \
                .then_inc(qlo_ok, 1)

            def times(b, s, t):
                dve.wait_ge(q_cast, (NCK - 1) * b + t)
                m = nc.vector.tensor_tensor(kq[t % 2][:], pd[:, 1, :], cached[s][:, t, :], ALU.mult)
                m.then_inc(kq_made, 1)

            def summed(b, t):
                g, i = (t - 1) // 4 + 1, (t - 1) % 4
                dve.wait_ge(kq_made, (NCK - 1) * b + t)
                own = s_sc[:, g, bass.ds(32 * b, 32)].rearrange("p (c i h) -> p c i h", c=GC, h=2)[:, :, i, :]
                nc.vector.reduce_sum(own, kq[t % 2][:].rearrange("p (c h d) -> p c h d", c=GC, h=2), axis=AX_X) \
                    .then_inc(kq_used, 1)

            def kv_turn(i, nxt, j, b=None, s=0):
                if b is None:
                    round_lo("kv", 1, i)
                    round_lo(nxt, 0, j)
                    return
                dve.wait_ge(kc_t, b + 1)
                if not first_turn(b):
                    dve.wait_ge(kc_used, b)
                nc.vector.tensor_copy(k_t[:], pd[:, 1, :]).then_inc(kc_ok, 1)
                for t in range(1, NCK):
                    if t > 2:
                        dve.wait_ge(kq_used, (NCK - 1) * b + t - 2)
                    elif not first_turn(b):
                        dve.wait_ge(kq_used, (NCK - 1) * b)
                    times(b, s, t)
                    if t == 2:
                        round_lo("kv", 1, i)
                    if t == 6:
                        round_lo(nxt, 0, j)
                    summed(b, t)

            round_lo("kv", 0, 1)
            kv_turn(1, "kv", 2)
            kv_turn(2, "kv", 3, 0, 0)
            kv_turn(3, "kv", 4, 1, 1)
            with dve.Fori(1, DEC_B // 2) as n:
                kv_turn(2 * n + 2, "kv", 2 * n + 3, 2 * n, 0)
                kv_turn(2 * n + 3, "kv", 2 * n + 4, 2 * n + 1, 1)
            kv_turn(10, "kv", 11)
            kv_turn(11, None, 0)

            for h in range(HEADS):
                m = nc.vector.memset(b0[0:32, h, 0:P], NEG)
            m.then_inc(b0_pad, 1)

            def qk_tile(r, c):
                q = qt[:, :, 0:SEQ].rearrange("p (g c) (q r) -> p g c q r", g=NG, r=QB)
                k = kt12[:].rearrange("p (g c) (q r) -> p g c q r", g=2, r=QB)
                for g in range(NG):
                    nc.vector.tensor_copy(q_r[:, g * GC + c, :], q[:, g, c, :, r])
                for g in range(2):
                    m = nc.vector.tensor_copy(k_r[:, g * GC + c, :], k[:, g, c, :, r])
                m.then_inc(qk_ok, 1)

            dve.wait_ge(kt_in, 32)
            for s in range(2):
                dve.wait_ge(w_used[s], FIRST["wo"])
            for c in range(GC):
                qk_tile(0, c)

            dve.wait_ge(srow_t, 1)
            dve.wait_ge(sb_evac, 1)
            for k in range(2):
                nc.vector.tensor_tensor(s_row[:, k, 0:NG * P], pa[:, k, 0:NG * P], s_bias[:, 0:NG * P], ALU.add)
                seen = s_bias[:, NG * P:].rearrange("p (g n) -> p g n", g=NG)[:, :, 16 - 16 * k:16 - 16 * k + SAMP]
                m = nc.vector.tensor_tensor(s_row[:, k, NG * P:SK].rearrange("p (g n) -> p g n", g=NG),
                                            pa[:, k, NG * P:SK].rearrange("p (g n) -> p g n", g=NG), seen, ALU.add)
            m.then_inc(srow_ok, 1)
            dve.wait_ge(srow_ok, 1)
            step.add(nc.vector.reduce_max(s_stat[:, 0:2], s_row, axis=AX_X))
            dve.wait_ge(dve_step, step.value())
            nc.vector.tensor_scalar(s_stat[:, 2:4], s_stat[:, 0:2], -1.0, None, ALU.mult).then_inc(smax_ok, 1)
            dve.wait_ge(sexp_ok, 2)
            step.add(nc.vector.reciprocal(s_stat[:, 6:8], s_stat[:, 4:6]))
            dve.wait_ge(dve_step, step.value())
            for k in range(2):
                m = nc.vector.tensor_scalar(s_row[:, k, :], s_row[:, k, :], s_stat[:, 6 + k:7 + k], None, ALU.mult)
            m.then_inc(snorm_ok, 1)

            dve.wait_ge(snv_done, 1)
            for h in range(2):
                part = slice(DH * h, DH * h + DH)
                m = nc.vector.tensor_copy(
                    ot[part, :, SEQ:T],
                    pc[part, 1, 0:GC * 2 * SAMP].rearrange("p (c t h) -> p c t h", c=GC, h=2)[:, :, :, h])
            m.then_inc(snv_ok, 1)

            def sample_values(r):
                dve.wait_ge(sv_done, 2 * r + 2)
                if not first_turn(r):
                    dve.wait_ge(os_t, r)
                nc.vector.tensor_copy(o_s, pd[0:64, 0, :]).then_inc(sv_evac, 1)

            def sample_outputs(r):
                dve.wait_ge(os_t, r + 1)
                for h in range(2):
                    part = slice(DH * h, DH * h + DH)
                    dst = ot[part, :, bass.ds(SEQ + 2 * DEC_S * r, 2 * DEC_S)]
                    src = pd[part, 1, 0:GC * 16].rearrange("p (c t h) -> p c t h", c=GC, h=2)
                    m = nc.vector.tensor_tensor(dst, src[:, :, :, h], dst, ALU.add)
                m.then_inc(ots_ok, 1)

            def head(r, h):
                dve.wait_ge(s_done, HEADS * r + h + 1)
                dve.wait_ge(b0_in[h // 4], 64 * (r + 1))
                b = h % 2
                if not (first_turn(r) and h < 2):
                    dve.wait_ge(p_ok, HEADS * r + h - 1)
                nc.vector.tensor_tensor(s_p[b][:, 0:256], pa[:, b, 0:256], b0[:, h, :], ALU.add)
                step.add(nc.vector.tensor_tensor(s_p[b][:, 256:512], pa[:, b, 256:512], b12[:, h, :], ALU.add))
                dve.wait_ge(dve_step, step.value())
                step.add(nc.vector.reduce_max(a_stat[:, 0, r, h:h + 1], s_p[b][:], axis=AX_X))
                dve.wait_ge(dve_step, step.value())
                nc.vector.tensor_scalar(a_stat[:, 1, r, h:h + 1], a_stat[:, 0, r, h:h + 1], -1.0, None, ALU.mult) \
                    .then_inc(s_ok, 1)

            def tile(r, last):
                for h in range(HEADS):
                    head(r, h)
                    if h % 2 and not last:
                        qk_tile(r + 1, h // 2)
                if last:
                    round_lo("wo", 0, 0)
                    round_lo("wo", 1, 0)
                dve.wait_ge(p_ok, HEADS * (r + 1))
                step.add(nc.vector.reciprocal(a_stat[:, 3, r, :], a_stat[:, 2, r, :]))
                dve.wait_ge(dve_step, step.value())
                sample_values(r)
                dve.wait_ge(pv_done, HEADS * (r + 1))
                if not first_turn(r):
                    dve.wait_ge(on_t, r)
                nc.vector.tensor_tensor(o_n[:].rearrange("p (h d) -> p h d", d=DH),
                                        pc[:, 0, :].rearrange("p (h d) -> p h d", d=DH),
                                        a_stat[:, 3, r, :].unsqueeze(2).to_broadcast([P, HEADS, DH]), ALU.mult) \
                    .then_inc(on_ok, 1)
                sample_outputs(r)

            dve.wait_ge(kvn_out, 16 * NG)
            dve.wait_ge(b12_in, 32)
            tile(0, False)
            with dve.Fori(1, QB - 1) as r:
                step.turn(r - 1, 2 * HEADS + 1)
                tile(r, False)
                step.turns(QB - 2)
            tile(QB - 1, True)
            for c in range(GC):
                dve.wait_ge(ohi_ok, c + 1)
                nc.vector.tensor_tensor(olo[:, c, :], ot[:, c, :], ohi[:, c, :].bitcast(F32), ALU.subtract) \
                    .then_inc(o_ready, 1)
            residual_pair("wo")
            norm("wo")
            up("up3")
            down("down3")
            norm("down3", last=True)
            for j in range(QB + 1):
                n = P if j < QB else SAMP
                dve.wait_ge(y_t, j + 1)
                nc.vector.tensor_copy(ytok[0:n, j, 512:D], ps[j % QB][0:n, 1, :]).then_inc(y_ok[1], 1)

        @block.gpsimd
        def _(pool):
            def sums(stage):
                nc.gpsimd.memset(accs[:], 0.0).then_inc(acc_zero, 1)
                nc.gpsimd.memset(accq[:], 0.0).then_inc(acc_zero, 1)
                pool.wait_ge(acc_zero, 2 * RES.index(stage) + 2)
                base = RES.index(stage)

                def add(c):
                    if not first_turn(c):
                        pool.wait_ge(acc_made, ACCS * base + 2 * c)
                    pool.wait_ge(res_made, DC * base + c + 1)
                    nc.gpsimd.tensor_tensor(accs[:], accs[:], x[:, c, :], ALU.add).then_inc(acc_made, 1)
                    pool.wait_ge(sq_made, DC * base + c + 1)
                    nc.gpsimd.tensor_tensor(accq[:], accq[:], sq[:], ALU.add).then_inc(acc_made, 1)

                add(0)
                with pool.Fori(1, DC - 1) as c:
                    add(c)

            def centre(stage):
                pool.wait_ge(stats, 2 * RES.index(stage) + 2)
                pool.wait_ge(ln_mean, RES.index(stage) + 1)
                for c in range(EARLY, DC):
                    nc.gpsimd.tensor_tensor(x[:, c, :], x[:, c, :], mean[:], ALU.subtract).then_inc(ln_sub, 1)

            sums("down0")
            centre("down0")
            pool.wait_ge(utok_ok, 1)
            pool.dma_start(O["pool_p"][0, 0, :, :], utok[0:PAD, :]).then_inc(utok_out, 16)
            pool.dma_start(O["pool_s"][0, :, PAD - DEC_S:PAD, :], utok[PAD:PAD + SAMP, :]).then_inc(utok_out, 16)
            sums("pout")
            centre("pout")
            sums("down1")
            centre("down1")

            sums("down2")
            centre("down2")

            c0 = A["cache_kv_w128"].rearrange("b p k h d -> b p k (h d)")
            c1 = A["cache_kv_w512"].rearrange("b (p i) k h d -> b p i k (h d)", i=DIL[1])
            c2 = A["cache_kv_w2048"].rearrange("b (p i) k h d -> b p i k (h d)", i=DIL[2])

            def load(b, first, rest, kv, into):
                pool.dma_start(first, c0[b, :, kv, :]).then_inc(into, 16)
                pool.dma_start(rest[:, 0:4, :], c1[b, :, :, kv, :]).then_inc(into, 16)
                pool.dma_start(rest[:, 4:8, :], c2[b, :, 0:DEC_S, kv, :]).then_inc(into, 16)

            def load_keys(b, s):
                load(b, cached[s][:, 0, :], cached[s][:, 1:NCK, :], 0, cached_in[s])

            def load_values(b, s):
                load(b, v_c0[s][:], v_c[s], 1, value_in[s])

            def queries(b, s):
                nc.gpsimd.tensor_copy(sel[s][:], ident[0:SAMP, bass.ds(DEC_S * b, DEC_S)].unsqueeze(2)
                                      .to_broadcast([SAMP, DEC_S, P]))
                nc.gpsimd.tensor_copy(q_b[s][:], q_bd[:, 0:GC, bass.ds(2 * DEC_S * b, 2 * DEC_S)]).then_inc(qb_ok, 1)

            for s in range(2):
                pool.wait_ge(w_used[s], FIRST["kv"])
            load_keys(0, 0)
            load_keys(1, 1)
            nc.gpsimd.memset(q_bd[:], 0.0).then_inc(qbd_ok, 1)
            pool.wait_ge(qbd_ok, 1)
            pool.wait_ge(q_evac, NG * GC)
            for h in range(2):
                part = slice(DH * h, DH * h + DH)
                nc.gpsimd.tensor_copy(q_bd[part].rearrange("p c (t h) -> p c t h", h=2)[:, :, :, h],
                                      qt[part, :, SEQ:T]).then_inc(qbd_ok, 1)
            pool.wait_ge(qbd_ok, 3)
            queries(0, 0)
            queries(1, 1)
            with pool.Fori(1, DEC_B // 2) as n:
                for s in range(2):
                    pool.wait_ge(kq_made, (NCK - 1) * (2 * n + s - 1))
                    queries(2 * n + s, s)
                    load_keys(2 * n + s, s)
            for s in range(2):
                pool.wait_ge(w_used[s], FIRST["wo"])
            pool.wait_ge(v_in, 16 * NG)
            load_values(0, 0)
            pool.wait_ge(kq_used, (NCK - 1) * DEC_B)
            load_values(1, 1)

            def probs(b, s):
                own = p_key.rearrange("p (g n) -> p g n", g=NG)[:, :, bass.ds(32 * b, 32)]
                nc.gpsimd.tensor_copy(p_b[s][:, 0, :], own[:, 0, :])
                own = own.rearrange("p g (c i h) -> p g c i h", c=GC, h=2)
                tiles = p_b[s][:, 1:, :].rearrange("p (g i) n -> p g i n", g=2)
                for i in range(DEC_S):
                    m = nc.gpsimd.tensor_copy(
                        tiles[:, :, i, :].rearrange("p g (c i h) -> p g c i h", c=GC, h=2)[:, :, :, i, :],
                        own[:, 1:, :, i, :])
                m.then_inc(pb_ok, 1)

            pool.wait_ge(srow_t, 1)
            for s in range(2):
                nc.gpsimd.memset(p_b[s], 0.0).then_inc(pb_zero, 1)
            pool.wait_ge(pb_zero, 2)
            pool.wait_ge(pkey_ok, 4)
            probs(0, 0)
            probs(1, 1)
            with pool.Fori(1, DEC_B // 2) as n:
                for s in range(2):
                    pool.wait_ge(sv_done, 2 * n + s - 1)
                    load_values(2 * n + s, s)
                    probs(2 * n + s, s)
            pool.wait_ge(o_ready, GC)
            sums("wo")
            centre("wo")
            sums("down3")
            centre("down3")


OUTPUTS = [("y_p", (1, SEQ, D)), ("y_s", (DEC_B, DEC_S, D)), ("pool_p", (1, 1, PAD, D)), ("pool_s", (1, DEC_B, PAD, D)),
           ("kv_p0", (1, 128, 2, HEADS, DH)), ("kv_p1", (1, SEQ, 2, HEADS, DH)), ("kv_p2", (1, SEQ, 2, HEADS, DH)),
           ("kv_s0", (DEC_B, DEC_S, 2, HEADS, DH)), ("kv_s1", (DEC_B, DEC_S, 2, HEADS, DH)),
           ("kv_s2", (DEC_B, DEC_S, 2, HEADS, DH))]


def kernel(**inputs):
    import concourse.bacc as bacc
    from concourse.bass_utils import run_bass_kernel_spmd

    nc = bacc.Bacc("TRN2", target_bir_lowering=False, num_devices=1)
    arrays, A, O = {}, {}, {}
    for name, a in {**inputs, **shape_constants()}.items():
        a = np.ascontiguousarray(a)
        arrays["in_" + name] = a
        A[name] = nc.dram_tensor("in_" + name, a.shape, mybir.dt.from_np(a.dtype), kind="ExternalInput").ap()
    for name, shape in OUTPUTS:
        O[name] = nc.dram_tensor("out_" + name, shape, F32, kind="ExternalOutput").ap()
    build(nc, A, O)
    r = run_bass_kernel_spmd(nc, [arrays], core_ids=[0])
    return tuple(r.results[0]["out_" + name] for name, _ in OUTPUTS)
```
